# Optimizing a Trainium2 kernel written in Bass

```python
import jax
import jax.numpy as jnp
from jax import lax
import numpy as np

D_MODEL = 1024
BATCH = 1
SEQ = 512
DEPTH = 1

CHUNK = 64
HEAD_DIM = 64
ROPE_THETA = 10000.0
EPS = 1e-6
SWA_HEADS = 8
SWA_KV_HEADS = 2
SWA_WINDOW = 128
SWA_WINDOW_CHUNKS = SWA_WINDOW // CHUNK
DSA_HEADS = 8
DSA_KV_HEADS = 2
IDX_HEADS = 4
IDX_DIM = 64
DSA_TOPK_MAX = 256
Q_BLOCK = 128
N_BRANCH = 2
BRANCH_WIDTH = SWA_HEADS * HEAD_DIM
N_GROUPS = 4
EXPERTS_PER_GROUP = 8
EXPERT_TOPK = 2
D_EXPERT = 512
N_MOD = 6

IN_SIZES = (
    SWA_HEADS * HEAD_DIM, SWA_KV_HEADS * HEAD_DIM, SWA_KV_HEADS * HEAD_DIM,
    DSA_HEADS * HEAD_DIM, DSA_KV_HEADS * HEAD_DIM, DSA_KV_HEADS * HEAD_DIM,
    IDX_HEADS * IDX_DIM, IDX_DIM, IDX_HEADS,
    N_BRANCH * D_MODEL,
)
D_IN = sum(IN_SIZES)
IN_SPLITS = tuple(int(s) for s in np.cumsum(IN_SIZES)[:-1])

kernel_name = "hybrid_swa_sink_dsa_hmoe_adaln"

def rms_norm(x, gain):
    xf = x.astype(jnp.float32)
    y = xf * lax.rsqrt(jnp.mean(xf * xf, axis=-1, keepdims=True) + EPS)
    return (y * gain.astype(jnp.float32)).astype(x.dtype)

def rope(x, pos):
    half = x.shape[-1] // 2
    inv_freq = ROPE_THETA ** (-jnp.arange(half, dtype=jnp.float32) / half)
    ang = pos.astype(jnp.float32)[..., None] * inv_freq
    cos = jnp.cos(ang)[:, :, None, :]
    sin = jnp.sin(ang)[:, :, None, :]
    x1 = x[..., :half].astype(jnp.float32)
    x2 = x[..., half:].astype(jnp.float32)
    return jnp.concatenate([x1 * cos - x2 * sin, x2 * cos + x1 * sin], axis=-1).astype(x.dtype)

def swa_sink_attention(q, k, v, sinks):
    b, s, h, d = q.shape
    kvh = k.shape[2]
    g = h // kvh
    nc = s // CHUNK
    w = SWA_WINDOW_CHUNKS
    qc = q.reshape(b, nc, CHUNK, kvh, g, d)
    kc = k.reshape(b, nc, CHUNK, kvh, d)
    vc = v.reshape(b, nc, CHUNK, kvh, d)

    def band(t):
        return jnp.concatenate(
            [jnp.pad(t, ((0, 0), (j, 0), (0, 0), (0, 0), (0, 0)))[:, :nc] for j in range(w - 1, -1, -1)],
            axis=2)

    kw, vw = band(kc), band(vc)
    key_lag = jnp.repeat(jnp.arange(w - 1, -1, -1), CHUNK)
    valid = jnp.arange(nc)[:, None] >= key_lag[None, :]
    scores = jnp.einsum('bnqkgd,bnskd->bnkgqs', qc, kw).astype(jnp.float32) * (d ** -0.5)
    scores = jnp.where(valid[None, :, None, None, None, :], scores, -jnp.inf)
    sink = jnp.broadcast_to(sinks.astype(jnp.float32).reshape(1, 1, kvh, g, 1, 1),
                            scores.shape[:-1] + (1,))
    probs = jax.nn.softmax(jnp.concatenate([scores, sink], axis=-1), axis=-1)[..., :-1]
    out = jnp.einsum('bnkgqs,bnskd->bnqkgd', probs.astype(v.dtype), vw)
    return out.reshape(b, s, h * d)

def dsa_sparse_attention(q, k, v, iq, ik, iw):
    b, s, h, d = q.shape
    kvh = k.shape[2]
    g = h // kvh
    L = k.shape[1]
    topk = min(DSA_TOPK_MAX, L // 4)
    nb = s // Q_BLOCK

    def to_blocks(t):
        return jnp.moveaxis(t.reshape((b, nb, Q_BLOCK) + t.shape[2:]), 1, 0)

    t_blocks = jnp.arange(s, dtype=jnp.int32).reshape(nb, Q_BLOCK)
    key_pos = jnp.arange(L, dtype=jnp.int32)
    idx_scale = (IDX_DIM ** -0.5) * (IDX_HEADS ** -0.5)

    def block(args):
        q_blk, iq_blk, iw_blk, t = args
        limit = (t // CHUNK + 1) * CHUNK
        logits = jnp.einsum('bqhe,bse->bqhs', iq_blk, ik).astype(jnp.float32)
        index = jnp.einsum('bqhs,bqh->bqs', jax.nn.relu(logits), iw_blk.astype(jnp.float32)) * idx_scale
        admissible = key_pos[None, :] < limit[:, None]
        index = jnp.where(admissible[None], index, -jnp.inf)
        _, sel = lax.top_k(index, topk)
        sel_valid = sel < limit[None, :, None]
        k_sel = jax.vmap(lambda kk, ii: kk[ii])(k, sel)
        v_sel = jax.vmap(lambda vv, ii: vv[ii])(v, sel)
        qg = q_blk.reshape(b, Q_BLOCK, kvh, g, d)
        scores = jnp.einsum('bqkgd,bqskd->bqkgs', qg, k_sel).astype(jnp.float32) * (d ** -0.5)
        scores = jnp.where(sel_valid[:, :, None, None, :], scores, -jnp.inf)
        probs = jax.nn.softmax(scores, axis=-1)
        out = jnp.einsum('bqkgs,bqskd->bqkgd', probs.astype(v.dtype), v_sel)
        return out.reshape(b, Q_BLOCK, h * d)

    out = lax.map(block, (to_blocks(q), to_blocks(iq), to_blocks(iw), t_blocks))
    return jnp.moveaxis(out, 0, 1).reshape(b, s, h * d)

def hierarchical_moe(h, w_group, b_group, w_router, b_router, w_gate, w_up, w_down):
    b, s, dm = h.shape
    hf = h.reshape(b * s, dm)
    group_probs = jax.nn.softmax((hf @ w_group + b_group).astype(jnp.float32), axis=-1)
    g_sel = jnp.argmax(group_probs, axis=-1)
    p_group = jnp.max(group_probs, axis=-1)
    e_logits = (jnp.einsum('td,gde->tge', hf, w_router) + b_router).astype(jnp.float32)
    e_logits = jnp.take_along_axis(e_logits, g_sel[:, None, None], axis=1)[:, 0]
    top_v, top_i = lax.top_k(jax.nn.softmax(e_logits, axis=-1), EXPERT_TOPK)
    top_v = top_v / jnp.sum(top_v, axis=-1, keepdims=True)
    combine = jnp.sum(jax.nn.one_hot(top_i, EXPERTS_PER_GROUP, dtype=jnp.float32) * top_v[..., None],
                      axis=1) * p_group[:, None]
    y = jnp.zeros_like(hf)
    for grp in range(N_GROUPS):
        cw = jnp.where((g_sel == grp)[:, None], combine, 0.0).astype(hf.dtype)
        a = jnp.einsum('td,edf->tef', hf, w_gate[grp])
        u = jnp.einsum('td,edf->tef', hf, w_up[grp])
        hid = jax.nn.silu(a) * u * cw[..., None]
        y = y + jnp.einsum('tef,efd->td', hid, w_down[grp])
    return y.reshape(b, s, dm)

def hybrid_layer(x, c, positions, w_ada, b_ada, g_norm_mix, w_in, q_norm_a, k_norm_a, sinks_a,
                 q_norm_b, k_norm_b, w_branch, w_out, g_norm_ffn, w_group, b_group, w_router,
                 b_router, w_expert_gate, w_expert_up, w_expert_down):
    b, s, dm = x.shape
    mod = (c @ w_ada + b_ada)[:, None, :]
    sh_m, sc_m, gt_m, sh_f, sc_f, gt_f = jnp.split(mod, N_MOD, axis=-1)

    h = rms_norm(x, g_norm_mix) * (1.0 + sc_m) + sh_m
    proj = h @ w_in
    qa, ka, va, qb, kb, vb, iq, ik, iw, gate_logits = jnp.split(proj, IN_SPLITS, axis=-1)
    qa = rope(rms_norm(qa.reshape(b, s, SWA_HEADS, HEAD_DIM), q_norm_a), positions)
    ka = rope(rms_norm(ka.reshape(b, s, SWA_KV_HEADS, HEAD_DIM), k_norm_a), positions)
    va = va.reshape(b, s, SWA_KV_HEADS, HEAD_DIM)
    qb = rope(rms_norm(qb.reshape(b, s, DSA_HEADS, HEAD_DIM), q_norm_b), positions)
    kb = rope(rms_norm(kb.reshape(b, s, DSA_KV_HEADS, HEAD_DIM), k_norm_b), positions)
    vb = vb.reshape(b, s, DSA_KV_HEADS, HEAD_DIM)
    iq = rope(iq.reshape(b, s, IDX_HEADS, IDX_DIM), positions)
    ik = rope(ik[:, :, None, :], positions)[:, :, 0, :]

    y_a = swa_sink_attention(qa, ka, va, sinks_a)
    y_b = dsa_sparse_attention(qb, kb, vb, iq, ik, iw)
    branches = jnp.stack([y_a, y_b], axis=2)
    up = jnp.einsum('bsnw,nwd->bsnd', branches, w_branch)
    gates = jax.nn.sigmoid(gate_logits.reshape(b, s, N_BRANCH, dm))
    merged = jnp.sum(gates * up, axis=2)
    x = x + gt_m * (merged @ w_out)

    h2 = rms_norm(x, g_norm_ffn) * (1.0 + sc_f) + sh_f
    y_ffn = hierarchical_moe(h2, w_group, b_group, w_router, b_router,
                             w_expert_gate, w_expert_up, w_expert_down)
    return x + gt_f * y_ffn

def setup_inputs(seed: int = 0) -> dict:
    key = jax.random.key(seed)
    ks = jax.random.split(key, 24)

    def nrm(k, shape, scale):
        return jax.random.normal(k, shape, jnp.float32) * scale

    x = nrm(ks[0], (BATCH, SEQ, D_MODEL), 1.0)
    c = nrm(ks[1], (BATCH, D_MODEL), 1.0)
    offsets = jax.random.randint(ks[2], (BATCH, 1), 0, 4096, dtype=jnp.int32)
    positions = offsets + jnp.arange(SEQ, dtype=jnp.int32)[None, :]
    return {
        "x": x,
        "c": c,
        "positions": positions,
        "w_ada": nrm(ks[3], (DEPTH, D_MODEL, N_MOD * D_MODEL), 0.5 * D_MODEL ** -0.5),
        "b_ada": nrm(ks[4], (DEPTH, N_MOD * D_MODEL), 0.01),
        "g_norm_mix": 1.0 + nrm(ks[5], (DEPTH, D_MODEL), 0.02),
        "w_in": nrm(ks[6], (DEPTH, D_MODEL, D_IN), D_MODEL ** -0.5),
        "q_norm_a": 1.0 + nrm(ks[7], (DEPTH, HEAD_DIM), 0.02),
        "k_norm_a": 1.0 + nrm(ks[8], (DEPTH, HEAD_DIM), 0.02),
        "sinks_a": nrm(ks[9], (DEPTH, SWA_HEADS), 0.5),
        "q_norm_b": 1.0 + nrm(ks[10], (DEPTH, HEAD_DIM), 0.02),
        "k_norm_b": 1.0 + nrm(ks[11], (DEPTH, HEAD_DIM), 0.02),
        "w_branch": nrm(ks[12], (DEPTH, N_BRANCH, BRANCH_WIDTH, D_MODEL), BRANCH_WIDTH ** -0.5),
        "w_out": nrm(ks[13], (DEPTH, D_MODEL, D_MODEL), D_MODEL ** -0.5),
        "g_norm_ffn": 1.0 + nrm(ks[14], (DEPTH, D_MODEL), 0.02),
        "w_group": nrm(ks[15], (DEPTH, D_MODEL, N_GROUPS), D_MODEL ** -0.5),
        "b_group": nrm(ks[16], (DEPTH, N_GROUPS), 0.01),
        "w_router": nrm(ks[17], (DEPTH, N_GROUPS, D_MODEL, EXPERTS_PER_GROUP), D_MODEL ** -0.5),
        "b_router": nrm(ks[18], (DEPTH, N_GROUPS, EXPERTS_PER_GROUP), 0.01),
        "w_expert_gate": nrm(ks[19], (DEPTH, N_GROUPS, EXPERTS_PER_GROUP, D_MODEL, D_EXPERT), D_MODEL ** -0.5),
        "w_expert_up": nrm(ks[20], (DEPTH, N_GROUPS, EXPERTS_PER_GROUP, D_MODEL, D_EXPERT), D_MODEL ** -0.5),
        "w_expert_down": nrm(ks[21], (DEPTH, N_GROUPS, EXPERTS_PER_GROUP, D_EXPERT, D_MODEL), D_EXPERT ** -0.5),
    }

def reference(x, c, positions, w_ada, b_ada, g_norm_mix, w_in, q_norm_a, k_norm_a, sinks_a,
              q_norm_b, k_norm_b, w_branch, w_out, g_norm_ffn, w_group, b_group, w_router,
              b_router, w_expert_gate, w_expert_up, w_expert_down):
    for layer in range(DEPTH):
        x = hybrid_layer(x, c, positions, w_ada[layer], b_ada[layer], g_norm_mix[layer], w_in[layer],
                         q_norm_a[layer], k_norm_a[layer], sinks_a[layer], q_norm_b[layer],
                         k_norm_b[layer], w_branch[layer], w_out[layer], g_norm_ffn[layer],
                         w_group[layer], b_group[layer], w_router[layer], b_router[layer],
                         w_expert_gate[layer], w_expert_up[layer], w_expert_down[layer])
    return x


_drawn_inputs = setup_inputs


def setup_inputs(seed=0):
    import zlib

    import numpy as np

    out = dict(_drawn_inputs(seed))
    spreads = {}
    factors = {'g_norm_mix': 3.825,
     'q_norm_a': 8.0,
     'k_norm_a': 8.0,
     'sinks_a': 8.0,
     'q_norm_b': 8.0,
     'k_norm_b': 8.0,
     'b_group': 29.304,
     'b_router': 16.375,
     'g_norm_ffn': 5.421}
    for name, (base, spread) in spreads.items():
        noise = np.random.default_rng([zlib.crc32(name.encode()), seed]).standard_normal(out[name].shape)
        drawn = base * np.exp(spread * noise) if base else spread * noise
        out[name] = jnp.asarray(drawn.astype(out[name].dtype))
    for name, factor in factors.items():
        out[name] = (out[name] * factor).astype(out[name].dtype)
    return out
```

```python
from contextlib import ExitStack

import concourse.bass as bass
from concourse import mybir
import numpy as np

F32 = mybir.dt.float32
I32 = mybir.dt.int32
U32 = mybir.dt.uint32
ALU = mybir.AluOpType
ACT = mybir.ActivationFunctionType
AX = mybir.AxisListType.X

P = 128
D = 1024
S = 512
CHUNK = 64
HD = 64
KD = D // P
NB = S // P
HEADS = 8
KVH = 2
IDXH = 4
TOPK = min(256, S // 4)
G = 4
EPG = 8
NE = G * EPG
FE = 512
NROUTE = G + NE
EPS = 1e-6
NEG = -1e30
TAKEN = -3e38
SLOTS = 64
PAIRS = NE // 2
MAXOVER = (2 * S) // SLOTS
OPAIRS = MAXOVER // 2
ALLPAIRS = PAIRS + OPAIRS
GATE0 = 1860
WCH = 4096
TWO_PI_HI = 6.28125
TWO_PI_MID = float(np.float32(2 * np.pi - 6.28125))
TWO_PI_LO = float(2 * np.pi - 6.28125 - TWO_PI_MID)
ROUNDER = 12582912.0
PI_IN = 3.1415925

CONST = {}
_at = 0
for _name, _w in (("ident", P), ("tri", P), ("ones", P), ("win", 2 * P), ("freq", 32),
                  ("prio", NE), ("e64", NE), ("over", MAXOVER)):
    CONST[_name] = (_at, _at + _w)
    _at += _w
CONST_W = _at


def shape_constants():
    c = np.zeros((P, CONST_W), np.float32)

    def put(name, a):
        lo, hi = CONST[name]
        c[:, lo:hi] = a

    i = np.arange(P)
    put("ident", np.eye(P))
    put("tri", (i[:, None] < i[None, :]))
    put("ones", 1.0)
    win = np.full((P, 2 * P), NEG)
    win[:CHUNK, CHUNK:3 * CHUNK] = 0.0
    win[CHUNK:, 2 * CHUNK:] = 0.0
    put("win", win)
    half = HD // 2
    put("freq", np.float32(10000.0) ** (-np.arange(half, dtype=np.float32) / np.float32(half)))
    put("prio", NE - np.arange(NE))
    put("e64", SLOTS * np.arange(NE))
    put("over", np.arange(MAXOVER))
    return c


def token_ids():
    return (np.arange(P)[:, None] + P * np.arange(NB)[None, :]).astype(np.int32)


def build_block(nc, A):
    with ExitStack() as ctx:
        def sb(name, shape, dt=F32):
            return ctx.enter_context(nc.sbuf_tensor(name, shape, dt))

        def sem(name):
            return ctx.enter_context(nc.semaphore(name))

        bank = [ctx.enter_context(nc.psum_tensor(f"bank{i}", [P, 512], F32)) for i in range(8)]

        ring = sb("ring", [P, 5 * WCH])
        qk = sb("qk", [P, 2 * WCH])
        scr = sb("scr", [P, 2 * WCH])
        r1 = sb("r1", [P, WCH])
        hT_ = sb("hT", [P, WCH])
        vt = sb("vt", [P, NB, 2, KVH * HD])
        idx = sb("idx", [P, 3, S])
        bias_ada = sb("bias_ada", [P, 3, 512])
        mod = sb("mod", [P, 512])
        con = sb("con", [P, CONST_W])
        rope_cs = sb("rope_cs", [P, NB, 2, HD])
        gains = sb("gains", [P, 2, 4, HD])
        wr = sb("wr", [P, KD, NROUTE])
        route_bias = sb("route_bias", [P, NROUTE])
        rows24 = sb("rows24", [24, P])
        cols24 = sb("cols24", [P, 24])
        modT = sb("modT", [P, 48])
        scm = sb("scm", [P, 4, KD])
        cb = sb("cb", [P, KD, 32])
        pos_i = sb("pos_i", [P, NB], I32)
        pos_f = sb("pos_f", [P, NB])
        sinks = sb("sinks", [P, 2, HEADS])
        tok = sb("tok", [P, NB], I32)
        st = sb("st", [P, 3, NB])
        hst = sb("hst", [P, 3, 20])
        iw = sb("iw", [P, NB, IDXH])
        top8 = sb("top8", [P, 8])
        nmax = sb("nmax", [P, 2, HEADS])
        rsum = sb("rsum", [P, 2, HEADS])
        sinkt = sb("sinkt", [P, 2, HEADS])
        zero_i = sb("zero_i", [P, ALLPAIRS], I32)
        slot_tok = sb("slot_tok", [P, ALLPAIRS], I32)
        loc_i = sb("loc_i", [P, 2, NB], I32)
        addr_i = sb("addr_i", [P, 3, 2 * NB], I32)
        nover_i = sb("nover_i", [P, 1], I32)
        oexp_i = sb("oexp_i", [P, MAXOVER], I32)
        cw = sb("cw", [P, 2, NB])
        logits = sb("logits", [P, NB, NROUTE])
        rexp = sb("rexp", [P, 5 * NB])

        def C(name):
            lo, hi = CONST[name]
            return con[:, lo:hi]

        ident, tri, ones = C("ident"), C("tri"), C("ones")
        win = C("win")

        def slot(i):
            if i == 5:
                return qk[:, 0:WCH]
            return ring[:, WCH * i:WCH * (i + 1)]

        hT = hT_[:, :].rearrange("p (k t) -> p k t", k=KD)
        x_tok = r1[:, :].rearrange("p (b d) -> p b d", b=NB)
        yT = r1[:, :].rearrange("p (n j t) -> p n j t", n=2, j=4)
        qT = qk[:, 0:WCH].rearrange("p (n j t) -> p n j t", n=2, j=4)
        kz = qk[:, WCH:WCH + 2048].rearrange("p (n z t) -> p n z t", n=2, z=2)
        iqT = qk[:, WCH + 2048:WCH + 3072].rearrange("p (c t) -> p c t", c=2)
        ikz = qk[:, WCH + 3072:WCH + 4096].rearrange("p (z t) -> p z t", z=2)
        gt_rows = qk[:, WCH + 2048:WCH + 4096].rearrange("p (m d) -> p m d", m=2)
        raw = [scr[:, 1280 * i:1280 * (i + 1)] for i in range(2)]
        ta, tb, rt = (scr[:, 2560 + 1280 * i:3840 + 1280 * i] for i in range(3))
        sq = scr[:, 6400:7680]
        gtab = scr[:, 7680:8192].rearrange("p (u k d) -> p u k d", u=2, k=4)
        sq_junk = scr[:, 0:4096].rearrange("p (b d) -> p b d", b=NB)
        args = scr[:, 4096:4608]
        atmp = scr[:, 4608:5120].rearrange("p (u n) -> p u n", u=4)
        rawd = r1[:, 0:1296].rearrange("p (b c) -> p b c", b=NB)
        rtd = r1[:, 1296:1296 + 768].rearrange("p (u c) -> p u c", u=2)
        tad = r1[:, 2064:2384]
        tbd = r1[:, 2384:2704]
        relu = r1[:, 3072:4096].rearrange("p (u s) -> p u s", u=2)
        prob = {0: scr[:, 0:2048], 1: scr[:, 2048:6144]}
        pt = [scr[:, 6144 + 1024 * i:7168 + 1024 * i] for i in range(2)]
        merged = scr[:, 0:WCH].rearrange("p (k t) -> p k t", k=KD)
        sig = scr[:, 4096:6144].rearrange("p (u n t) -> p u n t", u=2, n=2)
        mtmp = scr[:, 6144:7168].rearrange("p (n t) -> p n t", n=2)
        ores = scr[:, 7168:7680]
        xn2 = scr[:, 4096:6144].rearrange("p (u d) -> p u d", u=2)
        h2T = scr[:, 6144:7168].rearrange("p (k t) -> p k t", k=KD)
        xg = hT_[:, 0:1024]
        xT = hT_[:, 1024:2048].rearrange("p (k t) -> p k t", k=KD)
        act_g = hT_[:, 2048:2304]
        hid = hT_[:, 2304:2560]
        hidT = hT_[:, 2560:2816].rearrange("p (c h s) -> p c h s", c=2, h=2)
        ysb = hT_[:, 3072:4096].rearrange("p (u d) -> p u d", u=2)
        y12 = scr[:, 0:4096].rearrange("p (u n d) -> p u n d", u=2, n=2)
        def rw(at, n):
            return scr[:, at:at + n]

        vt_flat = vt[:, :, :, :].rearrange("p b n d -> p (b n d)")

        r_top = rw(0, 8 * NB).rearrange("p (u b) -> p u b", u=8)
        r_hotg = rw(32, 16).rearrange("p (b g) -> p b g", b=NB)
        r_le = rw(64, P).rearrange("p (b e) -> p b e", b=NB)
        r_hot = rw(192, 2 * P).rearrange("p (u b e) -> p u b e", u=2, b=NB)
        picks, before, per_part, r_cnt, r_loc = rw(448, P), rw(576, P), rw(704, NE), rw(736, NE), rw(768, P)
        r_ov = rw(896, 3 * NE).rearrange("p (u e) -> p u e", u=3)
        r_exp = rw(992, MAXOVER)
        r_cmp = rw(1024, MAXOVER * NE).rearrange("p (j e) -> p j e", j=MAXOVER)

        xn_dram = nc.dram_tensor("xn_rows", [S, D], F32, kind="Internal").ap()
        y_dram = nc.dram_tensor("expert_rows", [ALLPAIRS * P, D], F32, kind="Internal").ap()
        table = nc.dram_tensor("slot_table", [P * ALLPAIRS, 1], I32, kind="Internal").ap()

        w_ada = A["w_ada"][0].rearrange("(k p) n -> p k n", p=P)
        w_in = A["w_in"][0].rearrange("(k p) n -> p k n", p=P)
        w_out = A["w_out"][0].rearrange("(k p) n -> p k n", p=P)

        def wide(i, w=512):
            return slot(i % 5)[:, 0:KD * w].rearrange("p (k n) -> p k n", k=KD)

        def ada(i, m):
            return [(wide(i), w_ada[:, :, 512 * m:512 * (m + 1)])]

        def inproj(i, c0, w=512):
            return [(wide(i, w), w_in[:, :, c0:c0 + w])]

        def branch(i, n):
            dst = slot(i % 5).rearrange("p (j n) -> p j n", j=4)
            src = A["w_branch"][0, n].rearrange("(g j p) n -> g p j n", g=2, j=4)
            return [(dst[64 * g:64 * (g + 1)], src[g]) for g in range(2)]

        cA, cC, cB = 5, 6, 7
        kv_dst = wide(cC).rearrange("p k (u n) -> p k u n", u=2)
        chunks = [ada(m, m) for m in range(4)]
        chunks += [inproj(4, 1536, 324), inproj(cA, 0),
                   [(kv_dst[:, :, 0], w_in[:, :, 512:768]), (kv_dst[:, :, 1], w_in[:, :, 1280:1536])],
                   inproj(cB, 768)]
        chunks += [ada(8 + m, 4 + m) for m in range(8)]
        cG = {(0, 0): 16, (1, 0): 18, (0, 1): 20, (1, 1): 21}
        cBr = {0: 17, 1: 19}
        cO = {0: 22, 1: 23}
        chunks += [inproj(16, GATE0), branch(17, 0), inproj(18, GATE0 + D), branch(19, 1),
                   inproj(20, GATE0 + 512), inproj(21, GATE0 + D + 512)]
        chunks += [[(wide(22 + h), w_out[:, :, 512 * h:512 * (h + 1)])] for h in range(2)]
        chunk_in = [sem(f"chunk_in{i}") for i in range(5)]
        const_in, x_in, rows_in, bias_in = sem("const_in"), sem("x_in"), sem("rows_in"), sem("bias_in")
        pos_in, tok_in, gains_in, router_in, xre_in = (sem("pos_in"), sem("tok_in"), sem("gains_in"),
                                                       sem("router_in"), sem("xre_in"))
        cols_pe, cols_dve = sem("cols_pe"), sem("cols_dve")
        ss_act, rstd_t, rstd_act, x_scaled = sem("ss_act"), sem("rstd_t"), sem("rstd_act"), sem("x_scaled")
        xt_pe, xt_act = sem("xt_pe"), sem("xt_act")
        ada_pe, ada_dve, adaT_pe, adaT_dve = sem("ada_pe"), sem("ada_dve"), sem("adaT_pe"), sem("adaT_dve")
        h_ready = sem("h_ready")
        gt_pe, gt_dve = sem("gt_pe"), sem("gt_dve")
        ang_dve, ang_act = sem("ang_dve"), sem("ang_act")
        zeros_pool = sem("zeros_pool")
        d_pe, d_act, d_rope, dT_pe, dT_act = sem("d_pe"), sem("d_act"), sem("d_rope"), sem("dT_pe"), sem("dT_act")
        is_pe, is_act, is_dve = sem("is_pe"), sem("is_act"), sem("is_dve")
        pr_pe, pr_act, hss_dve, hrt_act, qk_rope = (sem("pr_pe"), sem("pr_act"), sem("hss_dve"), sem("hrt_act"),
                                                    sem("qk_rope"))
        qkT_pe, qkT_act = sem("qkT_pe"), sem("qkT_act")
        s_pe, s_dve, p_act = sem("s_pe"), sem("s_dve"), sem("p_act")
        sink_dve, sink_act, p_scaled = sem("sink_dve"), sem("sink_act"), sem("p_scaled")
        pT_pe, pT_act, pT_dve, pv_pe, y_dve = sem("pT_pe"), sem("pT_act"), sem("pT_dve"), sem("pv_pe"), sem("y_dve")
        gate_pe, up_pe, sig_act, merge_dve = sem("gate_pe"), sem("up_pe"), sem("sig_act"), sem("merge_dve")
        o_pe, x1_dve, ss2_act, rt2_dve, rt2_act, xn2_dve = (sem("o_pe"), sem("x1_dve"), sem("ss2_act"),
                                                            sem("rt2_dve"), sem("rt2_act"), sem("xn2_dve"))
        xn_stored = [sem(f"xn_stored{i}") for i in range(2)]
        x2T_pe, x2T_act, x2T_dve, lg_pe, lg_dve = (sem("x2T_pe"), sem("x2T_act"), sem("x2T_dve"),
                                                   sem("lg_pe"), sem("lg_dve"))
        rexp_dve, rexp_act, m_dve, rank_pe, locs_dve = (sem("rexp_dve"), sem("rexp_act"), sem("m_dve"),
                                                        sem("rank_pe"), sem("locs_dve"))
        over_dve = sem("over_dve")
        table_zeroed, ids_put, table_in, x_got = sem("table_zeroed"), sem("ids_put"), sem("table_in"), sem("x_got")
        piece_in = [[sem(f"{n}_in{s}") for n in ("wg", "wu", "wd")] for s in range(2)]
        wg_used, wu_used, wd_used = sem("wg_used"), sem("wu_used"), sem("wd_used")
        xgT_pe, xgT_act, xgT_dve = sem("xgT_pe"), sem("xgT_act"), sem("xgT_dve")
        silu_act, hid_dve, hidT_pe, hidT_act, ydn_dve = (
            sem("silu_act"), sem("hid_dve"), sem("hidT_pe"), sem("hidT_act"), sem("ydn_dve"))
        y_stored = [sem(f"y_stored{s}") for s in range(2)]
        y_got = [sem(f"y_got{i}") for i in range(2)]
        fin_dve, out_stored = sem("fin_dve"), sem("out_stored")
        dve_step = sem("dve_step")
        ang_part, h_part, v_act = sem("ang_part"), sem("h_part"), sem("v_act")

        arrivals = {}
        loaded = [0] * 5
        for i, pieces in enumerate(chunks):
            loaded[i % 5] += 16 * len(pieces)
            arrivals[i] = (chunk_in[i % 5], loaded[i % 5])

        through = {m: (ada_pe, 1) for m in range(4)} | {8 + m: (ada_pe, 2 + m // 4) for m in range(8)}
        through |= {4: (d_pe, NB), cA: (pr_pe, 3 * NB - 2), cC: (pr_pe, 3 * NB - 1), cB: (pr_pe, 3 * NB)}
        through |= {cG[n, h]: (gate_pe, 8 * h + 7 + n) for n in range(2) for h in range(2)}
        through |= {cBr[n]: (up_pe, 2 * KD - 1 + n) for n in range(2)}
        through |= {cO[h]: (o_pe, 2 * NB - 1 + h) for h in range(2)}

        eslots = ((4, 0, 1), (5, 2, 3))
        last_in_slot = {4: 19, 0: 20, 1: 21, 2: 22, 3: 23}

        def wg_t(s):
            return slot(eslots[s][0]).rearrange("p (k n) -> p k n", k=KD)

        def wu_t(s):
            return slot(eslots[s][1]).rearrange("p (k n) -> p k n", k=KD)

        def wd_t(s):
            return slot(eslots[s][2]).rearrange("p (k n) -> p k n", k=4)

        eg_dram = A["w_expert_gate"][0].rearrange("g e (k p) n -> (g e) p k n", p=P)
        eu_dram = A["w_expert_up"][0].rearrange("g e (k p) n -> (g e) p k n", p=P)
        ed_dram = A["w_expert_down"][0].rearrange("g e (k p) n -> (g e) p k n", p=P)

        GROUPS = [(n, b) for b in range(NB) for n in range(2)]

        def key_tiles(n, b):
            return list(range(max(0, b - 1), b + 1)) if n == 0 else list(range(b + 1))

        TILES = [(g, i, t) for g, (n, b) in enumerate(GROUPS) for i, t in enumerate(key_tiles(n, b))]
        tiles_to = [sum(len(key_tiles(*GROUPS[x])) for x in range(g)) for g in range(len(GROUPS) + 1)]

        MOD_AT = {1: 1, 3: 2}

        block = ctx.enter_context(nc.Block())

        @block.sync
        def _(sp):
            sp.dma_start(con[:, :], A["consts"]).then_inc(const_in, 16)
            sp.dma_start(x_tok, A["x"][0].rearrange("(b p) d -> p b d", p=P)).then_inc(x_in, 16)
            for i, pieces in enumerate(chunks):
                if i >= 5:
                    sp.wait_ge(*through[i - 5])
                for dst, src in pieces:
                    sp.dma_start(dst, src).then_inc(chunk_in[i % 5], 16)

            def load_pair(i, expert, first):
                for s in range(2):
                    e = expert(s)
                    for n, (dst, src, used) in enumerate(((wg_t(s), eg_dram, wg_used), (wu_t(s), eu_dram, wu_used),
                                                          (wd_t(s), ed_dram, wd_used))):
                        if not first:
                            sp.wait_ge(used, 2 * i + s - 1)
                        elif eslots[s][n] in last_in_slot:
                            sp.wait_ge(*through[last_in_slot[eslots[s][n]]])
                        else:
                            sp.wait_ge(s_pe, HEADS * len(GROUPS))
                        sp.dma_start(dst, src[bass.ds(e, 1)].rearrange("o p k n -> (o p) k n")
                                     if not isinstance(e, int) else src[e]).then_inc(piece_in[s][n], 16)

            load_pair(0, lambda s: s, True)
            with sp.Fori(1, PAIRS) as i:
                load_pair(i, lambda s: i * 2 + s, False)
            sp.wait_ge(over_dve, 1)
            n_over = sp.value_load(nover_i[0:1, 0:1], min_val=0, max_val=MAXOVER)
            with sp.If(n_over > 0):
                with sp.Fori(0, OPAIRS) as j:
                    load_pair(j + PAIRS, lambda s: sp.value_load(oexp_i[0:1, bass.ds(j * 2 + s, 1)], min_val=0,
                                                                 max_val=NE - 1), False)

        @block.gpsimd
        def _(pool):
            nc.gpsimd.memset(zero_i[:, :], 0).then_inc(zeros_pool, 1)
            nc.gpsimd.memset(kz, 0.0).then_inc(zeros_pool, 1)
            nc.gpsimd.memset(ikz, 0.0).then_inc(zeros_pool, 1)
            pool.wait_ge(zeros_pool, 1)
            pool.dma_start(table.rearrange("(p i) o -> p (i o)", p=P), zero_i[:, :]).then_inc(table_zeroed, 16)
            pool.wait_ge(table_zeroed, 16)
            pool.wait_ge(locs_dve, 1)
            pool.wait_ge(tok_in, 16)
            for n in range(2):
                for b in range(NB):
                    nc.gpsimd.indirect_dma_start(
                        out=table, out_offset=bass.IndirectOffsetOnAxis(
                            ap=addr_i[:, 2, NB * n + b:NB * n + b + 1].bitcast(U32), axis=0),
                        in_=tok[:, b:b + 1], in_offset=None).then_inc(ids_put, 16)
            pool.wait_ge(ids_put, 16 * 2 * NB)
            pool.dma_start(slot_tok[:, :], table.rearrange("(p i) o -> p (i o)", p=P)).then_inc(table_in, 16)
            pool.wait_ge(table_in, 16)
            for u in range(2):
                pool.wait_ge(xn_stored[u], 16 * NB // 2)

            def fetch_tokens(i):
                if i >= 1:
                    pool.wait_ge(xgT_pe, i)
                nc.gpsimd.indirect_dma_start(
                    out=xg, out_offset=None, in_=xn_dram,
                    in_offset=bass.IndirectOffsetOnAxis(ap=slot_tok[:, i:i + 1].bitcast(U32), axis=0)
                ).then_inc(x_got, 16)

            for i in range(PAIRS):
                fetch_tokens(i)
            pool.wait_ge(over_dve, 1)
            n_over = pool.value_load(nover_i[0:1, 0:1], min_val=0, max_val=MAXOVER)

            def fetch_results(rows, pairs):
                for s in range(2):
                    pool.wait_ge(y_stored[s], 32 * pairs)
                for b in range(NB):
                    if b >= 2:
                        pool.wait_ge(fin_dve, b - 1)
                    for n in range(2):
                        nc.gpsimd.indirect_dma_start(
                            out=y12[:, b % 2, n], out_offset=None, in_=rows,
                            in_offset=bass.IndirectOffsetOnAxis(ap=loc_i[:, n, b:b + 1].bitcast(U32), axis=0)
                        ).then_inc(y_got[b % 2], 16)

            with pool.If(n_over > 0):
                for i in range(PAIRS, ALLPAIRS):
                    fetch_tokens(i)
                fetch_results(y_dram, ALLPAIRS)
            with pool.Else():
                fetch_results(y_dram[0:PAIRS * P, :], PAIRS)

        @block.scalar
        def _(act):
            for k, name in enumerate(("g_norm_mix", "g_norm_ffn", "c")):
                act.dma_start(rows24[8 * k:8 * k + 8, :], A[name][0].rearrange("(k p) -> k p", p=P)
                              ).then_inc(rows_in, 16)
            ba = A["b_ada"].rearrange("o (m g n) -> o g m n", m=3, g=4)
            for g in range(4):
                act.dma_start(bias_ada[32 * g:32 * (g + 1)], ba[:, g].broadcast_to([32, 3, 512])).then_inc(bias_in, 16)
            act.dma_start(pos_i[:, :], A["positions"]).then_inc(pos_in, 16)
            act.dma_start(sinks[:, 0, :], A["sinks_a"].broadcast_to([P, HEADS])).then_inc(gains_in, 16)
            act.dma_start(gains[:, :, :, :].rearrange("p u k d -> p (u k d)"),
                          A["head_gains"].broadcast_to([P, 8 * HD])).then_inc(gains_in, 16)
            act.dma_start(tok[:, :], A["token_ids"]).then_inc(tok_in, 16)
            act.dma_start(route_bias[:, :], A["route_bias"].broadcast_to([P, NROUTE])).then_inc(router_in, 16)
            act.dma_start(wr[:, :, :], A["w_route"].rearrange("(k p) n -> p k n", p=P)).then_inc(router_in, 16)

            act.wait_ge(x_in, 16)
            for b in range(NB):
                nc.scalar.activation(sq_junk[:, b], x_tok[:, b], ACT.Square, accum_out=st[:, 0, b:b + 1]).then_inc(ss_act, 1)
            act.wait_ge(rstd_t, 1)
            nc.scalar.activation(st[:, 2], st[:, 1], ACT.Sqrt).then_inc(rstd_act, 1)
            for n in range(2 * NB):
                b, h = n // 2, n % 2
                act.wait_ge(xt_pe, n + 1)
                nc.scalar.activation(hT[:, 4 * h:4 * h + 4, P * b:P * (b + 1)],
                                     bank[2 + n % 4][:, :].rearrange("p (k t) -> p k t", k=4),
                                     ACT.Copy).then_inc(xt_act, 1)
            act.wait_ge(ang_dve, 1)
            nc.scalar.activation(rope_cs[:, :, :, :].rearrange("p b u d -> p (b u d)"), args,
                                 ACT.Sin).then_inc(ang_act, 1)

            for b in range(NB):
                act.wait_ge(d_pe, b + 1)
                nc.scalar.activation(rawd[:, b], bank[2 + b][:, 0:324], ACT.Copy).then_inc(d_act, 1)

            def evac_projection(b):
                if b >= 2:
                    act.wait_ge(qk_rope, b - 1)
                act.wait_ge(pr_pe, 3 * (b + 1))
                ba_, bc_, bb_ = (bank[2 + 3 * (b % 2) + i] for i in range(3))
                kv = bc_[:, :].rearrange("p (n u d) -> p n u d", n=2, u=2)
                nc.scalar.activation(raw[b % 2][:, 0:512], ba_[:, :], ACT.Copy)
                nc.scalar.activation(raw[b % 2][:, 640:1152], bb_[:, :], ACT.Copy)
                for n in range(2):
                    nc.scalar.activation(raw[b % 2][:, 512 + 640 * n:640 + 640 * n], kv[:, n, 0], ACT.Copy)
                nc.scalar.activation(vt[:, b], kv[:, :, 1], ACT.Copy).then_inc(v_act, 1)
                if b >= 1:
                    act.wait_ge(hss_dve, b)
                nc.scalar.activation(sq[:, 0:512], ba_[:, :], ACT.Square)
                nc.scalar.activation(sq[:, 640:1152], bb_[:, :], ACT.Square)
                for n in range(2):
                    last = nc.scalar.activation(sq[:, 512 + 640 * n:640 + 640 * n], kv[:, n, 0], ACT.Square)
                last.then_inc(pr_act, 1)

            def root_heads(b):
                act.wait_ge(hss_dve, b + 1)
                nc.scalar.activation(hst[:, 2], hst[:, 1], ACT.Sqrt).then_inc(hrt_act, 1)

            def evac_heads(b):
                act.wait_ge(qkT_pe, b + 1)
                base = 2 + 3 * (b % 2)
                t = slice(P * b, P * (b + 1))
                for n in range(2):
                    nc.scalar.activation(qT[:, n, :, t], bank[base + n][:, :].rearrange("p (j t) -> p j t", j=4),
                                         ACT.Copy)
                for n in range(2):
                    for z in range(2):
                        r = slice(64 * z, 64 * (z + 1))
                        last = nc.scalar.activation(kz[r, n, z, t], bank[base + 2][r, P * n:P * (n + 1)], ACT.Copy)
                last.then_inc(qkT_act, 1)

            evac_projection(0)
            act.wait_ge(zeros_pool, 3)
            for b in range(NB):
                act.wait_ge(dT_pe, b + 1)
                t = slice(P * b, P * (b + 1))
                bk = bank[b % 2]
                nc.scalar.activation(iqT[:, :, t], bk[:, 0:256].rearrange("p (c t) -> p c t", c=2), ACT.Copy)
                for z in range(2):
                    r = slice(64 * z, 64 * (z + 1))
                    last = nc.scalar.activation(ikz[r, z, t], bk[r, 256:384], ACT.Copy)
                last.then_inc(dT_act, 1)
            for n in range(3 * IDXH):
                b = 1 + n // IDXH
                act.wait_ge(is_pe, n + 1)
                if n >= 2:
                    act.wait_ge(is_dve, n - 1)
                nc.scalar.activation(relu[:, n % 2, 0:P * (b + 1)], bank[5 + n % 3][:, 0:P * (b + 1)],
                                     ACT.Relu).then_inc(is_act, 1)
            for b in range(1, NB):
                root_heads(b - 1)
                evac_projection(b)
                evac_heads(b - 1)
            root_heads(NB - 1)
            evac_heads(NB - 1)

            def exps(g):
                n, b = GROUPS[g]
                w = P * len(key_tiles(n, b))
                for h in range(HEADS):
                    act.wait_ge(s_dve, HEADS * g + h + 1)
                    pr = prob[n][:, w * h:w * (h + 1)]
                    nc.scalar.activation(pr, pr, ACT.Exp, bias=nmax[:, g % 2, h:h + 1], scale=-1.0,
                                         accum_out=rsum[:, g % 2, h:h + 1]).then_inc(p_act, 1)
                if n == 0:
                    act.wait_ge(sink_dve, b + 1)
                    nc.scalar.activation(sinkt[:, 1], sinkt[:, 0], ACT.Exp).then_inc(sink_act, 1)

            def evac_probs(g):
                for k in range(tiles_to[g], tiles_to[g + 1]):
                    act.wait_ge(pT_pe, 2 * k + 1)
                    if k >= 2:
                        act.wait_ge(pv_pe, k - 1)
                    nc.scalar.activation(pt[k % 2][:, 0:512], bank[4][:, :], ACT.Copy).then_inc(pT_act, 1)

            for g in range(len(GROUPS)):
                exps(g)
                if g >= 1:
                    evac_probs(g - 1)
            evac_probs(len(GROUPS) - 1)

            for d in range(KD):
                act.wait_ge(gate_pe, 2 * (d + 1))
                if d >= 2:
                    act.wait_ge(merge_dve, d - 1)
                for n in range(2):
                    last = nc.scalar.activation(sig[:, d % 2, n], bank[4 * (d % 2) + n][:, :], ACT.Sigmoid)
                last.then_inc(sig_act, 1)
            act.wait_ge(up_pe, 2 * KD)
            act.dma_start(x_tok, A["x"][0].rearrange("(b p) d -> p b d", p=P)).then_inc(xre_in, 16)

            def norm2(b):
                act.wait_ge(x1_dve, b + 1)
                nc.scalar.activation(vt_flat, x_tok[:, b], ACT.Square, accum_out=st[:, 0, b:b + 1]).then_inc(ss2_act, 1)
                act.wait_ge(rt2_dve, b + 1)
                nc.scalar.activation(st[:, 2, b:b + 1], st[:, 1, b:b + 1], ACT.Sqrt).then_inc(rt2_act, 1)
                act.wait_ge(xn2_dve, b + 1)
                act.dma_start(xn_dram[P * b:P * (b + 1), :], xn2[:, b % 2]).then_inc(xn_stored[b % 2], 16)

            def evac_h2(b):
                act.wait_ge(x2T_pe, 2 * b + 1)
                if b >= 1:
                    act.wait_ge(lg_pe, b)
                for k in range(4):
                    last = nc.scalar.activation(h2T[:, k], bank[4][:, P * k:P * (k + 1)], ACT.Identity,
                                                scale=scm[:, 2, k:k + 1], bias=scm[:, 3, k:k + 1])
                last.then_inc(x2T_act, 1)

            norm2(0)
            for b in range(1, NB):
                norm2(b)
                evac_h2(b - 1)
            evac_h2(NB - 1)
            act.wait_ge(rexp_dve, 1)
            nc.scalar.activation(rexp[:, :], rexp[:, :], ACT.Exp).then_inc(rexp_act, 1)

            def experts(i):
                act.wait_ge(xgT_pe, i + 1)
                for k in range(4):
                    last = nc.scalar.activation(xT[:, k], bank[0][:, P * k:P * (k + 1)], ACT.Identity,
                                                scale=scm[:, 2, k:k + 1], bias=scm[:, 3, k:k + 1])
                last.then_inc(xgT_act, 1)
                for s in range(2):
                    act.wait_ge(wg_used, i * 2 + s + 1)
                    nc.scalar.activation(act_g, bank[2][:, 0:256], ACT.Silu).then_inc(silu_act, 1)
                    act.wait_ge(hidT_pe, i * 2 + s + 1)
                    nc.scalar.activation(hidT, bank[4][:, 0:256].rearrange("p (c h s) -> p c h s", c=2, h=2),
                                         ACT.Copy).then_inc(hidT_act, 1)
                    act.wait_ge(ydn_dve, i * 2 + s + 1)
                    rows = y_dram[bass.ds(i * P + SLOTS * s, SLOTS), :].rearrange("r (g n) -> g r n", g=2)
                    for g in range(2):
                        act.dma_start(rows[g], ysb[64 * g:64 * (g + 1), s]).then_inc(y_stored[s], 16)

            experts(0)
            with act.Fori(1, PAIRS) as i:
                experts(i)
            act.wait_ge(over_dve, 1)
            n_over = act.value_load(nover_i[0:1, 0:1], min_val=0, max_val=MAXOVER)
            with act.If(n_over > 0):
                with act.Fori(PAIRS, ALLPAIRS) as i:
                    experts(i)

            for b in range(NB):
                act.wait_ge(fin_dve, b + 1)
                act.dma_start(A["out"][0, P * b:P * (b + 1), :], x_tok[:, b]).then_inc(out_stored, 16)
            act.wait_ge(out_stored, 16 * NB)

        @block.tensor
        def _(pe):
            def arrived(i):
                pe.wait_ge(*arrivals[i])

            mm = nc.tensor.matmul

            def transpose(out, in_):
                return nc.tensor.transpose(out, in_, ident)

            pe.wait_ge(const_in, 16)
            pe.wait_ge(rows_in, 48)
            nc.tensor.transpose(bank[1][:, 0:24], rows24[:, :], ident[0:24, 0:24]).then_inc(cols_pe, 1)

            for n in range(2 * NB):
                b, h = n // 2, n % 2
                if h == 0:
                    pe.wait_ge(x_scaled, b + 1)
                if n >= 4:
                    pe.wait_ge(xt_act, n - 3)
                for k in range(4):
                    last = transpose(bank[2 + n % 4][:, P * k:P * (k + 1)], x_tok[:, b, P * (4 * h + k):P * (4 * h + k + 1)])
                last.then_inc(xt_pe, 1)

            def modulation(m, bk):
                first = (0, 8, 12)[m]
                for g in range(4):
                    arrived(first + g)
                for k in range(KD):
                    for g in range(4):
                        last = mm(bk[32 * g:32 * (g + 1), :], cb[:, k], wide(first + g)[:, k],
                                  start=k == 0, stop=k == KD - 1)
                last.then_inc(ada_pe, 1)

            def modulation_columns(m, bk):
                pe.wait_ge(ada_dve, m + 1)
                for j in range(4):
                    last = transpose(bk[:, P * j:P * (j + 1)], mod[:, P * j:P * (j + 1)])
                last.then_inc(adaT_pe, 1)

            def gate_rows(m, bk):
                pe.wait_ge(adaT_dve, m + 1)
                for h in range(2):
                    if h:
                        pe.wait_ge(gt_dve, 2 * (m - 1) + h)
                    g = 2 * (m - 1) + h
                    mm(bk[:, :], ident[:, 32 * g:32 * g + 1].broadcast_to([P, P]), mod[:, :],
                       start=True, stop=True).then_inc(gt_pe, 1)

            pe.wait_ge(cols_dve, 1)
            modulation(0, bank[0])
            modulation_columns(0, bank[0])

            pe.wait_ge(h_ready, 1)
            pe.wait_ge(xt_act, 2 * NB)
            arrived(4)
            for b in range(NB):
                for k in range(KD):
                    last = mm(bank[2 + b][:, 0:324], hT[:, k, P * b:P * (b + 1)], wide(4, 324)[:, k],
                              start=k == 0, stop=k == KD - 1)
                last.then_inc(d_pe, 1)

            def project(b):
                if b == 0:
                    pe.wait_ge(d_act, 3)
                elif b == 1:
                    pe.wait_ge(is_act, 3 * IDXH)
                else:
                    pe.wait_ge(qkT_act, b - 1)
                for n, c in enumerate((cA, cC, cB)):
                    if b == 0:
                        arrived(c)
                    bk = bank[2 + 3 * (b % 2) + n]
                    for k in range(KD):
                        last = mm(bk[:, :], hT[:, k, P * b:P * (b + 1)], wide(c)[:, k], start=k == 0, stop=k == KD - 1)
                    last.then_inc(pr_pe, 1)

            def transpose_heads(b):
                pe.wait_ge(qk_rope, b + 1)
                base = 2 + 3 * (b % 2)
                for n in range(2):
                    for j in range(4):
                        transpose(bank[base + n][:, P * j:P * (j + 1)], rt[:, 640 * n + P * j:640 * n + P * (j + 1)])
                for n in range(2):
                    last = transpose(bank[base + 2][:, P * n:P * (n + 1)], rt[:, 640 * n + 512:640 * n + 640])
                last.then_inc(qkT_pe, 1)

            project(0)
            for b in range(NB):
                pe.wait_ge(d_rope, b + 1)
                if b >= 2:
                    pe.wait_ge(dT_act, b - 1)
                for c in range(3):
                    last = transpose(bank[b % 2][:, P * c:P * (c + 1)], rtd[:, b % 2, P * c:P * (c + 1)])
                last.then_inc(dT_pe, 1)
            pe.wait_ge(dT_act, NB)
            pe.wait_ge(d_act, NB)
            for n in range(3 * IDXH):
                b, h = 1 + n // IDXH, n % IDXH
                if n >= 3:
                    pe.wait_ge(is_act, n - 2)
                mm(bank[5 + n % 3][:, 0:P * (b + 1)], iqT[:, h // 2, P * b:P * (b + 1)], ikz[:, h % 2, 0:P * (b + 1)],
                   start=True, stop=True).then_inc(is_pe, 1)
            for b in range(1, NB):
                project(b)
                transpose_heads(b - 1)
            transpose_heads(NB - 1)

            def scores(g):
                n, b = GROUPS[g]
                tiles = key_tiles(n, b)
                w = P * len(tiles)
                for h in range(HEADS):
                    u = HEADS * g + h
                    if u >= 3:
                        pe.wait_ge(s_dve, u - 2)
                    mm(bank[u % 3][:, 0:w], qT[:, n, h % 4, P * b:P * (b + 1)],
                       kz[:, n, h // 4, P * tiles[0]:P * tiles[0] + w], start=True, stop=True).then_inc(s_pe, 1)

            def weigh(g):
                n, b = GROUPS[g]
                tiles = key_tiles(n, b)
                w = P * len(tiles)
                pe.wait_ge(p_scaled, g + 1)
                if g >= 2:
                    pe.wait_ge(y_dve, g - 1)
                for i, t in enumerate(tiles):
                    k = tiles_to[g] + i
                    for z in range(2):
                        if k:
                            pe.wait_ge((pT_act, pT_dve)[z], k)
                        for j in range(4):
                            h = 4 * z + j
                            last = transpose(bank[4 + z][:, P * j:P * (j + 1)], prob[n][:, w * h + P * i:w * h + P * (i + 1)])
                        last.then_inc(pT_pe, 1)
                    for z in range(2):
                        pe.wait_ge((pT_act, pT_dve)[z], k + 1)
                        last = mm(bank[6 + g % 2][64 * z:64 * (z + 1), :], vt[:, t, n, 64 * z:64 * (z + 1)],
                                  pt[k % 2][:, 512 * z:512 * (z + 1)], start=i == 0, stop=i == len(tiles) - 1)
                    last.then_inc(pv_pe, 1)

            pe.wait_ge(qkT_act, NB)
            for g in range(len(GROUPS) + 1):
                if g < len(GROUPS):
                    scores(g)
                m = MOD_AT.get(g)
                if m:
                    if m == 2:
                        pe.wait_ge(gt_dve, 2)
                    modulation(m, bank[3])
                if g >= 1:
                    weigh(g - 1)
                if m:
                    modulation_columns(m, bank[3])
                    gate_rows(m, bank[3])

            pe.wait_ge(y_dve, len(GROUPS))
            pe.wait_ge(gt_dve, 4)
            for d in range(KD):
                if d >= 2:
                    pe.wait_ge(merge_dve, d - 1)
                base = 4 * (d % 2)
                for n in range(2):
                    c = cG[n, d // 4]
                    arrived(c)
                    for k in range(KD):
                        last = mm(bank[base + n][:, :], wide(c)[:, k, P * (d % 4):P * (d % 4 + 1)], hT[:, k],
                                  start=k == 0, stop=k == KD - 1)
                    last.then_inc(gate_pe, 1)
                for n in range(2):
                    c = cBr[n]
                    arrived(c)
                    w = slot(c % 5).rearrange("p (j n) -> p j n", j=4)
                    for j in range(4):
                        last = mm(bank[base + 2 + n][:, :], w[:, j, P * d:P * (d + 1)], yT[:, n, j],
                                  start=j == 0, stop=j == 3)
                    last.then_inc(up_pe, 1)

            def output_projection(b):
                if b == 0:
                    pe.wait_ge(merge_dve, KD)
                if b >= 2:
                    pe.wait_ge(x1_dve, b - 1)
                for h in range(2):
                    arrived(cO[h])
                    for k in range(KD):
                        last = mm(bank[2 * (b % 2) + h][:, :], merged[:, k, P * b:P * (b + 1)], wide(cO[h])[:, k],
                                  start=k == 0, stop=k == KD - 1)
                    last.then_inc(o_pe, 1)

            def route(b):
                pe.wait_ge(xn2_dve, b + 1)
                for h in range(2):
                    if b >= 1:
                        pe.wait_ge((x2T_act, x2T_dve)[h], b)
                    for k in range(4):
                        last = transpose(bank[4 + h][:, P * k:P * (k + 1)], xn2[:, b % 2, P * (4 * h + k):P * (4 * h + k + 1)])
                    last.then_inc(x2T_pe, 1)
                pe.wait_ge(x2T_act, b + 1)
                pe.wait_ge(x2T_dve, b + 1)
                if b == 0:
                    pe.wait_ge(router_in, 32)
                else:
                    pe.wait_ge(lg_dve, b)
                for k in range(KD):
                    last = mm(bank[6][:, 0:NROUTE], h2T[:, k], wr[:, k], start=k == 0, stop=k == KD - 1)
                last.then_inc(lg_pe, 1)

            output_projection(0)
            for b in range(1, NB):
                output_projection(b)
                route(b - 1)
            route(NB - 1)

            pe.wait_ge(m_dve, 1)
            mm(bank[0][:, 0:P], tri, picks, start=True, stop=False)
            mm(bank[0][:, 0:P], ones, before, start=False, stop=True)
            mm(bank[1][:, 0:NE], ones, per_part, start=True, stop=True).then_inc(rank_pe, 1)
            pe.wait_ge(locs_dve, 1)

            def experts(i):
                pe.wait_ge(x_got, i * 16 + 16)
                for k in range(KD):
                    last = transpose(bank[k // 4][:, P * (k % 4):P * (k % 4 + 1)], xg[:, P * k:P * (k + 1)])
                last.then_inc(xgT_pe, 1)
                pe.wait_ge(xgT_act, i + 1)
                pe.wait_ge(xgT_dve, i + 1)
                for s in range(2):
                    for n, (w, used) in enumerate(((wg_t(s), wg_used), (wu_t(s), wu_used))):
                        pe.wait_ge(piece_in[s][n], i * 16 + 16)
                        for k in range(KD):
                            for h in range(2):
                                last = mm(bank[2 + n][64 * h:64 * (h + 1), 0:256], xT[:, k, SLOTS * s:SLOTS * (s + 1)],
                                          w[:, k, 256 * h:256 * (h + 1)], start=k == 0, stop=k == KD - 1)
                        last.then_inc(used, 1)
                    pe.wait_ge(hid_dve, i * 2 + s + 1)
                    for c in range(2):
                        last = transpose(bank[4][:, P * c:P * (c + 1)], hid[:, P * c:P * (c + 1)])
                    last.then_inc(hidT_pe, 1)
                    pe.wait_ge(hidT_act, i * 2 + s + 1)
                    pe.wait_ge(piece_in[s][2], i * 16 + 16)
                    for q in range(4):
                        for g in range(2):
                            last = mm(bank[5 + s][64 * g:64 * (g + 1), :], hidT[:, q % 2, q // 2],
                                      wd_t(s)[:, q, 512 * g:512 * (g + 1)], start=q == 0, stop=q == 3)
                    last.then_inc(wd_used, 1)

            experts(0)
            with pe.Fori(1, PAIRS) as i:
                experts(i)
            pe.wait_ge(over_dve, 1)
            n_over = pe.value_load(nover_i[0:1, 0:1], min_val=0, max_val=MAXOVER)
            with pe.If(n_over > 0):
                with pe.Fori(PAIRS, ALLPAIRS) as i:
                    experts(i)

        @block.vector
        def _(dve):
            v = nc.vector
            own = [0]

            def mark(ins):
                own[0] += 1
                return ins.then_inc(dve_step, 1)

            def own_done():
                dve.wait_ge(dve_step, own[0])

            def step(ins):
                mark(ins)
                own_done()

            dve.wait_ge(cols_pe, 1)
            step(v.tensor_copy(cols24[:, :], bank[1][:, 0:24]))
            v.tensor_copy(cb[:, :, :], cols24[:, 16:24].unsqueeze(2).broadcast_to([P, KD, 32])).then_inc(cols_dve, 1)

            dve.wait_ge(ss_act, NB)
            v.tensor_scalar(st[:, 1], st[:, 0], 1.0 / D, EPS, ALU.mult, ALU.add).then_inc(rstd_t, 1)
            dve.wait_ge(rstd_act, 1)
            step(v.reciprocal(st[:, 2], st[:, 2]))
            for b in range(NB):
                v.tensor_scalar(x_tok[:, b], x_tok[:, b], st[:, 2, b:b + 1], None, ALU.mult).then_inc(x_scaled, 1)

            dve.wait_ge(pos_in, 16)
            dve.wait_ge(const_in, 16)
            step(v.tensor_copy(pos_f[:, :], pos_i[:, :]))
            ang, turns, red, tmp = (atmp[:, u] for u in range(4))
            for b in range(NB):
                mark(v.tensor_scalar(ang[:, 32 * b:32 * (b + 1)], C("freq"), pos_f[:, b:b + 1], None, ALU.mult))
            own_done()
            step(v.tensor_scalar(turns, ang, 1.0 / (2 * np.pi), None, ALU.mult))
            step(v.tensor_scalar(turns, turns, ROUNDER, None, ALU.add))
            step(v.tensor_scalar(turns, turns, ROUNDER, None, ALU.subtract))
            step(v.scalar_tensor_tensor(red, turns, -TWO_PI_HI, ang, ALU.mult, ALU.add))
            step(v.scalar_tensor_tensor(red, turns, -TWO_PI_MID, red, ALU.mult, ALU.add))
            step(v.scalar_tensor_tensor(red, turns, -TWO_PI_LO, red, ALU.mult, ALU.add))
            step(v.tensor_scalar(red, red, PI_IN, -PI_IN, ALU.min, ALU.max))
            step(v.tensor_scalar(tmp, red, np.pi / 2, None, ALU.is_gt))
            step(v.scalar_tensor_tensor(tmp, tmp, -2 * np.pi, red, ALU.mult, ALU.add))
            step(v.tensor_scalar(tmp, tmp, np.pi / 2, None, ALU.add))
            step(v.tensor_scalar(tmp, tmp, PI_IN, -PI_IN, ALU.min, ALU.max))
            a4 = args.rearrange("p (b u n) -> p b u n", b=NB, u=4)
            for u in range(2):
                v.tensor_copy(a4[:, :, u], tmp.rearrange("p (b n) -> p b n", b=NB)).then_inc(ang_part, 1)
            v.tensor_scalar(a4[:, :, 2], red.rearrange("p (b n) -> p b n", b=NB), -1.0, None,
                            ALU.mult).then_inc(ang_part, 1)
            v.tensor_copy(a4[:, :, 3], red.rearrange("p (b n) -> p b n", b=NB)).then_inc(ang_dve, 1)

            def modulation(m, bk):
                dve.wait_ge(ada_pe, m + 1)
                if m == 0:
                    dve.wait_ge(bias_in, 64)
                v.tensor_tensor(mod[:, :], bk[:, :], bias_ada[:, m], ALU.add).then_inc(ada_dve, 1)
                dve.wait_ge(adaT_pe, m + 1)
                cols = bk[:, :].rearrange("p (j g r) -> p g j r", j=4, g=4)[:, :, :, 0]
                v.tensor_copy(modT[:, 16 * m:16 * (m + 1)].rearrange("p (g j) -> p g j", g=4), cols
                              ).then_inc(adaT_dve, 1)

            def gate_rows(m, bk):
                for h in range(2):
                    dve.wait_ge(gt_pe, 2 * (m - 1) + h + 1)
                    v.tensor_copy(gt_rows[:, m - 1, 512 * h:512 * (h + 1)], bk[:, :]).then_inc(gt_dve, 1)

            def scale_shift(n, gain, sc, sh):
                mark(v.scalar_tensor_tensor(scm[:, 2 * n], modT[:, sc:sc + KD], 1.0, gain, ALU.add, ALU.mult))
                mark(v.tensor_copy(scm[:, 2 * n + 1], modT[:, sh:sh + KD]))
                own_done()

            modulation(0, bank[0])
            dve.wait_ge(adaT_dve, 1)
            scale_shift(0, cols24[:, 0:8], 8, 0)
            dve.wait_ge(xt_act, 2 * NB)
            for k in range(KD):
                last = v.tensor_scalar(hT[:, k], hT[:, k], scm[:, 0, k:k + 1], scm[:, 1, k:k + 1], ALU.mult, ALU.add)
                if k < KD - 1:
                    last.then_inc(h_part, 1)
            last.then_inc(h_ready, 1)

            def rotate(src, heads, cos, sin, a, b):
                s3 = src.rearrange("p (h d) -> p h d", h=heads)
                a3 = a.rearrange("p (h d) -> p h d", h=heads)
                s4 = src.rearrange("p (h u d) -> p h u d", h=heads, u=2)
                b4 = b.rearrange("p (h u d) -> p h u d", h=heads, u=2)
                mark(v.tensor_tensor(a3, s3, cos.unsqueeze(1).broadcast_to([P, heads, HD]), ALU.mult))
                for u in range(2):
                    mark(v.tensor_tensor(b4[:, :, u], s4[:, :, 1 - u],
                                         sin[:, 32 * u:32 * (u + 1)].unsqueeze(1).broadcast_to([P, heads, 32]), ALU.mult))

            dve.wait_ge(ang_act, 1)
            for b in range(NB):
                dve.wait_ge(d_act, b + 1)
                if b:
                    dve.wait_ge(d_rope, b)
                mark(v.tensor_scalar(iw[:, b], rawd[:, b, 320:324], (IDXH * HD) ** -0.5, None, ALU.mult))
                rotate(rawd[:, b, 0:320], 5, rope_cs[:, b, 0], rope_cs[:, b, 1], tad, tbd)
                own_done()
                if b >= 2:
                    dve.wait_ge(dT_pe, b - 1)
                mark(v.tensor_tensor(rtd[:, b % 2, 0:320], tad, tbd, ALU.add))
                v.tensor_tensor(rtd[:, b % 2, 320:384], tad[:, 256:320], tbd[:, 256:320], ALU.add).then_inc(d_rope, 1)

            for n in range(3 * IDXH):
                b, h = 1 + n // IDXH, n % IDXH
                w = P * (b + 1)
                dve.wait_ge(is_act, n + 1)
                if h:
                    dve.wait_ge(is_dve, n)
                    ins = v.scalar_tensor_tensor(idx[:, b - 1, 0:w], relu[:, n % 2, 0:w], iw[:, b, h:h + 1],
                                                 idx[:, b - 1, 0:w], ALU.mult, ALU.add)
                else:
                    ins = v.tensor_scalar(idx[:, b - 1, 0:w], relu[:, n % 2, 0:w], iw[:, b, h:h + 1], None, ALU.mult)
                ins.then_inc(is_dve, 1)

            def top_k(b):
                w = P * (b + 1)
                m = idx[:, b - 1, 0:w]
                dve.wait_ge(is_dve, IDXH * b)
                step(v.tensor_tensor(idx[:, b - 1, P * b:w], idx[:, b - 1, P * b:w], win[:, P:2 * P], ALU.add))
                for _ in range(TOPK // 8):
                    step(v.max(top8[:, :], m))
                    step(v.match_replace(m, top8[:, :], m, TAKEN))
                step(v.tensor_scalar(m, m, TAKEN / 2, NEG, ALU.is_gt, ALU.mult))

            kinds = ((0, 8), (8, 2), (10, 8), (18, 2))

            def norm_and_rotate(b):
                dve.wait_ge(pr_act, b + 1)
                if b:
                    dve.wait_ge(qk_rope, b)
                step(v.tensor_reduce(hst[:, 0], sq.rearrange("p (h d) -> p h d", h=20), AX, ALU.add))
                v.tensor_scalar(hst[:, 1], hst[:, 0], 1.0 / HD, EPS, ALU.mult, ALU.add).then_inc(hss_dve, 1)
                if b == 0:
                    dve.wait_ge(gains_in, 32)
                for u in range(2):
                    mark(v.tensor_tensor(gtab[:, u], gains[:, u], rope_cs[:, b, u].unsqueeze(1).broadcast_to([P, 4, HD]),
                                         ALU.mult))
                dve.wait_ge(hrt_act, b + 1)
                step(v.reciprocal(hst[:, 0], hst[:, 2]))
                r3 = raw[b % 2].rearrange("p (h d) -> p h d", h=20)
                step(v.tensor_tensor(r3, r3, hst[:, 0].unsqueeze(2).broadcast_to([P, 20, HD]), ALU.mult))
                for k, (h0, hn) in enumerate(kinds):
                    c = slice(HD * h0, HD * (h0 + hn))
                    rotate(raw[b % 2][:, c], hn, gtab[:, 0, k], gtab[:, 1, k], ta[:, c], tb[:, c])
                own_done()
                if b >= 1:
                    dve.wait_ge(qkT_pe, b)
                for k, (h0, hn) in enumerate(kinds):
                    c = slice(HD * h0, HD * (h0 + hn))
                    if hn == HEADS:
                        i0, i1 = (t[:, c].rearrange("p (z j d) -> p z j d", z=2, j=4) for t in (ta, tb))
                        ins = v.tensor_tensor(rt[:, c].rearrange("p (j z d) -> p z j d", z=2, j=4), i0, i1, ALU.add)
                    else:
                        ins = v.tensor_tensor(rt[:, c], ta[:, c], tb[:, c], ALU.add)
                    if k < 3:
                        mark(ins)
                    else:
                        ins.then_inc(qk_rope, 1)

            for b in range(NB - 1):
                top_k(b + 1)
                norm_and_rotate(b)
            norm_and_rotate(NB - 1)

            step(v.tensor_scalar(sinks[:, 1], sinks[:, 0], -1.0, None, ALU.mult))

            def soften(g):
                n, b = GROUPS[g]
                w = P * len(key_tiles(n, b))
                if b == 0:
                    mask = win[:, P:2 * P]
                else:
                    mask = win if n == 0 else idx[:, b - 1, 0:w]
                if g == 0:
                    dve.wait_ge(qk_rope, NB)
                elif g >= 2:
                    dve.wait_ge(y_dve, g - 1)
                for h in range(HEADS):
                    u = HEADS * g + h
                    dve.wait_ge(s_pe, u + 1)
                    v.tensor_tensor_reduce(out=prob[n][:, w * h:w * (h + 1)], in0=bank[u % 3][:, 0:w], in1=mask,
                                           scale=-(HD ** -0.5), scalar=sinks[:, 1, h:h + 1] if n == 0 else 3e38,
                                           op0=ALU.add, op1=ALU.min, accum_out=nmax[:, g % 2, h:h + 1]
                                           ).then_inc(s_dve, 1)
                if n == 0:
                    dve.wait_ge(s_dve, HEADS * (g + 1))
                    v.tensor_tensor(sinkt[:, 0], nmax[:, g % 2], sinks[:, 0], ALU.add).then_inc(sink_dve, 1)

            def finish(g):
                n, b = GROUPS[g]
                tiles = key_tiles(n, b)
                w = P * len(tiles)
                dve.wait_ge(p_act, HEADS * (g + 1))
                rs = rsum[:, g % 2]
                if n == 0:
                    dve.wait_ge(sink_act, b + 1)
                    step(v.tensor_tensor(rs, rs, sinkt[:, 1], ALU.add))
                step(v.reciprocal(rs, rs))
                for h in range(HEADS):
                    pr = prob[n][:, w * h:w * (h + 1)]
                    ins = v.tensor_scalar(pr, pr, rs[:, h:h + 1], None, ALU.mult)
                    if h < HEADS - 1:
                        mark(ins)
                    else:
                        ins.then_inc(p_scaled, 1)
                for k in range(tiles_to[g], tiles_to[g + 1]):
                    dve.wait_ge(pT_pe, 2 * k + 2)
                    if k >= 2:
                        dve.wait_ge(pv_pe, k - 1)
                    v.tensor_copy(pt[k % 2][:, 512:1024], bank[5][:, :]).then_inc(pT_dve, 1)
                dve.wait_ge(pv_pe, tiles_to[g + 1])
                v.tensor_copy(yT[:, n, :, P * b:P * (b + 1)], bank[6 + g % 2][:, :].rearrange("p (j t) -> p j t", j=4)
                              ).then_inc(y_dve, 1)

            for g in range(len(GROUPS) + 1):
                if g < len(GROUPS):
                    soften(g)
                if g >= 1:
                    finish(g - 1)
                m = MOD_AT.get(g)
                if m:
                    modulation(m, bank[3])
                    gate_rows(m, bank[3])
            dve.wait_ge(adaT_dve, 3)
            scale_shift(1, cols24[:, 8:16], 32, 24)

            for d in range(KD):
                base = 4 * (d % 2)
                dve.wait_ge(up_pe, 2 * (d + 1))
                dve.wait_ge(sig_act, d + 1)
                if d:
                    dve.wait_ge(merge_dve, d)
                for n in range(2):
                    mark(v.tensor_tensor(mtmp[:, n], bank[base + 2 + n][:, :], sig[:, d % 2, n], ALU.mult))
                own_done()
                v.tensor_tensor(merged[:, d], mtmp[:, 0], mtmp[:, 1], ALU.add).then_inc(merge_dve, 1)

            dve.wait_ge(xre_in, 16)

            def residual(b):
                for h in range(2):
                    c = slice(512 * h, 512 * (h + 1))
                    dve.wait_ge(o_pe, 2 * b + h + 1)
                    own_done()
                    step(v.tensor_tensor(ores, bank[2 * (b % 2) + h][:, :], gt_rows[:, 0, c], ALU.mult))
                    last = v.tensor_tensor(x_tok[:, b, c], x_tok[:, b, c], ores, ALU.add)
                    if h == 0:
                        mark(last)
                last.then_inc(x1_dve, 1)
                dve.wait_ge(ss2_act, b + 1)
                v.tensor_scalar(st[:, 1, b:b + 1], st[:, 0, b:b + 1], 1.0 / D, EPS, ALU.mult, ALU.add).then_inc(rt2_dve, 1)
                dve.wait_ge(rt2_act, b + 1)
                step(v.reciprocal(st[:, 2, b:b + 1], st[:, 2, b:b + 1]))
                if b >= 2:
                    dve.wait_ge(xn_stored[b % 2], 16)
                    dve.wait_ge(x2T_pe, 2 * (b - 1))
                v.tensor_scalar(xn2[:, b % 2], x_tok[:, b], st[:, 2, b:b + 1], None, ALU.mult).then_inc(xn2_dve, 1)

            def router_logits(b):
                dve.wait_ge(x2T_pe, 2 * b + 2)
                if b >= 1:
                    dve.wait_ge(lg_pe, b)
                for k in range(4, KD):
                    last = v.tensor_scalar(h2T[:, k], bank[5][:, P * (k - 4):P * (k - 3)], scm[:, 2, k:k + 1],
                                           scm[:, 3, k:k + 1], ALU.mult, ALU.add)
                    if k < KD - 1:
                        mark(last)
                last.then_inc(x2T_dve, 1)
                dve.wait_ge(lg_pe, b + 1)
                if b == 0:
                    dve.wait_ge(router_in, 32)
                v.tensor_tensor(logits[:, b], bank[6][:, 0:NROUTE], route_bias[:, :], ALU.add).then_inc(lg_dve, 1)

            residual(0)
            for b in range(1, NB):
                residual(b)
                router_logits(b - 1)
            router_logits(NB - 1)

            dve.wait_ge(lg_dve, NB)
            prio = C("prio")

            def b3(a, n):
                return a.unsqueeze(2).broadcast_to([*a.shape, n])

            def first_greatest(vals, n, top, hot, work):
                step(v.tensor_reduce(top, vals, AX, ALU.max))
                step(v.tensor_tensor(hot, vals, b3(top, n), ALU.is_equal))
                step(v.tensor_tensor(hot, hot, prio[:, 0:n].unsqueeze(1).broadcast_to([P, NB, n]), ALU.mult))
                step(v.tensor_reduce(work, hot, AX, ALU.max))
                step(v.tensor_tensor(hot, hot, b3(work, n), ALU.is_equal))

            first_greatest(logits[:, :, 0:G], G, r_top[:, 0], r_hotg, r_top[:, 3])
            mark(v.tensor_tensor(rexp[:, 0:16].rearrange("p (b g) -> p b g", b=NB), logits[:, :, 0:G],
                                 b3(r_top[:, 0], G), ALU.subtract))
            step(v.tensor_scalar(r_hotg, r_hotg, -NEG, NEG, ALU.mult, ALU.add))
            step(v.tensor_tensor(r_le.rearrange("p b (g e) -> p b g e", g=G),
                                 logits[:, :, G:].rearrange("p b (g e) -> p b g e", g=G),
                                 r_hotg.unsqueeze(3).broadcast_to([P, NB, G, EPG]), ALU.add))
            first_greatest(r_le, NE, r_top[:, 1], r_hot[:, 0], r_top[:, 3])
            step(v.scalar_tensor_tensor(r_le, r_hot[:, 0], 3 * NEG, r_le, ALU.mult, ALU.add))
            first_greatest(r_le, NE, r_top[:, 2], r_hot[:, 1], r_top[:, 3])
            v.tensor_tensor(rexp[:, 16:20], r_top[:, 2], r_top[:, 1], ALU.subtract).then_inc(rexp_dve, 1)
            picks3 = picks.rearrange("p (b e) -> p b e", b=NB)
            before3 = before.rearrange("p (b e) -> p b e", b=NB)
            mark(v.memset(before3[:, 0], 0.0))
            step(v.tensor_tensor(picks3, r_hot[:, 0], r_hot[:, 1], ALU.add))
            for b in range(1, NB):
                step(v.tensor_tensor(before3[:, b], before3[:, b - 1], picks3[:, b - 1], ALU.add))
            v.tensor_tensor(per_part, before3[:, NB - 1], picks3[:, NB - 1], ALU.add).then_inc(m_dve, 1)

            dve.wait_ge(rank_pe, 1)
            step(v.tensor_copy(r_cnt, bank[1][:, 0:NE]))
            step(v.tensor_scalar(r_ov[:, 0], r_cnt, float(SLOTS), None, ALU.is_gt))
            for k in range(2, S // SLOTS):
                step(v.scalar_tensor_tensor(r_ov[:, 0], r_cnt, float(SLOTS * k), r_ov[:, 0], ALU.is_gt, ALU.add))
            step(v.tensor_copy(r_ov[:, 1], r_ov[:, 0]))
            a, b_ = 1, 2
            for d in (1, 2, 4, 8, 16):
                mark(v.tensor_copy(r_ov[:, b_, 0:d], r_ov[:, a, 0:d]))
                step(v.tensor_tensor(r_ov[:, b_, d:], r_ov[:, a, d:], r_ov[:, a, 0:NE - d], ALU.add))
                a, b_ = b_, a
            upto = r_ov[:, a]
            step(v.tensor_tensor(r_cmp, upto.unsqueeze(1).broadcast_to([P, MAXOVER, NE]),
                                 C("over").unsqueeze(2).broadcast_to([P, MAXOVER, NE]), ALU.is_le))
            step(v.tensor_reduce(r_exp, r_cmp, AX, ALU.add))
            step(v.tensor_scalar(r_exp, r_exp, float(NE - 1), None, ALU.min))
            mark(v.tensor_copy(oexp_i[:, :], r_exp))
            own_done()
            v.tensor_copy(nover_i[:, :], upto[:, NE - 1:NE]).then_inc(over_dve, 1)
            step(v.tensor_tensor(r_ov[:, b_], upto, r_ov[:, 0], ALU.subtract))
            step(v.tensor_scalar(r_ov[:, b_], r_ov[:, b_], float(SLOTS), float(SLOTS * (NE - 1)), ALU.mult, ALU.add))
            step(v.tensor_tensor(r_ov[:, b_], r_ov[:, b_], C("e64"), ALU.subtract))
            step(v.tensor_copy(r_loc, bank[0][:, 0:P]))
            r_loc3 = r_loc.rearrange("p (b e) -> p b e", b=NB)
            step(v.tensor_scalar(r_le, r_loc3, float(SLOTS), None, ALU.is_ge))
            step(v.tensor_tensor(r_le, r_le, r_ov[:, b_].unsqueeze(1).broadcast_to([P, NB, NE]), ALU.mult))
            step(v.tensor_tensor(r_loc3, r_loc3, r_le, ALU.add))
            step(v.tensor_tensor(r_loc3, r_loc3, C("e64").unsqueeze(1).broadcast_to([P, NB, NE]), ALU.add))
            for n in range(2):
                step(v.tensor_tensor(r_le, r_loc3, r_hot[:, n], ALU.mult))
                step(v.tensor_reduce(r_top[:, 4 + n], r_le, AX, ALU.add))
            step(v.tensor_copy(loc_i[:, :, :], r_top[:, 4:6]))
            loc_flat = loc_i[:, :, :].rearrange("p n b -> p (n b)")
            mark(v.tensor_scalar(addr_i[:, 0], loc_flat, P - 1, None, ALU.bitwise_and))
            mark(v.tensor_scalar(addr_i[:, 1], loc_flat, 7, None, ALU.arith_shift_right))
            own_done()
            v.scalar_tensor_tensor(addr_i[:, 2], addr_i[:, 0], float(ALLPAIRS), addr_i[:, 1], ALU.mult, ALU.add
                                   ).then_inc(locs_dve, 1)
            dve.wait_ge(rexp_act, 1)
            step(v.tensor_reduce(r_top[:, 3], rexp[:, 0:16].rearrange("p (b g) -> p b g", b=NB), AX, ALU.add))
            step(v.reciprocal(r_top[:, 3], r_top[:, 3]))
            step(v.tensor_scalar(cw[:, 0], rexp[:, 16:20], 1.0, None, ALU.add))
            step(v.reciprocal(cw[:, 0], cw[:, 0]))
            step(v.tensor_tensor(cw[:, 0], cw[:, 0], r_top[:, 3], ALU.mult))
            step(v.tensor_tensor(cw[:, 1], cw[:, 0], rexp[:, 16:20], ALU.mult))

            def experts(i, first):
                dve.wait_ge(xgT_pe, i + 1)
                for k in range(4, KD):
                    last = v.tensor_scalar(xT[:, k], bank[1][:, P * (k - 4):P * (k - 3)], scm[:, 2, k:k + 1],
                                           scm[:, 3, k:k + 1], ALU.mult, ALU.add)
                last.then_inc(xgT_dve, 1)
                for s in range(2):
                    dve.wait_ge(silu_act, i * 2 + s + 1)
                    dve.wait_ge(wu_used, i * 2 + s + 1)
                    v.tensor_tensor(hid, bank[3][:, 0:256], act_g, ALU.mult).then_inc(hid_dve, 1)
                    dve.wait_ge(wd_used, i * 2 + s + 1)
                    if not first:
                        dve.wait_ge(y_stored[s], i * 32)
                    v.tensor_copy(ysb[:, s], bank[5 + s][:, :]).then_inc(ydn_dve, 1)

            experts(0, True)
            with dve.Fori(1, PAIRS) as i:
                experts(i, False)
            n_over = dve.value_load(nover_i[0:1, 0:1], min_val=0, max_val=MAXOVER)
            with dve.If(n_over > 0):
                with dve.Fori(PAIRS, ALLPAIRS) as i:
                    experts(i, False)

            for b in range(NB):
                dve.wait_ge(y_got[b % 2], 32 * (b // 2 + 1))
                ya, yb = y12[:, b % 2, 0], y12[:, b % 2, 1]
                step(v.tensor_scalar(ya, ya, cw[:, 0, b:b + 1], None, ALU.mult))
                step(v.scalar_tensor_tensor(ya, yb, cw[:, 1, b:b + 1], ya, ALU.mult, ALU.add))
                step(v.tensor_tensor(ya, ya, gt_rows[:, 1], ALU.mult))
                v.tensor_tensor(x_tok[:, b], x_tok[:, b], ya, ALU.add).then_inc(fin_dve, 1)


_INS = ("x", "c", "w_ada", "b_ada", "g_norm_mix", "w_in", "sinks_a", "w_branch", "w_out", "g_norm_ffn",
        "w_expert_gate", "w_expert_up", "w_expert_down")


def kernel(**inputs):
    import concourse.bacc as bacc
    from concourse.bass_utils import run_bass_kernel_spmd

    nc = bacc.Bacc("TRN2", target_bir_lowering=False, num_devices=1)
    arrays = {name: np.ascontiguousarray(inputs[name]) for name in _INS}
    arrays["positions"] = np.ascontiguousarray(np.reshape(inputs["positions"], (NB, P)).T)
    head = np.concatenate([inputs[n] for n in ("q_norm_a", "k_norm_a", "q_norm_b", "k_norm_b")])
    swapped = np.concatenate([head[:, HD // 2:], head[:, :HD // 2]], axis=1)
    arrays["head_gains"] = np.concatenate([head, swapped]).reshape(1, 8 * HD)
    arrays["route_bias"] = np.concatenate([inputs["b_group"], np.reshape(inputs["b_router"], (1, NE))], axis=1)
    by_model = np.transpose(inputs["w_router"][0], (1, 0, 2)).reshape(D, NE)
    arrays["w_route"] = np.concatenate([inputs["w_group"][0], by_model], axis=1)
    arrays["consts"] = shape_constants()
    arrays["token_ids"] = token_ids()
    access = {name: nc.dram_tensor(f"in_{name}", a.shape, mybir.dt.from_np(a.dtype), kind="ExternalInput").ap()
              for name, a in arrays.items()}
    access["out"] = nc.dram_tensor("out_y", (1, S, D), F32, kind="ExternalOutput").ap()
    build_block(nc, access)
    r = run_bass_kernel_spmd(nc, [{f"in_{name}": a for name, a in arrays.items()}], core_ids=[0])
    return r.results[0]["out_y"]
```

```python
from contextlib import ExitStack

import concourse.bass as bass
from concourse import mybir
import numpy as np

F32 = mybir.dt.float32
I32 = mybir.dt.int32
U32 = mybir.dt.uint32
ALU = mybir.AluOpType
ACT = mybir.ActivationFunctionType
AX = mybir.AxisListType.X

P = 128
D = 1024
S = 512
CHUNK = 64
HD = 64
KD = D // P
NB = S // P
HEADS = 8
KVH = 2
IDXH = 4
TOPK = min(256, S // 4)
G = 4
EPG = 8
NE = G * EPG
FE = 512
NROUTE = G + NE
EPS = 1e-6
NEG = -1e30
TAKEN = -3e38
SLOTS = 64
PAIRS = NE // 2
MAXOVER = (2 * S) // SLOTS
OPAIRS = MAXOVER // 2
ALLPAIRS = PAIRS + OPAIRS
HALF = D // 2
ROWS = 2 * S + P
GATE0 = 1860
WCH = 4096
TWO_PI_HI = 6.28125
TWO_PI_MID = float(np.float32(2 * np.pi - 6.28125))
TWO_PI_LO = float(2 * np.pi - 6.28125 - TWO_PI_MID)
ROUNDER = 12582912.0
PI_IN = 3.1415925

CONST = {}
_at = 0
for _name, _w in (("ident", P), ("tri", P), ("ones", P), ("win", 2 * P), ("freq", 32),
                  ("prio", NE), ("e64", NE), ("over", MAXOVER), ("count", SLOTS),
                  ("ids", 2 * NB), ("row0", 1), ("spare", 1)):
    CONST[_name] = (_at, _at + _w)
    _at += _w
CONST_W = _at


def shape_constants():
    c = np.zeros((P, CONST_W), np.float32)

    def put(name, a):
        lo, hi = CONST[name]
        c[:, lo:hi] = a

    i = np.arange(P)
    put("ident", np.eye(P))
    put("tri", (i[:, None] < i[None, :]))
    put("ones", 1.0)
    win = np.full((P, 2 * P), NEG)
    win[:CHUNK, CHUNK:3 * CHUNK] = 0.0
    win[CHUNK:, 2 * CHUNK:] = 0.0
    put("win", win)
    half = HD // 2
    put("freq", 10000.0 ** (-np.arange(half) / half))
    put("prio", NE - np.arange(NE))
    put("e64", SLOTS * np.arange(NE))
    put("over", np.arange(MAXOVER))
    put("count", np.arange(SLOTS))
    put("ids", np.tile(i[:, None] + P * np.arange(NB)[None, :] - S, 2))
    put("row0", (2 * S + (i >= SLOTS))[:, None])
    put("spare", (2 * (i % SLOTS))[:, None])
    return c


def place(where):
    kind, n = where
    tiles = (1, 2, 4, 6, 8, 11, 13, 17)
    if kind == "project":
        return (0, n, 0)
    if kind == "heads":
        return (0, n + 1, 1)
    if kind == "scores":
        return (1, n, 0)
    return (1, 1 + sum(n >= t for t in tiles), 1 + n)


def build_block(nc, A):
    with ExitStack() as ctx:
        def sb(name, shape, dt=F32):
            return ctx.enter_context(nc.sbuf_tensor(name, shape, dt))

        def sem(name):
            return ctx.enter_context(nc.semaphore(name))

        bank = [ctx.enter_context(nc.psum_tensor(f"bank{i}", [P, 512], F32)) for i in range(8)]

        ring = sb("ring", [P, 5 * WCH])
        qk = sb("qk", [P, 2 * WCH])
        scr = sb("scr", [P, 2 * WCH])
        r1 = sb("r1", [P, WCH])
        hT_ = sb("hT", [P, WCH])
        vt = sb("vt", [P, NB, 2, KVH * HD])
        idx = sb("idx", [P, 3, S])
        bias_ada = sb("bias_ada", [P, 3, 512])
        mod = sb("mod", [P, 512])
        con = sb("con", [P, CONST_W])
        rope_cs = sb("rope_cs", [P, NB, 2, HD])
        gains = sb("gains", [P, 2, 4, HD])
        wr = sb("wr", [P, KD, NROUTE])
        route_bias = sb("route_bias", [P, NROUTE])
        rows24 = sb("rows24", [24, P])
        cols24 = sb("cols24", [P, 24])
        modT = sb("modT", [P, 48])
        scm = sb("scm", [P, 4, KD])
        cb = sb("cb", [P, KD, 32])
        pos_i = sb("pos_i", [P, NB], I32)
        pos_f = sb("pos_f", [P, NB])
        sinks = sb("sinks", [P, 2, HEADS])
        picked = sb("picked", [P, 2 * NB, 2])
        st = sb("st", [P, 3, NB])
        hst = sb("hst", [P, 3, 20])
        iw = sb("iw", [P, NB, IDXH])
        top8 = sb("top8", [P, 8])
        nmax = sb("nmax", [P, 2, HEADS])
        rsum = sb("rsum", [P, 2, HEADS])
        sinkt = sb("sinkt", [P, 2, HEADS])
        slots_in = sb("slots_in", [P, ALLPAIRS], I32)
        ids_out = sb("ids_out", [P, 2 * ALLPAIRS])
        weights_out = sb("weights_out", [P, 2 * ALLPAIRS])
        row_f = sb("row_f", [P, 2, 2 * ALLPAIRS])
        row_i = sb("row_i", [P, 2 * ALLPAIRS], I32)
        loc_i = sb("loc_i", [P, 3, 2 * NB], I32)
        loc_f = sb("loc_f", [P, 2, 2 * NB])
        nover_i = sb("nover_i", [P, 1], I32)
        oexp_i = sb("oexp_i", [P, MAXOVER], I32)
        logits = sb("logits", [P, NB, NROUTE])
        rexp = sb("rexp", [P, 5 * NB])

        def C(name):
            lo, hi = CONST[name]
            return con[:, lo:hi]

        ident, tri, ones = C("ident"), C("tri"), C("ones")
        win = C("win")

        def slot(i):
            if i < 5:
                return ring[:, WCH * i:WCH * (i + 1)]
            return (qk[:, 0:WCH], qk[:, WCH:2 * WCH], hT_[:, :], r1[:, :])[i - 5]

        QK_LOW, QK_HIGH, HT, R1 = 5, 6, 7, 8
        GATE_SLOTS = (4, 0)

        hT = hT_[:, :].rearrange("p (k t) -> p k t", k=KD)
        x_tok = r1[:, :].rearrange("p (b d) -> p b d", b=NB)
        yT = r1[:, :].rearrange("p (n j t) -> p n j t", n=2, j=4)
        qT = qk[:, 0:WCH].rearrange("p (n j t) -> p n j t", n=2, j=4)
        kz = qk[:, WCH:WCH + 2048].rearrange("p (n z t) -> p n z t", n=2, z=2)
        iqT = qk[:, WCH + 2048:WCH + 3072].rearrange("p (c t) -> p c t", c=2)
        ikz = qk[:, WCH + 3072:WCH + 4096].rearrange("p (z t) -> p z t", z=2)
        gt_m = bias_ada[:, 0:2].rearrange("p h n -> p (h n)")
        gt_f = bias_ada[:, 2]
        raw = [scr[:, 1280 * i:1280 * (i + 1)] for i in range(2)]
        ta, tb, rt = (scr[:, 2560 + 1280 * i:3840 + 1280 * i] for i in range(3))
        sq = scr[:, 6400:7680]
        gtab = scr[:, 7680:8192].rearrange("p (u k d) -> p u k d", u=2, k=4)
        sq_junk = scr[:, 0:4096].rearrange("p (b d) -> p b d", b=NB)
        args = scr[:, 4096:4608]
        atmp = scr[:, 4608:5120].rearrange("p (u n) -> p u n", u=4)
        rawd = r1[:, 0:1296].rearrange("p (b c) -> p b c", b=NB)
        rtd = r1[:, 1296:1296 + 768].rearrange("p (u c) -> p u c", u=2)
        tad = r1[:, 2064:2384]
        tbd = r1[:, 2384:2704]
        relu = r1[:, 3072:4096].rearrange("p (u s) -> p u s", u=2)
        prob = {0: scr[:, 0:2048], 1: scr[:, 2048:6144]}
        pt = [scr[:, 6144 + 1024 * i:7168 + 1024 * i] for i in range(2)]
        merged = scr[:, 0:WCH].rearrange("p (k t) -> p k t", k=KD)
        gates = [slot(i).rearrange("p (n d t) -> p n d t", n=2, d=4) for i in GATE_SLOTS]
        mtmp = scr[:, 6144:7168].rearrange("p (n t) -> p n t", n=2)
        ores = scr[:, 7168:7680]
        xn2 = scr[:, 4096:6144].rearrange("p (u d) -> p u d", u=2)
        h2T = scr[:, 6144:7168].rearrange("p (k t) -> p k t", k=KD)
        xg = [scr[:, 2048 + 1024 * u:3072 + 1024 * u] for u in range(3)]
        xT = scr[:, 5120:6144].rearrange("p (k t) -> p k t", k=KD)
        act_g = scr[:, 6144:6400]
        hid = scr[:, 6400:6656]
        hidT = scr[:, 6656:6912].rearrange("p (c h s) -> p c h s", c=2, h=2)
        ysb = scr[:, 7168:8192].rearrange("p (u d) -> p u d", u=2)
        def rw(at, n):
            return scr[:, at:at + n]

        vt_flat = vt[:, :, :, :].rearrange("p b n d -> p (b n d)")

        r_top = rw(0, 8 * NB).rearrange("p (u b) -> p u b", u=8)
        r_hotg = rw(32, 16).rearrange("p (b g) -> p b g", b=NB)
        r_le = rw(64, P).rearrange("p (b e) -> p b e", b=NB)
        r_hot = rw(192, 2 * P).rearrange("p (u b e) -> p u b e", u=2, b=NB)
        picks, before, per_part, r_cnt, r_loc = rw(448, P), rw(576, P), rw(704, NE), rw(736, NE), rw(768, P)
        r_ov = rw(896, 3 * NE).rearrange("p (u e) -> p u e", u=3)
        r_exp = rw(992, MAXOVER)
        r_cmp = rw(1024, MAXOVER * NE).rearrange("p (j e) -> p j e", j=MAXOVER)

        in_tile = rw(1536, 2 * NB * 2 * ALLPAIRS).rearrange("p (u t) -> p u t", u=2 * NB)
        in_slot = rw(5120, 2 * NB * SLOTS).rearrange("p (u q) -> p u q", u=2 * NB)
        tile_vals = rw(6144, 4 * NB * 2 * ALLPAIRS).rearrange("p (u o t) -> p u o t", u=2 * NB, o=2)

        xn_dram = nc.dram_tensor("xn_rows", [S, D], F32, kind="Internal").ap()
        out_tokens = A["out"][0:2 * S, :].rearrange("(t g) n -> t (g n)", g=2)

        w_ada = A["w_ada"][0].rearrange("(k p) n -> p k n", p=P)
        w_in = A["w_in"][0].rearrange("(k p) n -> p k n", p=P)
        w_out = A["w_out"][0].rearrange("(k p) n -> p k n", p=P)

        def wide(i, w=512):
            return slot(chunk_slot[i])[:, 0:KD * w].rearrange("p (k n) -> p k n", k=KD)

        def deep(i):
            return slot(chunk_slot[i]).rearrange("p (k n) -> p k n", k=2)

        def ada(i, m, q):
            return [(deep(i), w_ada[:, 2 * q:2 * q + 2, 2048 * m:2048 * (m + 1)])]

        def inproj(i, c0, w=512):
            return [(wide(i, w), w_in[:, :, c0:c0 + w])]

        def branch(i, n):
            dst = slot(chunk_slot[i]).rearrange("p (j n) -> p j n", j=4)
            src = A["w_branch"][0, n].rearrange("(g j p) n -> g p j n", g=2, j=4)
            return [(dst[64 * g:64 * (g + 1)], src[g]) for g in range(2)]

        cA, cC, cB = 5, 6, 7
        cG = {(0, 0): 8, (1, 0): 9, (0, 1): 10, (1, 1): 11}
        cM = {(0, q): q for q in range(4)} | {(1, q): 12 + q for q in range(4)}
        cM |= {(2, 0): 16, (2, 1): 19, (2, 2): 20, (2, 3): 22}
        cBr = {0: 17, 1: 18}
        cO = {1: 21, 0: 23}
        chunk_slot = [0, 1, 2, 3, 4, 0, 1, 2, 3, R1, 3, 1, 2, 2, 2, 2, 2, 3, 1, HT, QK_LOW, QK_HIGH, HT, 2]
        kv_dst = wide(cC).rearrange("p k (u n) -> p k u n", u=2)
        chunks = ({c: ada(c, m, q) for (m, q), c in cM.items()}
                  | {4: inproj(4, 1536, 324), cA: inproj(cA, 0),
                     cC: [(kv_dst[:, :, 0], w_in[:, :, 512:768]), (kv_dst[:, :, 1], w_in[:, :, 1280:1536])],
                     cB: inproj(cB, 768)}
                  | {c: inproj(c, GATE0 + D * n + 512 * h) for (n, h), c in cG.items()}
                  | {c: branch(c, n) for n, c in cBr.items()}
                  | {c: [(wide(c), w_out[:, :, 512 * h:512 * (h + 1)])] for h, c in cO.items()})
        chunks = [chunks[i] for i in range(len(chunks))]
        chunk_in = [sem(f"chunk_in{i}") for i in range(9)]
        const_in, x_in, rows_in, bias_in = sem("const_in"), sem("x_in"), sem("rows_in"), sem("bias_in")
        pos_in, gains_in, router_in, xre_in = sem("pos_in"), sem("gains_in"), sem("router_in"), sem("xre_in")
        cols_pe, cols_dve = sem("cols_pe"), sem("cols_dve")
        ss_act, rstd_t, rstd_act, x_scaled = sem("ss_act"), sem("rstd_t"), sem("rstd_act"), sem("x_scaled")
        xt_pe, xt_act = sem("xt_pe"), sem("xt_act")
        ada_pe, ada_dve, adaT_pe, adaT_dve = sem("ada_pe"), sem("ada_dve"), sem("adaT_pe"), sem("adaT_dve")
        h_ready = sem("h_ready")
        gt_pe, gt_dve = sem("gt_pe"), sem("gt_dve")
        ang_dve, ang_act = sem("ang_dve"), sem("ang_act")
        zeros_pool = sem("zeros_pool")
        d_pe, d_act, d_rope, dT_pe, dT_act = sem("d_pe"), sem("d_act"), sem("d_rope"), sem("dT_pe"), sem("dT_act")
        is_pe, is_act, is_dve = sem("is_pe"), sem("is_act"), sem("is_dve")
        pr_pe, pr_act, hss_dve, hrt_act, qk_rope = (sem("pr_pe"), sem("pr_act"), sem("hss_dve"), sem("hrt_act"),
                                                    sem("qk_rope"))
        qkT_pe, qkT_act = sem("qkT_pe"), sem("qkT_act")
        s_pe, s_dve, p_act = sem("s_pe"), sem("s_dve"), sem("p_act")
        sink_dve, sink_act, p_scaled = sem("sink_dve"), sem("sink_act"), sem("p_scaled")
        pT_pe, pT_act, pT_dve, pv_pe, y_dve = sem("pT_pe"), sem("pT_act"), sem("pT_dve"), sem("pv_pe"), sem("y_dve")
        gate_pe, gate_act, up_pe, sig_act, merge_dve = (sem("gate_pe"), sem("gate_act"), sem("up_pe"),
                                                        sem("sig_act"), sem("merge_dve"))
        o_pe, x1_dve, ss2_act, rt2_dve, rt2_act, xn2_dve = (sem("o_pe"), sem("x1_dve"), sem("ss2_act"),
                                                            sem("rt2_dve"), sem("rt2_act"), sem("xn2_dve"))
        xn_stored = [sem(f"xn_stored{i}") for i in range(2)]
        x2T_pe, x2T_act, x2T_dve, lg_pe, lg_dve = (sem("x2T_pe"), sem("x2T_act"), sem("x2T_dve"),
                                                   sem("lg_pe"), sem("lg_dve"))
        rexp_dve, rexp_act, m_dve, rank_pe, locs_dve = (sem("rexp_dve"), sem("rexp_act"), sem("m_dve"),
                                                        sem("rank_pe"), sem("locs_dve"))
        over_dve = sem("over_dve")
        table_pe, slots_dve = sem("table_pe"), sem("slots_dve")
        x_got = [sem(f"x_got{i}") for i in range(3)]
        piece_in = [[sem(f"{n}_in{s}") for n in ("wg", "wu", "wd")] for s in range(3)]
        wg_used, wu_used, wd_used = sem("wg_used"), sem("wu_used"), sem("wd_used")
        xgT_pe, xgT_act, xgT_dve = sem("xgT_pe"), sem("xgT_act"), sem("xgT_dve")
        silu_act, hid_dve, hidT_pe, hidT_act, ydn_dve = (
            sem("silu_act"), sem("hid_dve"), sem("hidT_pe"), sem("hidT_act"), sem("ydn_dve"))
        y_added = [sem(f"y_added{s}") for s in range(2)]
        x1_stored, cw_dve, row_dve, xg_zero = sem("x1_stored"), sem("cw_dve"), sem("row_dve"), sem("xg_zero")
        dve_step = sem("dve_step")
        ang_part, h_part, v_act = sem("ang_part"), sem("h_part"), sem("v_act")

        arrivals = {}
        loaded = [0] * 9
        for i, pieces in enumerate(chunks):
            loaded[chunk_slot[i]] += 16 * len(pieces)
            arrivals[i] = (chunk_in[chunk_slot[i]], loaded[chunk_slot[i]])

        through = {cM[m, q]: (ada_pe, 4 * m + q + 1) for m in range(3) for q in range(4)}
        through |= {4: (d_pe, NB), cA: (pr_pe, 3 * NB - 2), cC: (pr_pe, 3 * NB - 1), cB: (pr_pe, 3 * NB)}
        through |= {cG[n, h]: (gate_pe, 8 * h + 4 * n + 4) for n in range(2) for h in range(2)}
        through |= {cBr[n]: (up_pe, 2 * KD - 1 + n) for n in range(2)}
        through |= {cO[h]: (o_pe, 2 * NB - 1 + h) for h in range(2)}

        eslots = ((3, 0, 1), (4, HT, QK_LOW), (2, QK_HIGH, R1))
        left = {3: through[cBr[0]], 1: through[cBr[1]], 4: (merge_dve, KD // 2), 0: (merge_dve, KD),
                HT: through[cM[2, 3]], QK_LOW: through[cM[2, 2]], QK_HIGH: through[cO[1]], 2: through[cO[0]]}

        def expert_weights(s):
            g, u, d = (slot(x) for x in eslots[s])
            return (g.rearrange("p (k n) -> p k n", k=KD), u.rearrange("p (k n) -> p k n", k=KD),
                    d.rearrange("p (k n) -> p k n", k=4))

        eg_dram = A["w_expert_gate"][0].rearrange("g e (k p) n -> (g e) p k n", p=P)
        eu_dram = A["w_expert_up"][0].rearrange("g e (k p) n -> (g e) p k n", p=P)
        ed_dram = A["w_expert_down"][0].rearrange("g e (k p) n -> (g e) p k n", p=P)

        GROUPS = [(n, b) for b in range(NB) for n in range(2)]

        def key_tiles(n, b):
            return list(range(max(0, b - 1), b + 1)) if n == 0 else list(range(b + 1))

        TILES = [(g, i, t) for g, (n, b) in enumerate(GROUPS) for i, t in enumerate(key_tiles(n, b))]
        tiles_to = [sum(len(key_tiles(*GROUPS[x])) for x in range(g)) for g in range(len(GROUPS) + 1)]

        ADA_AT = {0: (1, 0), 1: (1, 1), 2: (1, 2), 3: (1, 3), 7: (2, 0), 8: (2, 1)}

        GATE_STEPS = {("project", 1): 8, ("heads", 0): 4, ("project", 2): 6, ("heads", 1): 4, ("project", 3): 18,
                      ("heads", 2): 16, ("heads", 3): 8}
        GATE_STEPS |= {("scores", g): 8 for g in range(6)} | {("tile", k): 1 for k in range(8)} | {("scores", 6): 8}
        GATE_BANKS = [bank[u % 2] if u < KD else bank[7] for u in range(2 * KD)]
        UP_BANKS = ((bank[0], bank[1]), (bank[2], bank[4]), (bank[5], bank[6]))
        gate_steps_to = {}
        _done = 0
        for _at, _n in sorted(GATE_STEPS.items(), key=lambda kv: place(kv[0])):
            gate_steps_to[_at] = (_done, _done + _n)
            _done += _n

        block = ctx.enter_context(nc.Block())

        @block.sync
        def _(sp):
            sp.dma_start(con[:, :], A["consts"]).then_inc(const_in, 16)
            sp.dma_start(x_tok, A["x"][0].rearrange("(b p) d -> p b d", p=P)).then_inc(x_in, 16)
            for i, pieces in enumerate(chunks):
                before = [j for j in range(i) if chunk_slot[j] == chunk_slot[i]]
                if before:
                    sp.wait_ge(*through[before[-1]])
                elif chunk_slot[i] == R1:
                    sp.wait_ge(is_dve, 3 * IDXH)
                elif chunk_slot[i] == HT:
                    sp.wait_ge(gate_pe, 2 * KD)
                elif chunk_slot[i] in (QK_LOW, QK_HIGH):
                    sp.wait_ge(s_pe, HEADS * len(GROUPS))
                for dst, src in pieces:
                    sp.dma_start(dst, src).then_inc(chunk_in[chunk_slot[i]], 16)

            e_dram = (eg_dram, eu_dram, ed_dram)
            for t in range(3):
                for n, at in enumerate(eslots[t]):
                    if at == R1:
                        sp.wait_ge(x1_stored, 16 * (NB + 1))
                        sp.wait_ge(xn2_dve, NB)
                    else:
                        sp.wait_ge(*left[at])
                    sp.dma_start(expert_weights(t)[n], e_dram[n][t]).then_inc(piece_in[t][n], 16)

            def load_tile(j, s, e):
                before = (None, piece_in[s - 1][2], piece_in[s][0])
                for n, used in enumerate((wg_used, wu_used, wd_used)):
                    if n:
                        sp.wait_ge(before[n], j * 16 + (16 if n == 2 or s else 0))
                    sp.wait_ge(used, j * 3 + s - 2)
                    src = e_dram[n][bass.ds(e, 1)].rearrange("o p k n -> (o p) k n")
                    sp.dma_start(expert_weights(s)[n], src).then_inc(piece_in[s][n], 16)

            with sp.Fori(1, NE // 3) as j:
                for s in range(3):
                    load_tile(j, s, j * 3 + s)
            for s in range(NE % 3):
                load_tile(NE // 3, s, NE // 3 * 3 + s)
            sp.wait_ge(over_dve, 1)
            n_over = sp.value_load(nover_i[0:1, 0:1], min_val=0, max_val=MAXOVER)

            def overflow_expert(at):
                return sp.value_load(oexp_i[0:1, at], min_val=0, max_val=NE - 1)

            with sp.If(n_over > 0):
                load_tile(NE // 3, 2, overflow_expert(slice(0, 1)))
                with sp.Fori(NE // 3 + 1, (NE + MAXOVER) // 3) as j:
                    for s in range(3):
                        load_tile(j, s, overflow_expert(bass.ds(j * 3 + (s - NE), 1)))

        @block.gpsimd
        def _(pool):
            nc.gpsimd.memset(kz, 0.0).then_inc(zeros_pool, 1)
            nc.gpsimd.memset(ikz, 0.0).then_inc(zeros_pool, 1)
            pool.wait_ge(cw_dve, 2)
            for u in range(2):
                pool.wait_ge(xn_stored[u], 16 * NB // 2)
            for u in range(3):
                nc.gpsimd.memset(xg[u], 0.0).then_inc(xg_zero, 1)
            pool.wait_ge(slots_dve, 2)
            pool.wait_ge(xg_zero, 3)

            def fetch_tokens(i):
                if i >= 3:
                    pool.wait_ge(xgT_pe, i - 2)
                nc.gpsimd.indirect_dma_start(
                    out=xg[i % 3], out_offset=None, in_=xn_dram,
                    in_offset=bass.IndirectOffsetOnAxis(ap=slots_in[:, i:i + 1].bitcast(U32), axis=0),
                    bounds_check=S - 1, oob_is_err=False).then_inc(x_got[i % 3], 16)

            def add_rows(e):
                if e:
                    pool.wait_ge(y_added[(e - 1) % 2], 16 * ((e - 1) // 2 + 1))
                pool.wait_ge(ydn_dve, e + 1)
                nc.gpsimd.indirect_dma_start(
                    out=A["out"], out_offset=bass.IndirectOffsetOnAxis(
                        ap=row_i[:, e:e + 1].bitcast(U32), axis=0),
                    in_=ysb[:, e % 2], in_offset=None, compute_op=ALU.add).then_inc(y_added[e % 2], 16)

            fetch_tokens(0)
            fetch_tokens(1)
            pool.wait_ge(row_dve, 1)
            pool.wait_ge(x1_stored, 16 * (NB + 1))
            fetch_tokens(2)
            for i in range(PAIRS):
                if i + 3 < PAIRS:
                    fetch_tokens(i + 3)
                for s in range(2):
                    add_rows(2 * i + s)
            pool.wait_ge(over_dve, 1)
            n_over = pool.value_load(nover_i[0:1, 0:1], min_val=0, max_val=MAXOVER)
            with pool.If(n_over > 0):
                for i in range(PAIRS, ALLPAIRS):
                    fetch_tokens(i)
                    for s in range(2):
                        add_rows(2 * i + s)
                for s in range(2):
                    pool.wait_ge(y_added[s], 16 * ALLPAIRS)
            with pool.Else():
                for s in range(2):
                    pool.wait_ge(y_added[s], 16 * PAIRS)

        @block.scalar
        def _(act):
            for k, name in enumerate(("g_norm_mix", "g_norm_ffn", "c")):
                act.dma_start(rows24[8 * k:8 * k + 8, :], A[name][0].rearrange("(k p) -> k p", p=P)
                              ).then_inc(rows_in, 16)
            ba = A["b_ada"].rearrange("o (m g n) -> o g m n", m=3, g=4)
            for g in range(4):
                act.dma_start(bias_ada[32 * g:32 * (g + 1)], ba[:, g].broadcast_to([32, 3, 512])).then_inc(bias_in, 16)
            act.dma_start(pos_i[:, :], A["positions"]).then_inc(pos_in, 16)
            act.dma_start(sinks[:, 0, :], A["sinks_a"].broadcast_to([P, HEADS])).then_inc(gains_in, 16)
            act.dma_start(gains[:, :, :, :].rearrange("p u k d -> p (u k d)"),
                          A["head_gains"].broadcast_to([P, 8 * HD])).then_inc(gains_in, 16)
            act.dma_start(A["out"][2 * S:ROWS, :], A["zero_rows"]).then_inc(x1_stored, 16)
            act.dma_start(route_bias[:, :], A["route_bias"].broadcast_to([P, NROUTE])).then_inc(router_in, 16)
            act.dma_start(wr[:, :, :], A["w_route"].rearrange("(k p) n -> p k n", p=P)).then_inc(router_in, 16)

            act.wait_ge(x_in, 16)
            for b in range(NB):
                nc.scalar.activation(sq_junk[:, b], x_tok[:, b], ACT.Square, accum_out=st[:, 0, b:b + 1]).then_inc(ss_act, 1)
            act.wait_ge(rstd_t, 1)
            nc.scalar.activation(st[:, 2], st[:, 1], ACT.Sqrt).then_inc(rstd_act, 1)
            for n in range(2 * NB):
                b, h = n // 2, n % 2
                act.wait_ge(xt_pe, n + 1)
                nc.scalar.activation(hT[:, 4 * h:4 * h + 4, P * b:P * (b + 1)],
                                     bank[2 + n % 4][:, :].rearrange("p (k t) -> p k t", k=4),
                                     ACT.Copy).then_inc(xt_act, 1)
            act.wait_ge(ang_dve, 1)
            nc.scalar.activation(rope_cs[:, :, :, :].rearrange("p b u d -> p (b u d)"), args,
                                 ACT.Sin).then_inc(ang_act, 1)

            for b in range(NB):
                act.wait_ge(d_pe, b + 1)
                nc.scalar.activation(rawd[:, b], bank[2 + b][:, 0:324], ACT.Copy).then_inc(d_act, 1)

            def evac_projection(b):
                if b >= 2:
                    act.wait_ge(qk_rope, b - 1)
                act.wait_ge(pr_pe, 3 * (b + 1))
                ba_, bc_, bb_ = (bank[2 + 3 * (b % 2) + i] for i in range(3))
                kv = bc_[:, :].rearrange("p (n u d) -> p n u d", n=2, u=2)
                nc.scalar.activation(raw[b % 2][:, 0:512], ba_[:, :], ACT.Copy)
                nc.scalar.activation(raw[b % 2][:, 640:1152], bb_[:, :], ACT.Copy)
                for n in range(2):
                    nc.scalar.activation(raw[b % 2][:, 512 + 640 * n:640 + 640 * n], kv[:, n, 0], ACT.Copy)
                nc.scalar.activation(vt[:, b], kv[:, :, 1], ACT.Copy).then_inc(v_act, 1)
                if b >= 1:
                    act.wait_ge(hss_dve, b)
                nc.scalar.activation(sq[:, 0:512], ba_[:, :], ACT.Square)
                nc.scalar.activation(sq[:, 640:1152], bb_[:, :], ACT.Square)
                for n in range(2):
                    last = nc.scalar.activation(sq[:, 512 + 640 * n:640 + 640 * n], kv[:, n, 0], ACT.Square)
                last.then_inc(pr_act, 1)

            def store_gates(where):
                lo, hi = gate_steps_to.get(where, (0, 0))
                for u in range(lo // KD, hi // KD):
                    act.wait_ge(gate_pe, u + 1)
                    nc.scalar.activation(gates[u // 8][:, u // 4 % 2, u % 4], GATE_BANKS[u][:, :], ACT.Copy
                                         ).then_inc(gate_act, 1)

            def root_heads(b):
                act.wait_ge(hss_dve, b + 1)
                nc.scalar.activation(hst[:, 2], hst[:, 1], ACT.Sqrt).then_inc(hrt_act, 1)

            def evac_heads(b):
                act.wait_ge(qkT_pe, b + 1)
                base = 2 + 3 * (b % 2)
                t = slice(P * b, P * (b + 1))
                for n in range(2):
                    nc.scalar.activation(qT[:, n, :, t], bank[base + n][:, :].rearrange("p (j t) -> p j t", j=4),
                                         ACT.Copy)
                for n in range(2):
                    for z in range(2):
                        r = slice(64 * z, 64 * (z + 1))
                        last = nc.scalar.activation(kz[r, n, z, t], bank[base + 2][r, P * n:P * (n + 1)], ACT.Copy)
                last.then_inc(qkT_act, 1)

            evac_projection(0)
            act.wait_ge(zeros_pool, 2)
            for b in range(NB):
                act.wait_ge(dT_pe, b + 1)
                t = slice(P * b, P * (b + 1))
                bk = bank[b % 2]
                nc.scalar.activation(iqT[:, :, t], bk[:, 0:256].rearrange("p (c t) -> p c t", c=2), ACT.Copy)
                for z in range(2):
                    r = slice(64 * z, 64 * (z + 1))
                    last = nc.scalar.activation(ikz[r, z, t], bk[r, 256:384], ACT.Copy)
                last.then_inc(dT_act, 1)
            for n in range(3 * IDXH):
                b = 1 + n // IDXH
                act.wait_ge(is_pe, n + 1)
                if n >= 2:
                    act.wait_ge(is_dve, n - 1)
                nc.scalar.activation(relu[:, n % 2, 0:P * (b + 1)], bank[5 + n % 3][:, 0:P * (b + 1)],
                                     ACT.Relu).then_inc(is_act, 1)
            for b in range(1, NB):
                root_heads(b - 1)
                evac_projection(b)
                if b == NB - 1:
                    root_heads(b)
                store_gates(("project", b))
                evac_heads(b - 1)
                store_gates(("heads", b - 1))
            evac_heads(NB - 1)
            store_gates(("heads", NB - 1))

            def exps(g):
                n, b = GROUPS[g]
                w = P * len(key_tiles(n, b))
                for h in range(HEADS):
                    act.wait_ge(s_dve, HEADS * g + h + 1)
                    pr = prob[n][:, w * h:w * (h + 1)]
                    nc.scalar.activation(pr, pr, ACT.Exp, bias=nmax[:, g % 2, h:h + 1], scale=-1.0,
                                         accum_out=rsum[:, g % 2, h:h + 1]).then_inc(p_act, 1)
                if n == 0:
                    act.wait_ge(sink_dve, b + 1)
                    nc.scalar.activation(sinkt[:, 1], sinkt[:, 0], ACT.Exp).then_inc(sink_act, 1)

            def evac_probs(g):
                for k in range(tiles_to[g], tiles_to[g + 1]):
                    act.wait_ge(pT_pe, 2 * k + 1)
                    if k >= 2:
                        act.wait_ge(pv_pe, k - 1)
                    nc.scalar.activation(pt[k % 2][:, 0:512], bank[4][:, :], ACT.Copy).then_inc(pT_act, 1)
                    store_gates(("tile", k))

            for g in range(len(GROUPS)):
                exps(g)
                store_gates(("scores", g))
                if g >= 1:
                    evac_probs(g - 1)
            evac_probs(len(GROUPS) - 1)

            act.wait_ge(gate_act, 2 * KD)
            for d in range(KD):
                raw_gates = gates[d // 4][:, :, d % 4]
                nc.scalar.activation(raw_gates, raw_gates, ACT.Sigmoid).then_inc(sig_act, 1)
            act.wait_ge(up_pe, 2 * KD)
            act.dma_start(x_tok, A["x"][0].rearrange("(b p) d -> p b d", p=P)).then_inc(xre_in, 16)

            def norm2(b):
                act.wait_ge(x1_dve, b + 1)
                act.dma_start(out_tokens[P * b:P * (b + 1), :], x_tok[:, b]).then_inc(x1_stored, 16)
                nc.scalar.activation(vt_flat, x_tok[:, b], ACT.Square, accum_out=st[:, 0, b:b + 1]).then_inc(ss2_act, 1)
                act.wait_ge(rt2_dve, b + 1)
                nc.scalar.activation(st[:, 2, b:b + 1], st[:, 1, b:b + 1], ACT.Sqrt).then_inc(rt2_act, 1)
                act.wait_ge(xn2_dve, b + 1)
                act.dma_start(xn_dram[P * b:P * (b + 1), :], xn2[:, b % 2]).then_inc(xn_stored[b % 2], 16)

            def evac_h2(b):
                act.wait_ge(x2T_pe, 2 * b + 1)
                if b >= 1:
                    act.wait_ge(lg_pe, b)
                for k in range(4):
                    last = nc.scalar.activation(h2T[:, k], bank[4][:, P * k:P * (k + 1)], ACT.Identity,
                                                scale=scm[:, 2, k:k + 1], bias=scm[:, 3, k:k + 1])
                last.then_inc(x2T_act, 1)

            norm2(0)
            for b in range(1, NB):
                norm2(b)
                evac_h2(b - 1)
            evac_h2(NB - 1)
            act.wait_ge(rexp_dve, 1)
            nc.scalar.activation(rexp[:, :], rexp[:, :], ACT.Exp).then_inc(rexp_act, 1)

            def experts(i):
                act.wait_ge(xgT_pe, i + 1)
                for k in range(4):
                    last = nc.scalar.activation(xT[:, k], bank[0][:, P * k:P * (k + 1)], ACT.Identity,
                                                scale=scm[:, 2, k:k + 1], bias=scm[:, 3, k:k + 1])
                last.then_inc(xgT_act, 1)
                for s in range(2):
                    act.wait_ge(wg_used, i * 2 + s + 1)
                    nc.scalar.activation(act_g, bank[2][:, 0:256], ACT.Silu).then_inc(silu_act, 1)
                    act.wait_ge(hidT_pe, i * 2 + s + 1)
                    nc.scalar.activation(hidT, bank[4][:, 0:256].rearrange("p (c h s) -> p c h s", c=2, h=2),
                                         ACT.Copy).then_inc(hidT_act, 1)

            experts(0)
            with act.Fori(1, PAIRS) as i:
                experts(i)
            act.wait_ge(over_dve, 1)
            n_over = act.value_load(nover_i[0:1, 0:1], min_val=0, max_val=MAXOVER)
            with act.If(n_over > 0):
                with act.Fori(PAIRS, ALLPAIRS) as i:
                    experts(i)

        @block.tensor
        def _(pe):
            def arrived(i):
                pe.wait_ge(*arrivals[i])

            mm = nc.tensor.matmul

            def transpose(out, in_):
                return nc.tensor.transpose(out, in_, ident)

            pe.wait_ge(const_in, 16)
            pe.wait_ge(rows_in, 48)
            nc.tensor.transpose(bank[1][:, 0:24], rows24[:, :], ident[0:24, 0:24]).then_inc(cols_pe, 1)

            for n in range(2 * NB):
                b, h = n // 2, n % 2
                if h == 0:
                    pe.wait_ge(x_scaled, b + 1)
                if n >= 4:
                    pe.wait_ge(xt_act, n - 3)
                for k in range(4):
                    last = transpose(bank[2 + n % 4][:, P * k:P * (k + 1)], x_tok[:, b, P * (4 * h + k):P * (4 * h + k + 1)])
                last.then_inc(xt_pe, 1)

            def modulate(m, q, bk):
                c = cM[m, q]
                arrived(c)
                for k in range(2):
                    for g in range(4):
                        last = mm(bk[32 * g:32 * (g + 1), :], cb[:, 2 * q + k], deep(c)[:, k, 512 * g:512 * (g + 1)],
                                  start=q + k == 0, stop=q == 3 and k == 1)
                last.then_inc(ada_pe, 1)

            def modulation_columns(m, bk):
                pe.wait_ge(ada_dve, m + 1)
                for j in range(4):
                    last = transpose(bk[:, P * j:P * (j + 1)], mod[:, P * j:P * (j + 1)])
                last.then_inc(adaT_pe, 1)

            def mixer_gate_rows(h, bk):
                if h == 0:
                    pe.wait_ge(adaT_dve, 2)
                else:
                    pe.wait_ge(gt_dve, 1)
                mm(bk[:, :], ident[:, 32 * h:32 * h + 1].broadcast_to([P, P]), mod[:, :],
                   start=True, stop=True).then_inc(gt_pe, 1)

            def expert_gate_rows(bk):
                pe.wait_ge(adaT_dve, 3)
                for h in range(2):
                    last = mm(bk[64 * h:64 * (h + 1), :], ident[:, 64 + 32 * h:65 + 32 * h].broadcast_to([P, 64]),
                              mod[:, :], start=True, stop=True)
                last.then_inc(gt_pe, 1)

            pe.wait_ge(cols_dve, 1)
            for q in range(4):
                modulate(0, q, bank[0])
            modulation_columns(0, bank[0])

            pe.wait_ge(h_ready, 1)
            pe.wait_ge(xt_act, 2 * NB)
            arrived(4)
            for b in range(NB):
                for k in range(KD):
                    last = mm(bank[2 + b][:, 0:324], hT[:, k, P * b:P * (b + 1)], wide(4, 324)[:, k],
                              start=k == 0, stop=k == KD - 1)
                last.then_inc(d_pe, 1)

            def project(b):
                if b == 0:
                    pe.wait_ge(d_act, 3)
                elif b == 1:
                    pe.wait_ge(is_act, 3 * IDXH)
                else:
                    pe.wait_ge(qkT_act, b - 1)
                for n, c in enumerate((cA, cC, cB)):
                    if b == 0:
                        arrived(c)
                    bk = bank[2 + 3 * (b % 2) + n]
                    for k in range(KD):
                        last = mm(bk[:, :], hT[:, k, P * b:P * (b + 1)], wide(c)[:, k], start=k == 0, stop=k == KD - 1)
                    last.then_inc(pr_pe, 1)

            def transpose_heads(b):
                pe.wait_ge(qk_rope, b + 1)
                base = 2 + 3 * (b % 2)
                for n in range(2):
                    for j in range(4):
                        transpose(bank[base + n][:, P * j:P * (j + 1)], rt[:, 640 * n + P * j:640 * n + P * (j + 1)])
                for n in range(2):
                    last = transpose(bank[base + 2][:, P * n:P * (n + 1)], rt[:, 640 * n + 512:640 * n + 640])
                last.then_inc(qkT_pe, 1)

            def gate_products(where):
                for i in range(*gate_steps_to.get(where, (0, 0))):
                    u, k = i // KD, i % KD
                    half, n, d = u // 8, u // 4 % 2, u % 4
                    if k == 0:
                        if d == 0:
                            arrived(cG[n, half])
                        if u != KD and u >= 2:
                            pe.wait_ge(gate_act, u - 1 if u < KD else u)
                    last = mm(GATE_BANKS[u][:, :], wide(cG[n, half])[:, k, P * d:P * (d + 1)], hT[:, k],
                              start=k == 0, stop=k == KD - 1)
                    if k == KD - 1:
                        last.then_inc(gate_pe, 1)

            project(0)
            for b in range(NB):
                pe.wait_ge(d_rope, b + 1)
                if b >= 2:
                    pe.wait_ge(dT_act, b - 1)
                for c in range(3):
                    last = transpose(bank[b % 2][:, P * c:P * (c + 1)], rtd[:, b % 2, P * c:P * (c + 1)])
                last.then_inc(dT_pe, 1)
            pe.wait_ge(dT_act, NB)
            pe.wait_ge(d_act, NB)
            for n in range(3 * IDXH):
                b, h = 1 + n // IDXH, n % IDXH
                if n >= 3:
                    pe.wait_ge(is_act, n - 2)
                mm(bank[5 + n % 3][:, 0:P * (b + 1)], iqT[:, h // 2, P * b:P * (b + 1)], ikz[:, h % 2, 0:P * (b + 1)],
                   start=True, stop=True).then_inc(is_pe, 1)
            for b in range(1, NB):
                project(b)
                gate_products(("project", b))
                transpose_heads(b - 1)
                gate_products(("heads", b - 1))
            transpose_heads(NB - 1)
            gate_products(("heads", NB - 1))

            def scores(g):
                n, b = GROUPS[g]
                tiles = key_tiles(n, b)
                w = P * len(tiles)
                for h in range(HEADS):
                    u = HEADS * g + h
                    if u >= 3:
                        pe.wait_ge(s_dve, u - 2)
                    mm(bank[u % 3][:, 0:w], qT[:, n, h % 4, P * b:P * (b + 1)],
                       kz[:, n, h // 4, P * tiles[0]:P * tiles[0] + w], start=True, stop=True).then_inc(s_pe, 1)

            def weigh(g):
                n, b = GROUPS[g]
                tiles = key_tiles(n, b)
                w = P * len(tiles)
                pe.wait_ge(p_scaled, g + 1)
                if g:
                    pe.wait_ge(y_dve, g)
                for i, t in enumerate(tiles):
                    k = tiles_to[g] + i
                    for z in range(2):
                        if k:
                            pe.wait_ge((pT_act, pT_dve)[z], k)
                        for j in range(4):
                            h = 4 * z + j
                            last = transpose(bank[4 + z][:, P * j:P * (j + 1)], prob[n][:, w * h + P * i:w * h + P * (i + 1)])
                        last.then_inc(pT_pe, 1)
                    gate_products(("tile", k))
                    for z in range(2):
                        pe.wait_ge((pT_act, pT_dve)[z], k + 1)
                        last = mm(bank[6][64 * z:64 * (z + 1), :], vt[:, t, n, 64 * z:64 * (z + 1)],
                                  pt[k % 2][:, 512 * z:512 * (z + 1)], start=i == 0, stop=i == len(tiles) - 1)
                    last.then_inc(pv_pe, 1)

            pe.wait_ge(qkT_act, NB)
            pe.wait_ge(gate_act, KD)
            for g in range(len(GROUPS) + 1):
                if g == 4:
                    modulation_columns(1, bank[3])
                if g in (5, 6):
                    mixer_gate_rows(g - 5, bank[3])
                if g < len(GROUPS):
                    scores(g)
                    gate_products(("scores", g))
                if g in ADA_AT:
                    if ADA_AT[g] == (2, 0):
                        pe.wait_ge(gt_dve, 2)
                    modulate(*ADA_AT[g], bank[3])
                if g >= 1:
                    weigh(g - 1)

            pe.wait_ge(y_dve, len(GROUPS))
            for d in range(KD):
                if d >= 3:
                    pe.wait_ge(merge_dve, d - 2)
                for n in range(2):
                    c = cBr[n]
                    arrived(c)
                    w = slot(chunk_slot[c]).rearrange("p (j n) -> p j n", j=4)
                    for j in range(4):
                        last = mm(UP_BANKS[d % 3][n][:, :], w[:, j, P * d:P * (d + 1)], yT[:, n, j],
                                  start=j == 0, stop=j == 3)
                    last.then_inc(up_pe, 1)
                if d == 0:
                    modulate(2, 2, bank[3])
                elif d == 2:
                    modulate(2, 3, bank[3])
                elif d == 4:
                    modulation_columns(2, bank[3])
                elif d == 6:
                    expert_gate_rows(bank[3])

            def output_projection(b):
                if b == 0:
                    pe.wait_ge(merge_dve, KD)
                    pe.wait_ge(gt_dve, 3)
                if b >= 2:
                    pe.wait_ge(x1_dve, b - 1)
                for h in range(2):
                    arrived(cO[h])
                    for k in range(KD):
                        last = mm(bank[2 * (b % 2) + h][:, :], merged[:, k, P * b:P * (b + 1)], wide(cO[h])[:, k],
                                  start=k == 0, stop=k == KD - 1)
                    last.then_inc(o_pe, 1)

            def transpose_normed(b):
                pe.wait_ge(xn2_dve, b + 1)
                for h in range(2):
                    if b >= 1:
                        pe.wait_ge((x2T_act, x2T_dve)[h], b)
                    for k in range(4):
                        last = transpose(bank[4 + h][:, P * k:P * (k + 1)], xn2[:, b % 2, P * (4 * h + k):P * (4 * h + k + 1)])
                    last.then_inc(x2T_pe, 1)

            def route(b):
                pe.wait_ge(x2T_act, b + 1)
                pe.wait_ge(x2T_dve, b + 1)
                if b == 0:
                    pe.wait_ge(router_in, 32)
                else:
                    pe.wait_ge(lg_dve, b)
                for k in range(KD):
                    last = mm(bank[6][:, 0:NROUTE], h2T[:, k], wr[:, k], start=k == 0, stop=k == KD - 1)
                last.then_inc(lg_pe, 1)

            output_projection(0)
            output_projection(1)
            transpose_normed(0)
            for b in range(2, NB):
                output_projection(b)
                route(b - 2)
                transpose_normed(b - 1)
            route(NB - 2)
            transpose_normed(NB - 1)
            route(NB - 1)

            pe.wait_ge(m_dve, 1)
            mm(bank[0][:, 0:P], tri, picks, start=True, stop=False)
            mm(bank[0][:, 0:P], ones, before, start=False, stop=True)
            mm(bank[1][:, 0:NE], ones, per_part, start=True, stop=True).then_inc(rank_pe, 1)

            pe.wait_ge(locs_dve, 2)
            for u in range(2 * NB):
                for g in range(2):
                    last = mm(bank[2][SLOTS * g:SLOTS * (g + 1), 0:4 * ALLPAIRS], in_slot[:, u],
                              tile_vals[:, u].rearrange("p o t -> p (o t)"), start=u == 0, stop=u == 2 * NB - 1)
            last.then_inc(table_pe, 1)
            pe.wait_ge(row_dve, 1)

            def experts(j, u):
                i = j * 3 + u
                pe.wait_ge(x_got[u], j * 16 + 16)
                for k in range(KD):
                    last = transpose(bank[k // 4][:, P * (k % 4):P * (k % 4 + 1)], xg[u][:, P * k:P * (k + 1)])
                last.then_inc(xgT_pe, 1)
                pe.wait_ge(xgT_act, i + 1)
                pe.wait_ge(xgT_dve, i + 1)

                for s in range(2):
                    t = (2 * u + s) % 3
                    weights = expert_weights(t)

                    def weights_in(n):
                        pe.wait_ge(piece_in[t][n], j * 32 + 16 * ((2 * u + s) // 3 + 1))

                    for n, used in enumerate((wg_used, wu_used)):
                        w = weights[n]
                        weights_in(n)
                        for k in range(KD):
                            for h in range(2):
                                last = mm(bank[2 + n][64 * h:64 * (h + 1), 0:256], xT[:, k, SLOTS * s:SLOTS * (s + 1)],
                                          w[:, k, 256 * h:256 * (h + 1)], start=k == 0, stop=k == KD - 1)
                        last.then_inc(used, 1)
                    pe.wait_ge(hid_dve, i * 2 + s + 1)
                    for c in range(2):
                        last = transpose(bank[4][:, P * c:P * (c + 1)], hid[:, P * c:P * (c + 1)])
                    last.then_inc(hidT_pe, 1)
                    pe.wait_ge(hidT_act, i * 2 + s + 1)
                    weights_in(2)
                    for q in range(4):
                        for g in range(2):
                            last = mm(bank[5 + s][64 * g:64 * (g + 1), :], hidT[:, q % 2, q // 2],
                                      weights[2][:, q, 512 * g:512 * (g + 1)], start=q == 0, stop=q == 3)
                    last.then_inc(wd_used, 1)

            experts(0, 0)
            experts(0, 1)
            experts(0, 2)
            with pe.Fori(1, PAIRS // 3) as j:
                for u in range(3):
                    experts(j, u)
            experts(PAIRS // 3, 0)
            pe.wait_ge(over_dve, 1)
            n_over = pe.value_load(nover_i[0:1, 0:1], min_val=0, max_val=MAXOVER)
            with pe.If(n_over > 0):
                experts(PAIRS // 3, 1)
                experts(PAIRS // 3, 2)
                with pe.Fori(PAIRS // 3 + 1, ALLPAIRS // 3) as j:
                    for u in range(3):
                        experts(j, u)

        @block.vector
        def _(dve):
            v = nc.vector
            own = [0]

            def mark(ins):
                own[0] += 1
                return ins.then_inc(dve_step, 1)

            def own_done():
                dve.wait_ge(dve_step, own[0])

            def step(ins):
                mark(ins)
                own_done()

            dve.wait_ge(cols_pe, 1)
            step(v.tensor_copy(cols24[:, :], bank[1][:, 0:24]))
            v.tensor_copy(cb[:, :, :], cols24[:, 16:24].unsqueeze(2).broadcast_to([P, KD, 32])).then_inc(cols_dve, 1)

            dve.wait_ge(ss_act, NB)
            v.tensor_scalar(st[:, 1], st[:, 0], 1.0 / D, EPS, ALU.mult, ALU.add).then_inc(rstd_t, 1)
            dve.wait_ge(rstd_act, 1)
            step(v.reciprocal(st[:, 2], st[:, 2]))
            for b in range(NB):
                v.tensor_scalar(x_tok[:, b], x_tok[:, b], st[:, 2, b:b + 1], None, ALU.mult).then_inc(x_scaled, 1)

            def modulation_rows(m, bk):
                dve.wait_ge(ada_pe, 4 * (m + 1))
                if m == 0:
                    dve.wait_ge(bias_in, 64)
                v.tensor_tensor(mod[:, :], bk[:, :], bias_ada[:, m], ALU.add).then_inc(ada_dve, 1)

            def modulation_columns(m, bk):
                dve.wait_ge(adaT_pe, m + 1)
                cols = bk[:, :].rearrange("p (j g r) -> p g j r", j=4, g=4)[:, :, :, 0]
                v.tensor_copy(modT[:, 16 * m:16 * (m + 1)].rearrange("p (g j) -> p g j", g=4), cols
                              ).then_inc(adaT_dve, 1)

            def gate_rows(n, out, bk):
                dve.wait_ge(gt_pe, n + 1)
                dve.wait_ge(ada_dve, 2 + n // 2)
                v.tensor_copy(out, bk[:, :]).then_inc(gt_dve, 1)

            def scale_shift(n, gain, sc, sh):
                mark(v.scalar_tensor_tensor(scm[:, 2 * n], modT[:, sc:sc + KD], 1.0, gain, ALU.add, ALU.mult))
                mark(v.tensor_copy(scm[:, 2 * n + 1], modT[:, sh:sh + KD]))
                own_done()

            modulation_rows(0, bank[0])
            modulation_columns(0, bank[0])
            dve.wait_ge(adaT_dve, 1)
            scale_shift(0, cols24[:, 0:8], 8, 0)
            dve.wait_ge(xt_act, 2 * NB)
            for k in range(KD):
                last = v.tensor_scalar(hT[:, k], hT[:, k], scm[:, 0, k:k + 1], scm[:, 1, k:k + 1], ALU.mult, ALU.add)
                if k < KD - 1:
                    last.then_inc(h_part, 1)
            last.then_inc(h_ready, 1)

            dve.wait_ge(pos_in, 16)
            dve.wait_ge(const_in, 16)
            step(v.tensor_copy(pos_f[:, :], pos_i[:, :]))
            ang, turns, red, tmp = (atmp[:, u] for u in range(4))
            for b in range(NB):
                mark(v.tensor_scalar(ang[:, 32 * b:32 * (b + 1)], C("freq"), pos_f[:, b:b + 1], None, ALU.mult))
            own_done()
            step(v.tensor_scalar(turns, ang, 1.0 / (2 * np.pi), None, ALU.mult))
            step(v.tensor_scalar(turns, turns, ROUNDER, None, ALU.add))
            step(v.tensor_scalar(turns, turns, ROUNDER, None, ALU.subtract))
            step(v.scalar_tensor_tensor(red, turns, -TWO_PI_HI, ang, ALU.mult, ALU.add))
            step(v.scalar_tensor_tensor(red, turns, -TWO_PI_MID, red, ALU.mult, ALU.add))
            step(v.scalar_tensor_tensor(red, turns, -TWO_PI_LO, red, ALU.mult, ALU.add))
            step(v.tensor_scalar(red, red, PI_IN, -PI_IN, ALU.min, ALU.max))
            step(v.tensor_scalar(tmp, red, np.pi / 2, None, ALU.is_gt))
            step(v.scalar_tensor_tensor(tmp, tmp, -2 * np.pi, red, ALU.mult, ALU.add))
            step(v.tensor_scalar(tmp, tmp, np.pi / 2, None, ALU.add))
            step(v.tensor_scalar(tmp, tmp, PI_IN, -PI_IN, ALU.min, ALU.max))
            a4 = args.rearrange("p (b u n) -> p b u n", b=NB, u=4)
            for u in range(2):
                v.tensor_copy(a4[:, :, u], tmp.rearrange("p (b n) -> p b n", b=NB)).then_inc(ang_part, 1)
            v.tensor_scalar(a4[:, :, 2], red.rearrange("p (b n) -> p b n", b=NB), -1.0, None,
                            ALU.mult).then_inc(ang_part, 1)
            v.tensor_copy(a4[:, :, 3], red.rearrange("p (b n) -> p b n", b=NB)).then_inc(ang_dve, 1)

            def rotate(src, heads, cos, sin, a, b):
                s3 = src.rearrange("p (h d) -> p h d", h=heads)
                a3 = a.rearrange("p (h d) -> p h d", h=heads)
                s4 = src.rearrange("p (h u d) -> p h u d", h=heads, u=2)
                b4 = b.rearrange("p (h u d) -> p h u d", h=heads, u=2)
                mark(v.tensor_tensor(a3, s3, cos.unsqueeze(1).broadcast_to([P, heads, HD]), ALU.mult))
                for u in range(2):
                    mark(v.tensor_tensor(b4[:, :, u], s4[:, :, 1 - u],
                                         sin[:, 32 * u:32 * (u + 1)].unsqueeze(1).broadcast_to([P, heads, 32]), ALU.mult))

            dve.wait_ge(ang_act, 1)
            for b in range(NB):
                dve.wait_ge(d_act, b + 1)
                if b:
                    dve.wait_ge(d_rope, b)
                mark(v.tensor_scalar(iw[:, b], rawd[:, b, 320:324], (IDXH * HD) ** -0.5, None, ALU.mult))
                rotate(rawd[:, b, 0:320], 5, rope_cs[:, b, 0], rope_cs[:, b, 1], tad, tbd)
                own_done()
                if b >= 2:
                    dve.wait_ge(dT_pe, b - 1)
                mark(v.tensor_tensor(rtd[:, b % 2, 0:320], tad, tbd, ALU.add))
                v.tensor_tensor(rtd[:, b % 2, 320:384], tad[:, 256:320], tbd[:, 256:320], ALU.add).then_inc(d_rope, 1)

            for n in range(3 * IDXH):
                b, h = 1 + n // IDXH, n % IDXH
                w = P * (b + 1)
                dve.wait_ge(is_act, n + 1)
                if h:
                    dve.wait_ge(is_dve, n)
                    ins = v.scalar_tensor_tensor(idx[:, b - 1, 0:w], relu[:, n % 2, 0:w], iw[:, b, h:h + 1],
                                                 idx[:, b - 1, 0:w], ALU.mult, ALU.add)
                else:
                    ins = v.tensor_scalar(idx[:, b - 1, 0:w], relu[:, n % 2, 0:w], iw[:, b, h:h + 1], None, ALU.mult)
                ins.then_inc(is_dve, 1)

            def top_k(b):
                w = P * (b + 1)
                m = idx[:, b - 1, 0:w]
                dve.wait_ge(is_dve, IDXH * b)
                step(v.tensor_tensor(idx[:, b - 1, P * b:w], idx[:, b - 1, P * b:w], win[:, P:2 * P], ALU.add))
                for _ in range(TOPK // 8):
                    step(v.max(top8[:, :], m))
                    step(v.match_replace(m, top8[:, :], m, TAKEN))
                step(v.tensor_scalar(m, m, TAKEN / 2, NEG, ALU.is_gt, ALU.mult))

            kinds = ((0, 8), (8, 2), (10, 8), (18, 2))

            def norm_and_rotate(b):
                dve.wait_ge(pr_act, b + 1)
                if b:
                    dve.wait_ge(qk_rope, b)
                step(v.tensor_reduce(hst[:, 0], sq.rearrange("p (h d) -> p h d", h=20), AX, ALU.add))
                v.tensor_scalar(hst[:, 1], hst[:, 0], 1.0 / HD, EPS, ALU.mult, ALU.add).then_inc(hss_dve, 1)
                if b == 0:
                    dve.wait_ge(gains_in, 32)
                for u in range(2):
                    mark(v.tensor_tensor(gtab[:, u], gains[:, u], rope_cs[:, b, u].unsqueeze(1).broadcast_to([P, 4, HD]),
                                         ALU.mult))
                dve.wait_ge(hrt_act, b + 1)
                step(v.reciprocal(hst[:, 0], hst[:, 2]))
                r3 = raw[b % 2].rearrange("p (h d) -> p h d", h=20)
                step(v.tensor_tensor(r3, r3, hst[:, 0].unsqueeze(2).broadcast_to([P, 20, HD]), ALU.mult))
                for k, (h0, hn) in enumerate(kinds):
                    c = slice(HD * h0, HD * (h0 + hn))
                    rotate(raw[b % 2][:, c], hn, gtab[:, 0, k], gtab[:, 1, k], ta[:, c], tb[:, c])
                own_done()
                if b >= 1:
                    dve.wait_ge(qkT_pe, b)
                for k, (h0, hn) in enumerate(kinds):
                    c = slice(HD * h0, HD * (h0 + hn))
                    if hn == HEADS:
                        i0, i1 = (t[:, c].rearrange("p (z j d) -> p z j d", z=2, j=4) for t in (ta, tb))
                        ins = v.tensor_tensor(rt[:, c].rearrange("p (j z d) -> p z j d", z=2, j=4), i0, i1, ALU.add)
                    else:
                        ins = v.tensor_tensor(rt[:, c], ta[:, c], tb[:, c], ALU.add)
                    if k < 3:
                        mark(ins)
                    else:
                        ins.then_inc(qk_rope, 1)

            for b in range(NB - 1):
                top_k(b + 1)
                norm_and_rotate(b)
            norm_and_rotate(NB - 1)

            step(v.tensor_scalar(sinks[:, 1], sinks[:, 0], -1.0, None, ALU.mult))

            def soften(g):
                n, b = GROUPS[g]
                w = P * len(key_tiles(n, b))
                if b == 0:
                    mask = win[:, P:2 * P]
                else:
                    mask = win if n == 0 else idx[:, b - 1, 0:w]
                if g == 0:
                    dve.wait_ge(qk_rope, NB)
                elif g >= 2:
                    dve.wait_ge(y_dve, g - 1)
                for h in range(HEADS):
                    u = HEADS * g + h
                    dve.wait_ge(s_pe, u + 1)
                    v.tensor_tensor_reduce(out=prob[n][:, w * h:w * (h + 1)], in0=bank[u % 3][:, 0:w], in1=mask,
                                           scale=-(HD ** -0.5), scalar=sinks[:, 1, h:h + 1] if n == 0 else 3e38,
                                           op0=ALU.add, op1=ALU.min, accum_out=nmax[:, g % 2, h:h + 1]
                                           ).then_inc(s_dve, 1)
                if n == 0:
                    dve.wait_ge(s_dve, HEADS * (g + 1))
                    v.tensor_tensor(sinkt[:, 0], nmax[:, g % 2], sinks[:, 0], ALU.add).then_inc(sink_dve, 1)

            def finish(g):
                n, b = GROUPS[g]
                tiles = key_tiles(n, b)
                w = P * len(tiles)
                dve.wait_ge(p_act, HEADS * (g + 1))
                rs = rsum[:, g % 2]
                if n == 0:
                    dve.wait_ge(sink_act, b + 1)
                    step(v.tensor_tensor(rs, rs, sinkt[:, 1], ALU.add))
                step(v.reciprocal(rs, rs))
                for h in range(HEADS):
                    pr = prob[n][:, w * h:w * (h + 1)]
                    ins = v.tensor_scalar(pr, pr, rs[:, h:h + 1], None, ALU.mult)
                    if h < HEADS - 1:
                        mark(ins)
                    else:
                        ins.then_inc(p_scaled, 1)
                for k in range(tiles_to[g], tiles_to[g + 1]):
                    dve.wait_ge(pT_pe, 2 * k + 2)
                    if k >= 2:
                        dve.wait_ge(pv_pe, k - 1)
                    v.tensor_copy(pt[k % 2][:, 512:1024], bank[5][:, :]).then_inc(pT_dve, 1)
                dve.wait_ge(pv_pe, tiles_to[g + 1])
                v.tensor_copy(yT[:, n, :, P * b:P * (b + 1)], bank[6][:, :].rearrange("p (j t) -> p j t", j=4)
                              ).then_inc(y_dve, 1)

            for g in range(len(GROUPS) + 1):
                if g < len(GROUPS):
                    soften(g)
                if g >= 1:
                    finish(g - 1)
                if g == 3:
                    modulation_rows(1, bank[3])
                elif g == 4:
                    modulation_columns(1, bank[3])
                elif g in (5, 6):
                    gate_rows(g - 5, gt_m[:, 512 * (g - 5):512 * (g - 4)], bank[3])

            for d in range(KD):
                dve.wait_ge(up_pe, 2 * (d + 1))
                dve.wait_ge(sig_act, d + 1)
                if d:
                    dve.wait_ge(merge_dve, d)
                for n in range(2):
                    mark(v.tensor_tensor(mtmp[:, n], UP_BANKS[d % 3][n][:, :], gates[d // 4][:, n, d % 4], ALU.mult))
                own_done()
                v.tensor_tensor(merged[:, d], mtmp[:, 0], mtmp[:, 1], ALU.add).then_inc(merge_dve, 1)
                if d == 2:
                    modulation_rows(2, bank[3])
                elif d == 4:
                    modulation_columns(2, bank[3])
                elif d == 6:
                    gate_rows(2, gt_f, bank[3])
            dve.wait_ge(adaT_dve, 3)
            scale_shift(1, cols24[:, 8:16], 32, 24)

            dve.wait_ge(xre_in, 16)

            def residual(b):
                for h in range(2):
                    c = slice(512 * h, 512 * (h + 1))
                    dve.wait_ge(o_pe, 2 * b + h + 1)
                    own_done()
                    step(v.tensor_tensor(ores, bank[2 * (b % 2) + h][:, :], gt_m[:, c], ALU.mult))
                    last = v.tensor_tensor(x_tok[:, b, c], x_tok[:, b, c], ores, ALU.add)
                    if h == 0:
                        mark(last)
                last.then_inc(x1_dve, 1)
                dve.wait_ge(ss2_act, b + 1)
                v.tensor_scalar(st[:, 1, b:b + 1], st[:, 0, b:b + 1], 1.0 / D, EPS, ALU.mult, ALU.add).then_inc(rt2_dve, 1)
                dve.wait_ge(rt2_act, b + 1)
                step(v.reciprocal(st[:, 2, b:b + 1], st[:, 2, b:b + 1]))
                if b >= 2:
                    dve.wait_ge(xn_stored[b % 2], 16)
                    dve.wait_ge(x2T_pe, 2 * (b - 1))
                v.tensor_scalar(xn2[:, b % 2], x_tok[:, b], st[:, 2, b:b + 1], None, ALU.mult).then_inc(xn2_dve, 1)

            def router_logits(b):
                dve.wait_ge(x2T_pe, 2 * b + 2)
                if b >= 1:
                    dve.wait_ge(lg_pe, b)
                for k in range(4, KD):
                    last = v.tensor_scalar(h2T[:, k], bank[5][:, P * (k - 4):P * (k - 3)], scm[:, 2, k:k + 1],
                                           scm[:, 3, k:k + 1], ALU.mult, ALU.add)
                    if k < KD - 1:
                        mark(last)
                last.then_inc(x2T_dve, 1)
                dve.wait_ge(lg_pe, b + 1)
                if b == 0:
                    dve.wait_ge(router_in, 32)
                v.tensor_tensor(logits[:, b], bank[6][:, 0:NROUTE], route_bias[:, :], ALU.add).then_inc(lg_dve, 1)

            residual(0)
            for b in range(1, NB):
                residual(b)
                router_logits(b - 1)
            router_logits(NB - 1)

            dve.wait_ge(lg_dve, NB)
            prio = C("prio")

            def b3(a, n):
                return a.unsqueeze(2).broadcast_to([*a.shape, n])

            def first_greatest(vals, n, top, hot, work):
                step(v.tensor_reduce(top, vals, AX, ALU.max))
                step(v.tensor_tensor(hot, vals, b3(top, n), ALU.is_equal))
                step(v.tensor_tensor(hot, hot, prio[:, 0:n].unsqueeze(1).broadcast_to([P, NB, n]), ALU.mult))
                step(v.tensor_reduce(work, hot, AX, ALU.max))
                step(v.tensor_tensor(hot, hot, b3(work, n), ALU.is_equal))

            first_greatest(logits[:, :, 0:G], G, r_top[:, 0], r_hotg, r_top[:, 3])
            mark(v.tensor_tensor(rexp[:, 0:16].rearrange("p (b g) -> p b g", b=NB), logits[:, :, 0:G],
                                 b3(r_top[:, 0], G), ALU.subtract))
            step(v.tensor_scalar(r_hotg, r_hotg, -NEG, NEG, ALU.mult, ALU.add))
            step(v.tensor_tensor(r_le.rearrange("p b (g e) -> p b g e", g=G),
                                 logits[:, :, G:].rearrange("p b (g e) -> p b g e", g=G),
                                 r_hotg.unsqueeze(3).broadcast_to([P, NB, G, EPG]), ALU.add))
            first_greatest(r_le, NE, r_top[:, 1], r_hot[:, 0], r_top[:, 3])
            step(v.scalar_tensor_tensor(r_le, r_hot[:, 0], 3 * NEG, r_le, ALU.mult, ALU.add))
            first_greatest(r_le, NE, r_top[:, 2], r_hot[:, 1], r_top[:, 3])
            v.tensor_tensor(rexp[:, 16:20], r_top[:, 2], r_top[:, 1], ALU.subtract).then_inc(rexp_dve, 1)
            picks3 = picks.rearrange("p (b e) -> p b e", b=NB)
            before3 = before.rearrange("p (b e) -> p b e", b=NB)
            mark(v.memset(before3[:, 0], 0.0))
            step(v.tensor_tensor(picks3, r_hot[:, 0], r_hot[:, 1], ALU.add))
            for b in range(1, NB):
                step(v.tensor_tensor(before3[:, b], before3[:, b - 1], picks3[:, b - 1], ALU.add))
            v.tensor_tensor(per_part, before3[:, NB - 1], picks3[:, NB - 1], ALU.add).then_inc(m_dve, 1)

            dve.wait_ge(rexp_act, 1)
            mark(v.tensor_copy(picked[:, :, 0], C("ids")))
            cw = [picked[:, NB * n:NB * (n + 1), 1] for n in range(2)]
            step(v.tensor_reduce(r_top[:, 3], rexp[:, 0:16].rearrange("p (b g) -> p b g", b=NB), AX, ALU.add))
            mark(v.reciprocal(r_top[:, 3], r_top[:, 3]))
            step(v.tensor_scalar(r_top[:, 6], rexp[:, 16:20], 1.0, None, ALU.add))
            step(v.reciprocal(r_top[:, 6], r_top[:, 6]))
            v.tensor_tensor(cw[0], r_top[:, 6], r_top[:, 3], ALU.mult).then_inc(cw_dve, 1)
            dve.wait_ge(cw_dve, 1)
            v.tensor_tensor(cw[1], cw[0], rexp[:, 16:20], ALU.mult).then_inc(cw_dve, 1)

            dve.wait_ge(rank_pe, 1)
            mark(v.tensor_copy(r_loc, bank[0][:, 0:P]))
            step(v.tensor_copy(r_cnt, bank[1][:, 0:NE]))
            step(v.tensor_scalar(r_ov[:, 0], r_cnt, float(SLOTS), None, ALU.is_gt))
            for k in range(2, S // SLOTS):
                step(v.scalar_tensor_tensor(r_ov[:, 0], r_cnt, float(SLOTS * k), r_ov[:, 0], ALU.is_gt, ALU.add))
            step(v.tensor_copy(r_ov[:, 1], r_ov[:, 0]))
            a, b_ = 1, 2
            for d in (1, 2, 4, 8, 16):
                mark(v.tensor_copy(r_ov[:, b_, 0:d], r_ov[:, a, 0:d]))
                step(v.tensor_tensor(r_ov[:, b_, d:], r_ov[:, a, d:], r_ov[:, a, 0:NE - d], ALU.add))
                a, b_ = b_, a
            upto = r_ov[:, a]
            step(v.tensor_tensor(r_ov[:, b_], upto, r_ov[:, 0], ALU.subtract))
            step(v.tensor_scalar(r_ov[:, b_], r_ov[:, b_], float(SLOTS), float(SLOTS * (NE - 1)), ALU.mult, ALU.add))
            step(v.tensor_tensor(r_ov[:, b_], r_ov[:, b_], C("e64"), ALU.subtract))
            r_loc3 = r_loc.rearrange("p (b e) -> p b e", b=NB)
            step(v.tensor_scalar(r_le, r_loc3, float(SLOTS), None, ALU.is_ge))
            step(v.tensor_tensor(r_le, r_le, r_ov[:, b_].unsqueeze(1).broadcast_to([P, NB, NE]), ALU.mult))
            step(v.tensor_tensor(r_loc3, r_loc3, r_le, ALU.add))
            step(v.tensor_tensor(r_loc3, r_loc3, C("e64").unsqueeze(1).broadcast_to([P, NB, NE]), ALU.add))
            for n in range(2):
                step(v.tensor_tensor(r_le, r_loc3, r_hot[:, n], ALU.mult))
                step(v.tensor_reduce(r_top[:, 4 + n], r_le, AX, ALU.add))
            step(v.tensor_copy(loc_i[:, 0].rearrange("p (n b) -> p n b", n=2), r_top[:, 4:6]))
            mark(v.tensor_scalar(loc_i[:, 1], loc_i[:, 0], SLOTS - 1, None, ALU.bitwise_and))
            step(v.tensor_scalar(loc_i[:, 2], loc_i[:, 0], SLOTS.bit_length() - 1, None, ALU.arith_shift_right))
            step(v.tensor_copy(loc_f[:, :, :], loc_i[:, 1:3]))
            dve.wait_ge(xn_stored[1], 16 * NB // 2)
            count = C("count").unsqueeze(1)
            mark(v.tensor_tensor(in_tile, count[:, :, 0:2 * ALLPAIRS].broadcast_to([P, 2 * NB, 2 * ALLPAIRS]),
                                 b3(loc_f[:, 1], 2 * ALLPAIRS), ALU.is_equal))
            mark(v.tensor_tensor(in_slot, count.broadcast_to([P, 2 * NB, SLOTS]), b3(loc_f[:, 0], SLOTS), ALU.is_equal))
            dve.wait_ge(cw_dve, 2)
            own_done()
            for o in range(2):
                v.tensor_tensor(tile_vals[:, :, o], in_tile, b3(picked[:, :, o], 2 * ALLPAIRS), ALU.mult
                                ).then_inc(locs_dve, 1)
            step(v.tensor_tensor(r_cmp, upto.unsqueeze(1).broadcast_to([P, MAXOVER, NE]),
                                 C("over").unsqueeze(2).broadcast_to([P, MAXOVER, NE]), ALU.is_le))
            step(v.tensor_reduce(r_exp, r_cmp, AX, ALU.add))
            step(v.tensor_scalar(r_exp, r_exp, float(NE - 1), None, ALU.min))
            step(v.tensor_copy(oexp_i[:, :], r_exp))
            v.tensor_copy(nover_i[:, :], upto[:, NE - 1:NE]).then_inc(over_dve, 1)
            dve.wait_ge(table_pe, 1)
            tab = bank[2][:, 0:4 * ALLPAIRS].rearrange("p (o t) -> p o t", o=2)
            for s in range(2):
                c = slice(SLOTS * s, SLOTS * (s + 1))
                by_pair = tab[c, 0].rearrange("p (i s) -> p s i", s=2)[:, s]
                v.tensor_scalar(slots_in[c], by_pair, float(S), None, ALU.add).then_inc(slots_dve, 1)
            mark(v.tensor_copy(ids_out[:, :], tab[:, 0]))
            mark(v.tensor_copy(weights_out[:, :], tab[:, 1]))
            own_done()
            mark(v.tensor_scalar(row_f[:, 0], ids_out[:, :], 2.0, C("row0"), ALU.mult, ALU.add))
            step(v.tensor_scalar(row_f[:, 1], ids_out[:, :], 0.0, C("spare"), ALU.is_equal, ALU.mult))
            step(v.tensor_tensor(row_f[:, 0], row_f[:, 0], row_f[:, 1], ALU.add))
            v.tensor_copy(row_i[:, :], row_f[:, 0]).then_inc(row_dve, 1)

            def experts(i, first):
                dve.wait_ge(xgT_pe, i + 1)
                for k in range(4, KD):
                    last = v.tensor_scalar(xT[:, k], bank[1][:, P * (k - 4):P * (k - 3)], scm[:, 2, k:k + 1],
                                           scm[:, 3, k:k + 1], ALU.mult, ALU.add)
                last.then_inc(xgT_dve, 1)
                for s in range(2):
                    dve.wait_ge(silu_act, i * 2 + s + 1)
                    dve.wait_ge(wu_used, i * 2 + s + 1)
                    v.tensor_tensor(hid, bank[3][:, 0:256], act_g, ALU.mult).then_inc(hid_dve, 1)
                    dve.wait_ge(wd_used, i * 2 + s + 1)
                    if not first:
                        dve.wait_ge(y_added[s], i * 16)
                    v.scalar_tensor_tensor(ysb[:, s], bank[5 + s][:, :], weights_out[:, bass.ds(i * 2 + s, 1)] if not first else
                                           weights_out[:, s:s + 1], gt_f,
                                           ALU.mult, ALU.mult).then_inc(ydn_dve, 1)

            experts(0, True)
            with dve.Fori(1, PAIRS) as i:
                experts(i, False)
            n_over = dve.value_load(nover_i[0:1, 0:1], min_val=0, max_val=MAXOVER)
            with dve.If(n_over > 0):
                with dve.Fori(PAIRS, ALLPAIRS) as i:
                    experts(i, False)


_INS = ("x", "c", "w_ada", "b_ada", "g_norm_mix", "w_in", "sinks_a", "w_branch", "w_out", "g_norm_ffn",
        "w_expert_gate", "w_expert_up", "w_expert_down")


def kernel(**inputs):
    import concourse.bacc as bacc
    from concourse.bass_utils import run_bass_kernel_spmd

    nc = bacc.Bacc("TRN2", target_bir_lowering=False, num_devices=1)
    arrays = {name: np.ascontiguousarray(inputs[name]) for name in _INS}
    arrays["positions"] = np.ascontiguousarray(np.reshape(inputs["positions"], (NB, P)).T)
    head = np.concatenate([inputs[n] for n in ("q_norm_a", "k_norm_a", "q_norm_b", "k_norm_b")])
    swapped = np.concatenate([head[:, HD // 2:], head[:, :HD // 2]], axis=1)
    arrays["head_gains"] = np.concatenate([head, swapped]).reshape(1, 8 * HD)
    arrays["route_bias"] = np.concatenate([inputs["b_group"], np.reshape(inputs["b_router"], (1, NE))], axis=1)
    by_model = np.transpose(inputs["w_router"][0], (1, 0, 2)).reshape(D, NE)
    arrays["w_route"] = np.concatenate([inputs["w_group"][0], by_model], axis=1)
    arrays["consts"] = shape_constants()
    arrays["zero_rows"] = np.zeros((P, HALF), np.float32)
    access = {name: nc.dram_tensor(f"in_{name}", a.shape, mybir.dt.from_np(a.dtype), kind="ExternalInput").ap()
              for name, a in arrays.items()}
    access["out"] = nc.dram_tensor("out_y", (ROWS, HALF), F32, kind="ExternalOutput").ap()
    build_block(nc, access)
    r = run_bass_kernel_spmd(nc, [{f"in_{name}": a for name, a in arrays.items()}], core_ids=[0])
    return r.results[0]["out_y"][:2 * S].reshape(1, S, D)
```

```python
from contextlib import ExitStack

import concourse.bass as bass
from concourse import mybir
import numpy as np

F32 = mybir.dt.float32
I32 = mybir.dt.int32
U32 = mybir.dt.uint32
ALU = mybir.AluOpType
ACT = mybir.ActivationFunctionType
AX = mybir.AxisListType.X

P = 128
D = 1024
S = 512
CHUNK = 64
HD = 64
KD = D // P
NB = S // P
HEADS = 8
KVH = 2
IDXH = 4
TOPK = min(256, S // 4)
G = 4
EPG = 8
NE = G * EPG
FE = 512
NROUTE = G + NE
EPS = 1e-6
NEG = -1e30
TAKEN = -3e38
SLOTS = 64
PAIRS = NE // 2
MAXOVER = (2 * S) // SLOTS
OPAIRS = MAXOVER // 2
ALLPAIRS = PAIRS + OPAIRS
HALF = D // 2
GATE0 = 1860
WCH = 4096
TWO_PI_HI = 6.28125
TWO_PI_MID = float(np.float32(2 * np.pi - 6.28125))
TWO_PI_LO = float(2 * np.pi - 6.28125 - TWO_PI_MID)
ROUNDER = 12582912.0
PI_IN = 3.1415925

CONST = {}
_at = 0
for _name, _w in (("ident", P), ("tri", P), ("ones", P), ("win", 2 * P), ("freq", 32),
                  ("prio", NE), ("over", MAXOVER), ("count", SLOTS),
                  ("ids", 2 * NB), ("row0", 1)):
    CONST[_name] = (_at, _at + _w)
    _at += _w
CONST_W = _at


def shape_constants():
    c = np.zeros((P, CONST_W), np.float32)

    def put(name, a):
        lo, hi = CONST[name]
        c[:, lo:hi] = a

    i = np.arange(P)
    put("ident", np.eye(P))
    put("tri", (i[:, None] < i[None, :]))
    put("ones", 1.0)
    win = np.full((P, 2 * P), NEG)
    win[:CHUNK, CHUNK:3 * CHUNK] = 0.0
    win[CHUNK:, 2 * CHUNK:] = 0.0
    put("win", win)
    half = HD // 2
    put("freq", 10000.0 ** (-np.arange(half) / half))
    put("prio", NE - np.arange(NE))
    put("over", np.arange(MAXOVER))
    put("count", np.arange(SLOTS))
    put("ids", np.tile(i[:, None] + P * np.arange(NB)[None, :] - S, 2))
    put("row0", (2 * S + (i >= SLOTS))[:, None])
    return c


def build_block(nc, A):
    with ExitStack() as ctx:
        def sb(name, shape, dt=F32):
            return ctx.enter_context(nc.sbuf_tensor(name, shape, dt))

        def sem(name):
            return ctx.enter_context(nc.semaphore(name))

        bank = [ctx.enter_context(nc.psum_tensor(f"bank{i}", [P, 512], F32)) for i in range(8)]

        ring = sb("ring", [P, 5 * WCH])
        qk = sb("qk", [P, 2 * WCH])
        scr = sb("scr", [P, 2 * WCH])
        r1 = sb("r1", [P, WCH])
        hT_ = sb("hT", [P, WCH])
        vt = sb("vt", [P, NB, 2, KVH * HD])
        idx = sb("idx", [P, 3, S])
        bias_ada = sb("bias_ada", [P, 3, 512])
        mod = sb("mod", [P, 512])
        con = sb("con", [P, CONST_W])
        rope_cs = sb("rope_cs", [P, NB, 2, HD])
        gains = sb("gains", [P, 2, 4, HD])
        wr = sb("wr", [P, KD, NROUTE])
        route_bias = sb("route_bias", [P, NROUTE])
        rows24 = sb("rows24", [24, P])
        cols24 = sb("cols24", [P, 24])
        modT = sb("modT", [P, 48])
        scm = sb("scm", [P, 4, KD])
        cb = sb("cb", [P, KD, 32])
        pos_i = sb("pos_i", [P, NB], I32)
        pos_f = sb("pos_f", [P, NB])
        sinks = sb("sinks", [P, 2, HEADS])
        picked = sb("picked", [P, 2 * NB, 2])
        st = sb("st", [P, 3, NB])
        hst = sb("hst", [P, 3, 20])
        iw = sb("iw", [P, NB, IDXH])
        top8 = sb("top8", [P, 8])
        nmax = sb("nmax", [P, 2, HEADS])
        rsum = sb("rsum", [P, 2, HEADS])
        sinkt = sb("sinkt", [P, 2, HEADS])
        slots_in = sb("slots_in", [P, ALLPAIRS], I32)
        weights_out = sb("weights_out", [P, 2 * ALLPAIRS])
        row_f = sb("row_f", [P, 2 * ALLPAIRS])
        row_i = sb("row_i", [P, 2 * ALLPAIRS], I32)
        loc_i = sb("loc_i", [P, 3, 2 * NB], I32)
        loc_f = sb("loc_f", [P, 2, 2 * NB])
        nover_i = sb("nover_i", [P, 1], I32)
        oexp_i = sb("oexp_i", [P, MAXOVER], I32)
        logits = sb("logits", [P, NB, NROUTE])
        rexp = sb("rexp", [P, 5 * NB])

        def C(name):
            lo, hi = CONST[name]
            return con[:, lo:hi]

        ident, tri, ones = C("ident"), C("tri"), C("ones")
        win = C("win")

        def slot(i):
            if i < 5:
                return ring[:, WCH * i:WCH * (i + 1)]
            return (qk[:, 0:WCH], qk[:, WCH:2 * WCH], hT_[:, :], r1[:, :])[i - 5]

        QK_LOW, QK_HIGH, HT, R1 = 5, 6, 7, 8
        GATE_SLOTS = (4, 0)

        hT = hT_[:, :].rearrange("p (k t) -> p k t", k=KD)
        x_tok = r1[:, :].rearrange("p (b d) -> p b d", b=NB)
        yT = r1[:, :].rearrange("p (n j t) -> p n j t", n=2, j=4)
        qT = qk[:, 0:WCH].rearrange("p (n j t) -> p n j t", n=2, j=4)
        kz = qk[:, WCH:WCH + 2048].rearrange("p (n z t) -> p n z t", n=2, z=2)
        iqT = qk[:, WCH + 2048:WCH + 3072].rearrange("p (c t) -> p c t", c=2)
        ikz = qk[:, WCH + 3072:WCH + 4096].rearrange("p (z t) -> p z t", z=2)
        gt_m = bias_ada[:, 0:2].rearrange("p h n -> p (h n)")
        gt_f = bias_ada[:, 2]
        raw = [scr[:, 1280 * i:1280 * (i + 1)] for i in range(2)]
        ta, tb, rt = (scr[:, 2560 + 1280 * i:3840 + 1280 * i] for i in range(3))
        sq = scr[:, 6400:7680]
        gtab = scr[:, 7680:8192].rearrange("p (u k d) -> p u k d", u=2, k=4)
        sq_junk = scr[:, 0:4096].rearrange("p (b d) -> p b d", b=NB)
        args = scr[:, 4096:4608]
        atmp = scr[:, 4608:5120].rearrange("p (u n) -> p u n", u=4)
        rawd = r1[:, 0:1296].rearrange("p (b c) -> p b c", b=NB)
        rtd = r1[:, 1296:1296 + 768].rearrange("p (u c) -> p u c", u=2)
        tad = r1[:, 2064:2384]
        tbd = r1[:, 2384:2704]
        relu = r1[:, 3072:4096].rearrange("p (u s) -> p u s", u=2)
        prob = {0: scr[:, 0:2048], 1: scr[:, 2048:6144]}
        pt = [scr[:, 6144 + 1024 * i:7168 + 1024 * i] for i in range(2)]
        merged = scr[:, 0:WCH].rearrange("p (k t) -> p k t", k=KD)
        gates = [slot(i).rearrange("p (n d t) -> p n d t", n=2, d=4) for i in GATE_SLOTS]
        mtmp = scr[:, 6144:7168].rearrange("p (n t) -> p n t", n=2)
        ores = scr[:, 7168:7680]
        xn2 = scr[:, 4096:6144].rearrange("p (u d) -> p u d", u=2)
        h2T = scr[:, 6144:7168].rearrange("p (k t) -> p k t", k=KD)
        xg = [scr[:, 2048 + 1024 * u:3072 + 1024 * u] for u in range(3)]
        xT = scr[:, 5120:6144].rearrange("p (k t) -> p k t", k=KD)
        act_g = scr[:, 6144:6400]
        hid = scr[:, 6400:6656]
        hidT = scr[:, 6656:6912].rearrange("p (c h s) -> p c h s", c=2, h=2)
        ysb = scr[:, 7168:8192].rearrange("p (u d) -> p u d", u=2)
        def rw(at, n):
            return scr[:, at:at + n]

        vt_flat = vt[:, :, :, :].rearrange("p b n d -> p (b n d)")

        r_top = rw(0, 8 * NB).rearrange("p (u b) -> p u b", u=8)
        r_hotg = rw(32, 16).rearrange("p (b g) -> p b g", b=NB)
        r_le = rw(64, P).rearrange("p (b e) -> p b e", b=NB)
        r_hot = rw(192, 2 * P).rearrange("p (u b e) -> p u b e", u=2, b=NB)
        picks, before, per_part, r_cnt, r_loc = rw(448, P), rw(576, P), rw(704, NE), rw(736, NE), rw(768, P)
        r_ov = rw(896, 3 * NE).rearrange("p (u e) -> p u e", u=3)
        r_exp = rw(992, MAXOVER)
        r_cmp = rw(1024, MAXOVER * NE).rearrange("p (j e) -> p j e", j=MAXOVER)

        r_rank = rw(1024, 2 * P).rearrange("p (n b e) -> p n b e", n=2, b=NB)
        in_slot = rw(5120, 2 * NB * SLOTS).rearrange("p (u q) -> p u q", u=2 * NB)
        tile_vals = rw(6144, 4 * NB * NE).rearrange("p (u o t) -> p u o t", u=2 * NB, o=2)
        over_tile = rw(1024, 2 * NB * MAXOVER).rearrange("p (u t) -> p u t", u=2 * NB)
        over_vals = rw(1152, 4 * NB * MAXOVER).rearrange("p (u o t) -> p u o t", u=2 * NB, o=2)
        over_slot = rw(1536, 2 * NB * SLOTS).rearrange("p (u q) -> p u q", u=2 * NB)

        xn_dram = nc.dram_tensor("xn_rows", [S, D], F32, kind="Internal").ap()
        out_tokens = A["out"].rearrange("(t g) n -> t (g n)", g=2)

        w_ada = A["w_ada"][0].rearrange("(k p) n -> p k n", p=P)
        w_in = A["w_in"][0].rearrange("(k p) n -> p k n", p=P)
        w_out = A["w_out"][0].rearrange("(k p) n -> p k n", p=P)

        def wide(i, w=512):
            return slot(chunk_slot[i])[:, 0:KD * w].rearrange("p (k n) -> p k n", k=KD)

        def deep(i):
            return slot(chunk_slot[i]).rearrange("p (k n) -> p k n", k=2)

        def ada(i, m, q):
            return [(deep(i), w_ada[:, 2 * q:2 * q + 2, 2048 * m:2048 * (m + 1)])]

        def inproj(i, c0, w=512):
            return [(wide(i, w), w_in[:, :, c0:c0 + w])]

        def branch(i, n):
            dst = slot(chunk_slot[i]).rearrange("p (j n) -> p j n", j=4)
            src = A["w_branch"][0, n].rearrange("(g j p) n -> g p j n", g=2, j=4)
            return [(dst[64 * g:64 * (g + 1)], src[g]) for g in range(2)]

        cA, cC, cB = 5, 6, 7
        cG = {(0, 0): 8, (1, 0): 9, (0, 1): 10, (1, 1): 11}
        cM = {(0, q): q for q in range(4)} | {(1, q): 12 + q for q in range(4)}
        cM |= {(2, 0): 16, (2, 1): 19, (2, 2): 20, (2, 3): 22}
        cBr = {0: 17, 1: 18}
        cO = {1: 21, 0: 23}
        chunk_slot = [0, 1, 2, 3, 4, 0, 1, 2, 3, R1, 3, 1, 2, 2, 2, 2, 2, 3, 1, HT, QK_LOW, QK_HIGH, HT, 2]
        kv_dst = wide(cC).rearrange("p k (u n) -> p k u n", u=2)
        chunks = ({c: ada(c, m, q) for (m, q), c in cM.items()}
                  | {4: inproj(4, 1536, 324), cA: inproj(cA, 0),
                     cC: [(kv_dst[:, :, 0], w_in[:, :, 512:768]), (kv_dst[:, :, 1], w_in[:, :, 1280:1536])],
                     cB: inproj(cB, 768)}
                  | {c: inproj(c, GATE0 + D * n + 512 * h) for (n, h), c in cG.items()}
                  | {c: branch(c, n) for n, c in cBr.items()}
                  | {c: [(wide(c), w_out[:, :, 512 * h:512 * (h + 1)])] for h, c in cO.items()})
        chunks = [chunks[i] for i in range(len(chunks))]
        chunk_in = [sem(f"chunk_in{i}") for i in range(9)]
        const_in, x_in, rows_in, bias_in = sem("const_in"), sem("x_in"), sem("rows_in"), sem("bias_in")
        late_bias_in = sem("late_bias_in")
        pos_in, gains_in, router_in, xre_in = sem("pos_in"), sem("gains_in"), sem("router_in"), sem("xre_in")
        cols_pe, cols_dve = sem("cols_pe"), sem("cols_dve")
        ss_act, rstd_t, rstd_act, x_scaled = sem("ss_act"), sem("rstd_t"), sem("rstd_act"), sem("x_scaled")
        xt_pe, xt_act = sem("xt_pe"), sem("xt_act")
        ada_pe, ada_dve, adaT_pe, adaT_dve = sem("ada_pe"), sem("ada_dve"), sem("adaT_pe"), sem("adaT_dve")
        gt_pe, gt_dve = sem("gt_pe"), sem("gt_dve")
        ang_dve, ang_act = sem("ang_dve"), sem("ang_act")
        zeros_pool = sem("zeros_pool")
        d_pe, d_act, d_rope, dT_pe, dT_act = sem("d_pe"), sem("d_act"), sem("d_rope"), sem("dT_pe"), sem("dT_act")
        is_pe, is_act, is_dve = sem("is_pe"), sem("is_act"), sem("is_dve")
        pr_pe, pr_act, hss_dve, hrt_act, qk_rope = (sem("pr_pe"), sem("pr_act"), sem("hss_dve"), sem("hrt_act"),
                                                    sem("qk_rope"))
        qkT_pe, qkT_act = sem("qkT_pe"), sem("qkT_act")
        s_pe, s_dve, p_act = sem("s_pe"), sem("s_dve"), sem("p_act")
        sink_dve, sink_act, p_scaled = sem("sink_dve"), sem("sink_act"), [sem(f"p_scaled{z}") for z in range(2)]
        rs_dve = sem("rs_dve")
        pT_pe, pT_act, pT_dve, pv_pe, y_dve = sem("pT_pe"), sem("pT_act"), sem("pT_dve"), sem("pv_pe"), sem("y_dve")
        gate_pe, gate_act, up_pe, sig_act, merge_dve = (sem("gate_pe"), sem("gate_act"), sem("up_pe"),
                                                        sem("sig_act"), sem("merge_dve"))
        o_pe, x1_dve, ss2_act, rt2_dve, rt2_act, xn2_dve = (sem("o_pe"), sem("x1_dve"), sem("ss2_act"),
                                                            sem("rt2_dve"), sem("rt2_act"), sem("xn2_dve"))
        xn_stored = [sem(f"xn_stored{i}") for i in range(2)]
        x2T_pe, x2T_act, x2T_dve, lg_pe, lg_dve = (sem("x2T_pe"), sem("x2T_act"), sem("x2T_dve"),
                                                   sem("lg_pe"), sem("lg_dve"))
        rexp_dve, rexp_act, m_dve, rank_pe, locs_dve = (sem("rexp_dve"), sem("rexp_act"), sem("m_dve"),
                                                        sem("rank_pe"), sem("locs_dve"))
        over_dve, x1_half = sem("over_dve"), sem("x1_half")
        table_pe, slots_dve, olocs_dve = sem("table_pe"), sem("slots_dve"), sem("olocs_dve")
        x_got = [sem(f"x_got{i}") for i in range(3)]
        piece_in = [[sem(f"{n}_in{s}") for n in ("wg", "wu", "wd")] for s in range(3)]
        wg_used, wu_used, wd_used = sem("wg_used"), sem("wu_used"), sem("wd_used")
        xgT_pe, xgT_act, xgT_dve = sem("xgT_pe"), sem("xgT_act"), sem("xgT_dve")
        silu_act, hid_dve, hidT_pe, hidT_act, ydn_dve = (
            sem("silu_act"), sem("hid_dve"), sem("hidT_pe"), sem("hidT_act"), sem("ydn_dve"))
        y_added = [sem(f"y_added{s}") for s in range(2)]
        x1_stored, cw_dve, row_dve, xg_zero = sem("x1_stored"), sem("cw_dve"), sem("row_dve"), sem("xg_zero")
        dve_step = sem("dve_step")
        ang_part, h_act, h_dve, scm_dve, v_act = (sem("ang_part"), sem("h_act"), sem("h_dve"), sem("scm_dve"),
                                                  sem("v_act"))

        arrivals = {}
        loaded = [0] * 9
        for i, pieces in enumerate(chunks):
            loaded[chunk_slot[i]] += 16 * len(pieces)
            arrivals[i] = (chunk_in[chunk_slot[i]], loaded[chunk_slot[i]])

        through = {cM[m, q]: (ada_pe, 4 * m + q + 1) for m in range(3) for q in range(4)}
        through |= {4: (d_pe, NB), cA: (pr_pe, 3 * NB - 2), cC: (pr_pe, 3 * NB - 1), cB: (pr_pe, 3 * NB)}
        through |= {cG[n, h]: (gate_pe, 8 * h + 4 * n + 4) for n in range(2) for h in range(2)}
        through |= {cBr[n]: (up_pe, 2 * KD - 1 + n) for n in range(2)}
        through |= {cO[h]: (o_pe, 2 * NB - 1 + h) for h in range(2)}

        eslots = ((3, 0, 1), (4, HT, QK_LOW), (2, QK_HIGH, R1))
        left = {3: through[cBr[0]], 1: through[cBr[1]], 4: (merge_dve, KD // 2), 0: (merge_dve, KD),
                HT: through[cM[2, 3]], QK_LOW: through[cM[2, 2]], QK_HIGH: through[cO[1]], 2: through[cO[0]]}

        def expert_weights(s):
            g, u, d = (slot(x) for x in eslots[s])
            return (g.rearrange("p (k n) -> p k n", k=KD), u.rearrange("p (k n) -> p k n", k=KD),
                    d.rearrange("p (k n) -> p k n", k=4))

        eg_dram = A["w_expert_gate"][0].rearrange("g e (k p) n -> (g e) p k n", p=P)
        eu_dram = A["w_expert_up"][0].rearrange("g e (k p) n -> (g e) p k n", p=P)
        ed_dram = A["w_expert_down"][0].rearrange("g e (k p) n -> (g e) p k n", p=P)

        GROUPS = [(n, b) for b in range(NB) for n in range(2)]

        def key_tiles(n, b):
            return list(range(max(0, b - 1), b + 1)) if n == 0 else list(range(b + 1))

        TILES = [(g, i, t) for g, (n, b) in enumerate(GROUPS) for i, t in enumerate(key_tiles(n, b))]
        tiles_to = [sum(len(key_tiles(*GROUPS[x])) for x in range(g)) for g in range(len(GROUPS) + 1)]

        ADA_AT = {0: (1, 0), 1: (1, 1), 2: (1, 2), 3: (1, 3), 7: (2, 0), 8: (2, 1)}

        GATE_STEPS = {("project", 0): 3} | {("indexer", b): 1 for b in range(NB)}
        GATE_STEPS |= {("project", 1): 8, ("heads", 0): 3, ("project", 2): 6, ("heads", 1): 3, ("project", 3): 16,
                       ("heads", 2): 11, ("heads", 3): 2}
        EARLY = 7
        assert sum(GATE_STEPS.values()) == EARLY * KD
        GATE_STEPS |= {("scores", g): n for g, n in enumerate((8, 6, 8, 7, 7, 6, 6))}
        GATE_STEPS |= {("first scores", g): n for g, n in enumerate((2, 4, 2, 2, 2, 2), 1)}
        GATE_STEPS |= {("tile", k): 1 for k in range(10)}
        assert sum(GATE_STEPS.values()) == 2 * KD * KD
        GATE_BANKS = [bank[u % 2] if u < EARLY else bank[7] for u in range(2 * KD)]
        UP_BANKS = ((bank[0], bank[1]), (bank[2], bank[4]), (bank[5], bank[6]))

        def place(where):
            kind, n = where
            if kind in ("project", "indexer", "heads"):
                return {"project": (0, n, 0), "indexer": (0, 0, n + 1), "heads": (0, n + 1, 1)}[kind]
            if kind == "tile":
                return 1, 1 + sum(n >= t for t in tiles_to[1:]), 1 + n
            return 1, n, -1 if kind == "first scores" else 0

        gate_steps_to = {}
        _done = 0
        for _at, _n in sorted(GATE_STEPS.items(), key=lambda kv: place(kv[0])):
            gate_steps_to[_at] = (_done, _done + _n)
            _done += _n

        block = ctx.enter_context(nc.Block())

        @block.sync
        def _(sp):
            sp.dma_start(con[:, :], A["consts"]).then_inc(const_in, 16)
            sp.dma_start(x_tok, A["x"][0].rearrange("(b p) d -> p b d", p=P)).then_inc(x_in, 16)
            for i, pieces in enumerate(chunks):
                before = [j for j in range(i) if chunk_slot[j] == chunk_slot[i]]
                if before:
                    sp.wait_ge(*through[before[-1]])
                elif chunk_slot[i] == R1:
                    sp.wait_ge(is_dve, 3 * IDXH)
                elif chunk_slot[i] == HT:
                    sp.wait_ge(gate_pe, 2 * KD)
                elif chunk_slot[i] in (QK_LOW, QK_HIGH):
                    sp.wait_ge(s_pe, HEADS * len(GROUPS))
                for dst, src in pieces:
                    sp.dma_start(dst, src).then_inc(chunk_in[chunk_slot[i]], 16)

            sp.wait_ge(up_pe, 2 * KD)
            sp.dma_start(x_tok, A["x"][0].rearrange("(b p) d -> p b d", p=P)).then_inc(xre_in, 16)
            e_dram = (eg_dram, eu_dram, ed_dram)
            for t in range(3):
                for n, at in enumerate(eslots[t]):
                    if at == R1:
                        sp.wait_ge(x1_stored, 16 * NB)
                        sp.wait_ge(xn2_dve, NB)
                    else:
                        sp.wait_ge(*left[at])
                    sp.dma_start(expert_weights(t)[n], e_dram[n][t]).then_inc(piece_in[t][n], 16)

            def load_tile(j, s, e):
                before = (None, piece_in[s - 1][2], piece_in[s][0])
                for n, used in enumerate((wg_used, wu_used, wd_used)):
                    if n:
                        sp.wait_ge(before[n], j * 16 + (16 if n == 2 or s else 0))
                    sp.wait_ge(used, j * 3 + s - 2)
                    src = e_dram[n][bass.ds(e, 1)].rearrange("o p k n -> (o p) k n")
                    sp.dma_start(expert_weights(s)[n], src).then_inc(piece_in[s][n], 16)

            with sp.Fori(1, NE // 3) as j:
                for s in range(3):
                    load_tile(j, s, j * 3 + s)
            for s in range(NE % 3):
                load_tile(NE // 3, s, NE // 3 * 3 + s)
            sp.wait_ge(over_dve, 1)
            n_over = sp.value_load(nover_i[0:1, 0:1], min_val=0, max_val=MAXOVER)

            def overflow_expert(at):
                return sp.value_load(oexp_i[0:1, at], min_val=0, max_val=NE - 1)

            with sp.If(n_over > 0):
                load_tile(NE // 3, 2, overflow_expert(slice(0, 1)))
                with sp.Fori(NE // 3 + 1, (NE + MAXOVER) // 3) as j:
                    for s in range(3):
                        load_tile(j, s, overflow_expert(bass.ds(j * 3 + (s - NE), 1)))

        @block.gpsimd
        def _(pool):
            nc.gpsimd.memset(kz, 0.0).then_inc(zeros_pool, 1)
            nc.gpsimd.memset(ikz, 0.0).then_inc(zeros_pool, 1)
            pool.wait_ge(cw_dve, 2)
            for u in range(2):
                pool.wait_ge(xn_stored[u], 16 * NB // 2)
            for u in range(3):
                nc.gpsimd.memset(xg[u], 0.0).then_inc(xg_zero, 1)
            pool.wait_ge(slots_dve, 2)
            pool.wait_ge(xg_zero, 3)

            def fetch_tokens(i):
                if i >= 3:
                    pool.wait_ge(xgT_pe, i - 2)
                nc.gpsimd.indirect_dma_start(
                    out=xg[i % 3], out_offset=None, in_=xn_dram,
                    in_offset=bass.IndirectOffsetOnAxis(ap=slots_in[:, i:i + 1].bitcast(U32), axis=0),
                    bounds_check=S - 1, oob_is_err=False).then_inc(x_got[i % 3], 16)

            def add_rows(e):
                if e:
                    pool.wait_ge(y_added[(e - 1) % 2], 16 * ((e - 1) // 2 + 1))
                pool.wait_ge(ydn_dve, e + 1)
                nc.gpsimd.indirect_dma_start(
                    out=A["out"], out_offset=bass.IndirectOffsetOnAxis(
                        ap=row_i[:, e:e + 1].bitcast(U32), axis=0),
                    in_=ysb[:, e % 2], in_offset=None, bounds_check=2 * S - 1, oob_is_err=False,
                    compute_op=ALU.add).then_inc(y_added[e % 2], 16)

            fetch_tokens(0)
            fetch_tokens(1)
            pool.wait_ge(row_dve, 1)
            pool.wait_ge(x1_stored, 16 * NB)
            fetch_tokens(2)
            for i in range(PAIRS):
                if i + 3 < PAIRS:
                    fetch_tokens(i + 3)
                for s in range(2):
                    add_rows(2 * i + s)
            pool.wait_ge(over_dve, 1)
            n_over = pool.value_load(nover_i[0:1, 0:1], min_val=0, max_val=MAXOVER)
            with pool.If(n_over > 0):
                pool.wait_ge(slots_dve, 4)
                pool.wait_ge(row_dve, 2)
                for i in range(PAIRS, ALLPAIRS):
                    fetch_tokens(i)
                    for s in range(2):
                        add_rows(2 * i + s)
                for s in range(2):
                    pool.wait_ge(y_added[s], 16 * ALLPAIRS)
            with pool.Else():
                for s in range(2):
                    pool.wait_ge(y_added[s], 16 * PAIRS)

        @block.scalar
        def _(act):
            for k, name in enumerate(("g_norm_mix", "g_norm_ffn", "c")):
                act.dma_start(rows24[8 * k:8 * k + 8, :], A[name][0].rearrange("(k p) -> k p", p=P)
                              ).then_inc(rows_in, 16)
            ba = A["b_ada"].rearrange("o (m g n) -> o g m n", m=3, g=4)

            def load_bias(m, n):
                for g in range(4):
                    act.dma_start(bias_ada[32 * g:32 * (g + 1), m:m + n], ba[:, g, m:m + n].broadcast_to([32, n, 512])
                                  ).then_inc(bias_in if m == 0 else late_bias_in, 16)

            load_bias(0, 1)
            act.dma_start(pos_i[:, :], A["positions"]).then_inc(pos_in, 16)

            act.wait_ge(x_in, 16)
            for b in range(NB):
                nc.scalar.activation(sq_junk[:, b], x_tok[:, b], ACT.Square, accum_out=st[:, 0, b:b + 1]).then_inc(ss_act, 1)
            load_bias(1, 2)
            act.dma_start(sinks[:, 0, :], A["sinks_a"].broadcast_to([P, HEADS])).then_inc(gains_in, 16)
            act.dma_start(gains[:, :, :, :].rearrange("p u k d -> p (u k d)"),
                          A["head_gains"].broadcast_to([P, 8 * HD])).then_inc(gains_in, 16)
            act.dma_start(route_bias[:, :], A["route_bias"].broadcast_to([P, NROUTE])).then_inc(router_in, 16)
            act.dma_start(wr[:, :, :], A["w_route"].rearrange("(k p) n -> p k n", p=P)).then_inc(router_in, 16)
            act.wait_ge(rstd_t, 1)
            nc.scalar.activation(st[:, 2], st[:, 1], ACT.Sqrt).then_inc(rstd_act, 1)
            for n in range(2 * NB):
                b, h = n // 2, n % 2
                act.wait_ge(xt_pe, n + 1)
                nc.scalar.activation(hT[:, 4 * h:4 * h + 4, P * b:P * (b + 1)],
                                     bank[2 + n % 4][:, :].rearrange("p (k t) -> p k t", k=4),
                                     ACT.Copy).then_inc(xt_act, 1)
            act.wait_ge(scm_dve, 2)
            act.wait_ge(xt_act, 2 * NB)
            for k in range(1, KD, 2):
                nc.scalar.activation(hT[:, k], hT[:, k], ACT.Identity, scale=scm[:, 0, k:k + 1],
                                     bias=scm[:, 1, k:k + 1]).then_inc(h_act, 1)
            act.wait_ge(ang_dve, 1)
            nc.scalar.activation(rope_cs[:, :, :, :].rearrange("p b u d -> p (b u d)"), args,
                                 ACT.Sin).then_inc(ang_act, 1)

            for b in range(NB):
                act.wait_ge(d_pe, b + 1)
                nc.scalar.activation(rawd[:, b], bank[2 + b][:, 0:324], ACT.Copy).then_inc(d_act, 1)

            def evac_projection(b):
                if b >= 2:
                    act.wait_ge(qk_rope, b - 1)
                act.wait_ge(pr_pe, 3 * (b + 1))
                ba_, bc_, bb_ = (bank[2 + 3 * (b % 2) + i] for i in range(3))
                kv = bc_[:, :].rearrange("p (n u d) -> p n u d", n=2, u=2)
                nc.scalar.activation(raw[b % 2][:, 0:512], ba_[:, :], ACT.Copy)
                nc.scalar.activation(raw[b % 2][:, 640:1152], bb_[:, :], ACT.Copy)
                for n in range(2):
                    nc.scalar.activation(raw[b % 2][:, 512 + 640 * n:640 + 640 * n], kv[:, n, 0], ACT.Copy)
                nc.scalar.activation(vt[:, b], kv[:, :, 1], ACT.Copy).then_inc(v_act, 1)
                if b >= 1:
                    act.wait_ge(hss_dve, b)
                nc.scalar.activation(sq[:, 0:512], ba_[:, :], ACT.Square)
                nc.scalar.activation(sq[:, 640:1152], bb_[:, :], ACT.Square)
                for n in range(2):
                    last = nc.scalar.activation(sq[:, 512 + 640 * n:640 + 640 * n], kv[:, n, 0], ACT.Square)
                last.then_inc(pr_act, 1)

            def root_heads(b):
                act.wait_ge(hss_dve, b + 1)
                nc.scalar.activation(hst[:, 2], hst[:, 1], ACT.Sqrt).then_inc(hrt_act, 1)

            def evac_heads(b):
                act.wait_ge(qkT_pe, b + 1)
                base = 2 + 3 * (b % 2)
                t = slice(P * b, P * (b + 1))
                for n in range(2):
                    nc.scalar.activation(qT[:, n, :, t], bank[base + n][:, :].rearrange("p (j t) -> p j t", j=4),
                                         ACT.Copy)
                for n in range(2):
                    for z in range(2):
                        r = slice(64 * z, 64 * (z + 1))
                        last = nc.scalar.activation(kz[r, n, z, t], bank[base + 2][r, P * n:P * (n + 1)], ACT.Copy)
                last.then_inc(qkT_act, 1)

            def store_gates(where):
                lo, hi = gate_steps_to.get(where, (0, 0))
                for u in range(lo // KD, hi // KD):
                    act.wait_ge(gate_pe, u + 1)
                    nc.scalar.activation(gates[u // 8][:, u // 4 % 2, u % 4], GATE_BANKS[u][:, :], ACT.Copy
                                         ).then_inc(gate_act, 1)

            evac_projection(0)
            act.wait_ge(zeros_pool, 2)
            for b in range(NB):
                act.wait_ge(dT_pe, b + 1)
                t = slice(P * b, P * (b + 1))
                bk = bank[6 + b % 2]
                nc.scalar.activation(iqT[:, :, t], bk[:, 0:256].rearrange("p (c t) -> p c t", c=2), ACT.Copy)
                for z in range(2):
                    r = slice(64 * z, 64 * (z + 1))
                    last = nc.scalar.activation(ikz[r, z, t], bk[r, 256:384], ACT.Copy)
                last.then_inc(dT_act, 1)
                store_gates(("indexer", b))
            for n in range(3 * IDXH):
                b = 1 + n // IDXH
                act.wait_ge(is_pe, n + 1)
                if n >= 2:
                    act.wait_ge(is_dve, n - 1)
                nc.scalar.activation(relu[:, n % 2, 0:P * (b + 1)], bank[5 + n % 3][:, 0:P * (b + 1)],
                                     ACT.Relu).then_inc(is_act, 1)
            for b in range(1, NB):
                root_heads(b - 1)
                evac_projection(b)
                if b == NB - 1:
                    root_heads(b)
                store_gates(("project", b))
                evac_heads(b - 1)
                store_gates(("heads", b - 1))
            evac_heads(NB - 1)
            store_gates(("heads", NB - 1))

            def exps(g):
                n, b = GROUPS[g]
                w = P * len(key_tiles(n, b))
                for h in range(HEADS):
                    act.wait_ge(s_dve, HEADS * g + h + 1)
                    pr = prob[n][:, w * h:w * (h + 1)]
                    nc.scalar.activation(pr, pr, ACT.Exp, bias=nmax[:, g % 2, h:h + 1], scale=-1.0,
                                         accum_out=rsum[:, g % 2, h:h + 1]).then_inc(p_act, 1)
                if n == 0:
                    act.wait_ge(sink_dve, b + 1)
                    nc.scalar.activation(sinkt[:, 1], sinkt[:, 0], ACT.Exp).then_inc(sink_act, 1)

            def scale_probs(g):
                n, b = GROUPS[g]
                w = P * len(key_tiles(n, b))
                act.wait_ge(rs_dve, g + 1)
                act.wait_ge(p_act, HEADS * (g + 1))
                for h in range(HEADS // 2, HEADS):
                    pr = prob[n][:, w * h:w * (h + 1)]
                    last = nc.scalar.activation(pr, pr, ACT.Copy, scale=rsum[:, g % 2, h:h + 1])
                last.then_inc(p_scaled[1], 1)

            def evac_probs(g):
                for k in range(tiles_to[g], tiles_to[g + 1]):
                    act.wait_ge(pT_pe, 2 * k + 1)
                    if k >= 2:
                        act.wait_ge(pv_pe, k - 1)
                    nc.scalar.activation(pt[k % 2][:, 0:512], bank[4][:, :], ACT.Copy).then_inc(pT_act, 1)
                    store_gates(("tile", k))

            for g in range(len(GROUPS)):
                store_gates(("first scores", g))
                exps(g)
                store_gates(("scores", g))
                if g >= 1:
                    scale_probs(g - 1)
                    evac_probs(g - 1)
            scale_probs(len(GROUPS) - 1)
            evac_probs(len(GROUPS) - 1)

            act.wait_ge(gate_act, 2 * KD)
            for d in range(KD):
                raw_gates = gates[d // 4][:, :, d % 4]
                nc.scalar.activation(raw_gates, raw_gates, ACT.Sigmoid).then_inc(sig_act, 1)

            def norm2(b):
                act.wait_ge(x1_dve, b + 1)
                act.dma_start(out_tokens[P * b:P * (b + 1), :], x_tok[:, b]).then_inc(x1_stored, 16)
                nc.scalar.activation(vt_flat, x_tok[:, b], ACT.Square, accum_out=st[:, 0, b:b + 1]).then_inc(ss2_act, 1)
                act.wait_ge(rt2_dve, b + 1)
                nc.scalar.activation(st[:, 2, b:b + 1], st[:, 1, b:b + 1], ACT.Sqrt).then_inc(rt2_act, 1)
                act.wait_ge(xn2_dve, b + 1)
                act.dma_start(xn_dram[P * b:P * (b + 1), :], xn2[:, b % 2]).then_inc(xn_stored[b % 2], 16)

            def evac_h2(b):
                act.wait_ge(x2T_pe, 2 * b + 1)
                if b >= 1:
                    act.wait_ge(lg_pe, b)
                for k in range(4):
                    last = nc.scalar.activation(h2T[:, k], bank[4][:, P * k:P * (k + 1)], ACT.Identity,
                                                scale=scm[:, 2, k:k + 1], bias=scm[:, 3, k:k + 1])
                last.then_inc(x2T_act, 1)

            norm2(0)
            for b in range(1, NB):
                evac_h2(b - 1)
                norm2(b)
            evac_h2(NB - 1)
            act.wait_ge(rexp_dve, 1)
            nc.scalar.activation(rexp[:, :], rexp[:, :], ACT.Exp).then_inc(rexp_act, 1)

            def experts(i):
                act.wait_ge(xgT_pe, i + 1)
                for k in range(4):
                    last = nc.scalar.activation(xT[:, k], bank[0][:, P * k:P * (k + 1)], ACT.Identity,
                                                scale=scm[:, 2, k:k + 1], bias=scm[:, 3, k:k + 1])
                last.then_inc(xgT_act, 1)
                for s in range(2):
                    act.wait_ge(wg_used, i * 2 + s + 1)
                    nc.scalar.activation(act_g, bank[2][:, 0:256], ACT.Silu).then_inc(silu_act, 1)
                    act.wait_ge(hidT_pe, i * 2 + s + 1)
                    nc.scalar.activation(hidT, bank[4][:, 0:256].rearrange("p (c h s) -> p c h s", c=2, h=2),
                                         ACT.Copy).then_inc(hidT_act, 1)

            experts(0)
            with act.Fori(1, PAIRS) as i:
                experts(i)
            act.wait_ge(over_dve, 1)
            n_over = act.value_load(nover_i[0:1, 0:1], min_val=0, max_val=MAXOVER)
            with act.If(n_over > 0):
                with act.Fori(PAIRS, ALLPAIRS) as i:
                    experts(i)

        @block.tensor
        def _(pe):
            def arrived(i):
                pe.wait_ge(*arrivals[i])

            mm = nc.tensor.matmul

            def transpose(out, in_):
                return nc.tensor.transpose(out, in_, ident)

            pe.wait_ge(const_in, 16)
            pe.wait_ge(rows_in, 48)
            nc.tensor.transpose(bank[1][:, 0:24], rows24[:, :], ident[0:24, 0:24]).then_inc(cols_pe, 1)

            for n in range(2 * NB):
                b, h = n // 2, n % 2
                if h == 0:
                    pe.wait_ge(x_scaled, b + 1)
                if n >= 4:
                    pe.wait_ge(xt_act, n - 3)
                for k in range(4):
                    last = transpose(bank[2 + n % 4][:, P * k:P * (k + 1)], x_tok[:, b, P * (4 * h + k):P * (4 * h + k + 1)])
                last.then_inc(xt_pe, 1)

            def modulate(m, q, bk):
                c = cM[m, q]
                arrived(c)
                for k in range(2):
                    for g in range(4):
                        last = mm(bk[32 * g:32 * (g + 1), :], cb[:, 2 * q + k], deep(c)[:, k, 512 * g:512 * (g + 1)],
                                  start=q + k == 0, stop=q == 3 and k == 1)
                last.then_inc(ada_pe, 1)

            def modulation_columns(m, bk):
                pe.wait_ge(ada_dve, m + 1)
                for j in range(4):
                    last = transpose(bk[:, P * j:P * (j + 1)], mod[:, P * j:P * (j + 1)])
                last.then_inc(adaT_pe, 1)

            def mixer_gate_rows(h, bk):
                if h == 0:
                    pe.wait_ge(adaT_dve, 2)
                else:
                    pe.wait_ge(gt_dve, 1)
                mm(bk[:, :], ident[:, 32 * h:32 * h + 1].broadcast_to([P, P]), mod[:, :],
                   start=True, stop=True).then_inc(gt_pe, 1)

            def expert_gate_rows(bk):
                pe.wait_ge(adaT_dve, 3)
                for h in range(2):
                    last = mm(bk[64 * h:64 * (h + 1), :], ident[:, 64 + 32 * h:65 + 32 * h].broadcast_to([P, 64]),
                              mod[:, :], start=True, stop=True)
                last.then_inc(gt_pe, 1)

            pe.wait_ge(cols_dve, 1)
            for q in range(4):
                modulate(0, q, bank[0])
            modulation_columns(0, bank[0])

            pe.wait_ge(xt_act, 2 * NB)
            arrived(4)
            for b in range(NB):
                for k in range(KD):
                    if b == 0:
                        pe.wait_ge((h_dve, h_act)[k % 2], k // 2 + 1)
                    last = mm(bank[2 + b][:, 0:324], hT[:, k, P * b:P * (b + 1)], wide(4, 324)[:, k],
                              start=k == 0, stop=k == KD - 1)
                last.then_inc(d_pe, 1)

            def project(b):
                if b == 0:
                    pe.wait_ge(d_act, 3)
                elif b == 1:
                    pe.wait_ge(is_act, 3 * IDXH)
                else:
                    pe.wait_ge(qkT_act, b - 1)
                for n, c in enumerate((cA, cC, cB)):
                    if b == 0:
                        arrived(c)
                    bk = bank[2 + 3 * (b % 2) + n]
                    for k in range(KD):
                        last = mm(bk[:, :], hT[:, k, P * b:P * (b + 1)], wide(c)[:, k], start=k == 0, stop=k == KD - 1)
                    last.then_inc(pr_pe, 1)

            def transpose_heads(b):
                pe.wait_ge(qk_rope, b + 1)
                base = 2 + 3 * (b % 2)
                for n in range(2):
                    for j in range(4):
                        transpose(bank[base + n][:, P * j:P * (j + 1)], rt[:, 640 * n + P * j:640 * n + P * (j + 1)])
                for n in range(2):
                    last = transpose(bank[base + 2][:, P * n:P * (n + 1)], rt[:, 640 * n + 512:640 * n + 640])
                last.then_inc(qkT_pe, 1)

            def gate_products(where):
                for i in range(*gate_steps_to.get(where, (0, 0))):
                    u, k = i // KD, i % KD
                    half, n, d = u // 8, u // 4 % 2, u % 4
                    if k == 0:
                        if d == 0:
                            arrived(cG[n, half])
                        if u != EARLY and u >= 2:
                            pe.wait_ge(gate_act, u - 1 if u < EARLY else u)
                    last = mm(GATE_BANKS[u][:, :], wide(cG[n, half])[:, k, P * d:P * (d + 1)], hT[:, k],
                              start=k == 0, stop=k == KD - 1)
                    if k == KD - 1:
                        last.then_inc(gate_pe, 1)

            project(0)
            gate_products(("project", 0))
            for b in range(NB):
                pe.wait_ge(d_rope, b + 1)
                if b >= 2:
                    pe.wait_ge(dT_act, b - 1)
                for c in range(3):
                    last = transpose(bank[6 + b % 2][:, P * c:P * (c + 1)], rtd[:, b % 2, P * c:P * (c + 1)])
                last.then_inc(dT_pe, 1)
                gate_products(("indexer", b))
            pe.wait_ge(dT_act, NB)
            pe.wait_ge(d_act, NB)
            for n in range(3 * IDXH):
                b, h = 1 + n // IDXH, n % IDXH
                if n >= 3:
                    pe.wait_ge(is_act, n - 2)
                mm(bank[5 + n % 3][:, 0:P * (b + 1)], iqT[:, h // 2, P * b:P * (b + 1)], ikz[:, h % 2, 0:P * (b + 1)],
                   start=True, stop=True).then_inc(is_pe, 1)
            for b in range(1, NB):
                project(b)
                gate_products(("project", b))
                transpose_heads(b - 1)
                gate_products(("heads", b - 1))
            transpose_heads(NB - 1)
            gate_products(("heads", NB - 1))

            def scores(g):
                n, b = GROUPS[g]
                tiles = key_tiles(n, b)
                w = P * len(tiles)
                for h in range(HEADS):
                    u = HEADS * g + h
                    if h == 3:
                        gate_products(("first scores", g))
                    if u >= 3:
                        pe.wait_ge(s_dve, u - 2)
                    mm(bank[u % 3][:, 0:w], qT[:, n, h % 4, P * b:P * (b + 1)],
                       kz[:, n, h // 4, P * tiles[0]:P * tiles[0] + w], start=True, stop=True).then_inc(s_pe, 1)

            def weigh(g):
                n, b = GROUPS[g]
                tiles = key_tiles(n, b)
                w = P * len(tiles)
                if g:
                    pe.wait_ge(y_dve, g)
                for i, t in enumerate(tiles):
                    k = tiles_to[g] + i
                    for z in range(2):
                        if i == 0:
                            pe.wait_ge(p_scaled[z], g + 1)
                        if k:
                            pe.wait_ge((pT_act, pT_dve)[z], k)
                        for j in range(4):
                            h = 4 * z + j
                            last = transpose(bank[4 + z][:, P * j:P * (j + 1)], prob[n][:, w * h + P * i:w * h + P * (i + 1)])
                        last.then_inc(pT_pe, 1)
                    gate_products(("tile", k))
                    for z in range(2):
                        pe.wait_ge((pT_act, pT_dve)[z], k + 1)
                        last = mm(bank[6][64 * z:64 * (z + 1), :], vt[:, t, n, 64 * z:64 * (z + 1)],
                                  pt[k % 2][:, 512 * z:512 * (z + 1)], start=i == 0, stop=i == len(tiles) - 1)
                    last.then_inc(pv_pe, 1)

            pe.wait_ge(qkT_act, NB)
            pe.wait_ge(gate_act, EARLY)
            for g in range(len(GROUPS) + 1):
                if g == 4:
                    modulation_columns(1, bank[3])
                if g in (5, 6):
                    mixer_gate_rows(g - 5, bank[3])
                if g < len(GROUPS):
                    scores(g)
                    gate_products(("scores", g))
                if g in ADA_AT:
                    if ADA_AT[g] == (2, 0):
                        pe.wait_ge(gt_dve, 2)
                    modulate(*ADA_AT[g], bank[3])
                if g >= 1:
                    weigh(g - 1)

            pe.wait_ge(y_dve, len(GROUPS))
            for d in range(KD):
                if d >= 3:
                    pe.wait_ge(merge_dve, d - 2)
                for n in range(2):
                    c = cBr[n]
                    arrived(c)
                    w = slot(chunk_slot[c]).rearrange("p (j n) -> p j n", j=4)
                    for j in range(4):
                        last = mm(UP_BANKS[d % 3][n][:, :], w[:, j, P * d:P * (d + 1)], yT[:, n, j],
                                  start=j == 0, stop=j == 3)
                    last.then_inc(up_pe, 1)
                if d == 0:
                    modulate(2, 2, bank[3])
                elif d == 2:
                    modulate(2, 3, bank[3])
                elif d == 4:
                    modulation_columns(2, bank[3])
                elif d == 6:
                    expert_gate_rows(bank[3])

            def output_projection(b, h):
                if b == 0 and h == 0:
                    pe.wait_ge(merge_dve, KD)
                    pe.wait_ge(gt_dve, 3)
                if b >= 2:
                    pe.wait_ge(x1_dve, b - 1)
                arrived(cO[h])
                for k in range(KD):
                    last = mm(bank[2 * (b % 2) + h][:, :], merged[:, k, P * b:P * (b + 1)], wide(cO[h])[:, k],
                              start=k == 0, stop=k == KD - 1)
                last.then_inc(o_pe, 1)

            def transpose_normed(b):
                pe.wait_ge(xn2_dve, b + 1)
                for h in range(2):
                    if b >= 1:
                        pe.wait_ge((x2T_act, x2T_dve)[h], b)
                    for k in range(4):
                        last = transpose(bank[4 + h][:, P * k:P * (k + 1)], xn2[:, b % 2, P * (4 * h + k):P * (4 * h + k + 1)])
                    last.then_inc(x2T_pe, 1)

            def route(b):
                pe.wait_ge(x2T_act, b + 1)
                pe.wait_ge(x2T_dve, b + 1)
                if b == 0:
                    pe.wait_ge(router_in, 32)
                else:
                    pe.wait_ge(lg_dve, b)
                for k in range(KD):
                    last = mm(bank[6][:, 0:NROUTE], h2T[:, k], wr[:, k], start=k == 0, stop=k == KD - 1)
                last.then_inc(lg_pe, 1)

            output_projection(0, 0)
            output_projection(0, 1)
            for b in range(1, NB):
                output_projection(b, 0)
                transpose_normed(b - 1)
                output_projection(b, 1)
                route(b - 1)
            transpose_normed(NB - 1)
            route(NB - 1)

            pe.wait_ge(m_dve, 1)
            mm(bank[0][:, 0:P], tri, picks, start=True, stop=False)
            mm(bank[0][:, 0:P], ones, before, start=False, stop=True)
            mm(bank[1][:, 0:NE], ones, per_part, start=True, stop=True).then_inc(rank_pe, 1)

            def slot_table(bk, in_slot, vals):
                for u in range(2 * NB):
                    for g in range(2):
                        last = mm(bk[SLOTS * g:SLOTS * (g + 1), 0:2 * vals.shape[3]], in_slot[:, u],
                                  vals[:, u].rearrange("p o t -> p (o t)"), start=u == 0, stop=u == 2 * NB - 1)
                last.then_inc(table_pe, 1)

            pe.wait_ge(locs_dve, 3)
            slot_table(bank[2], in_slot, tile_vals)
            pe.wait_ge(row_dve, 1)

            def experts(j, u):
                i = j * 3 + u
                pe.wait_ge(x_got[u], j * 16 + 16)
                for k in range(KD):
                    last = transpose(bank[k // 4][:, P * (k % 4):P * (k % 4 + 1)], xg[u][:, P * k:P * (k + 1)])
                last.then_inc(xgT_pe, 1)
                pe.wait_ge(xgT_act, i + 1)
                pe.wait_ge(xgT_dve, i + 1)

                for s in range(2):
                    t = (2 * u + s) % 3
                    weights = expert_weights(t)

                    def weights_in(n):
                        pe.wait_ge(piece_in[t][n], j * 32 + 16 * ((2 * u + s) // 3 + 1))

                    for n, used in enumerate((wg_used, wu_used)):
                        w = weights[n]
                        weights_in(n)
                        for k in range(KD):
                            for h in range(2):
                                last = mm(bank[2 + n][64 * h:64 * (h + 1), 0:256], xT[:, k, SLOTS * s:SLOTS * (s + 1)],
                                          w[:, k, 256 * h:256 * (h + 1)], start=k == 0, stop=k == KD - 1)
                        last.then_inc(used, 1)
                    pe.wait_ge(hid_dve, i * 2 + s + 1)
                    for c in range(2):
                        last = transpose(bank[4][:, P * c:P * (c + 1)], hid[:, P * c:P * (c + 1)])
                    last.then_inc(hidT_pe, 1)
                    pe.wait_ge(hidT_act, i * 2 + s + 1)
                    weights_in(2)
                    for q in range(4):
                        for g in range(2):
                            last = mm(bank[5 + s][64 * g:64 * (g + 1), :], hidT[:, q % 2, q // 2],
                                      weights[2][:, q, 512 * g:512 * (g + 1)], start=q == 0, stop=q == 3)
                    last.then_inc(wd_used, 1)

            experts(0, 0)
            experts(0, 1)
            experts(0, 2)
            with pe.Fori(1, PAIRS // 3) as j:
                for u in range(3):
                    experts(j, u)
            experts(PAIRS // 3, 0)
            pe.wait_ge(over_dve, 1)
            n_over = pe.value_load(nover_i[0:1, 0:1], min_val=0, max_val=MAXOVER)
            with pe.If(n_over > 0):
                pe.wait_ge(olocs_dve, 3)
                slot_table(bank[7], over_slot, over_vals)
                experts(PAIRS // 3, 1)
                experts(PAIRS // 3, 2)
                with pe.Fori(PAIRS // 3 + 1, ALLPAIRS // 3) as j:
                    for u in range(3):
                        experts(j, u)

        @block.vector
        def _(dve):
            v = nc.vector
            own = [0]

            def mark(ins):
                own[0] += 1
                return ins.then_inc(dve_step, 1)

            def own_done():
                dve.wait_ge(dve_step, own[0])

            def step(ins):
                mark(ins)
                own_done()

            dve.wait_ge(cols_pe, 1)
            step(v.tensor_copy(cols24[:, :], bank[1][:, 0:24]))
            v.tensor_copy(cb[:, :, :], cols24[:, 16:24].unsqueeze(2).broadcast_to([P, KD, 32])).then_inc(cols_dve, 1)

            dve.wait_ge(ss_act, NB)
            v.tensor_scalar(st[:, 1], st[:, 0], 1.0 / D, EPS, ALU.mult, ALU.add).then_inc(rstd_t, 1)
            dve.wait_ge(rstd_act, 1)
            step(v.reciprocal(st[:, 2], st[:, 2]))
            for b in range(NB):
                v.tensor_scalar(x_tok[:, b], x_tok[:, b], st[:, 2, b:b + 1], None, ALU.mult).then_inc(x_scaled, 1)

            def modulation_rows(m, bk):
                dve.wait_ge(ada_pe, 4 * (m + 1))
                if m < 2:
                    dve.wait_ge((bias_in, late_bias_in)[m], 64)
                v.tensor_tensor(mod[:, :], bk[:, :], bias_ada[:, m], ALU.add).then_inc(ada_dve, 1)

            def modulation_columns(m, bk):
                dve.wait_ge(adaT_pe, m + 1)
                cols = bk[:, :].rearrange("p (j g r) -> p g j r", j=4, g=4)[:, :, :, 0]
                v.tensor_copy(modT[:, 16 * m:16 * (m + 1)].rearrange("p (g j) -> p g j", g=4), cols
                              ).then_inc(adaT_dve, 1)

            def gate_rows(n, out, bk):
                dve.wait_ge(gt_pe, n + 1)
                dve.wait_ge(ada_dve, 2 + n // 2)
                v.tensor_copy(out, bk[:, :]).then_inc(gt_dve, 1)

            def scale_shift(n, gain, sc, sh):
                v.scalar_tensor_tensor(scm[:, 2 * n], modT[:, sc:sc + KD], 1.0, gain, ALU.add, ALU.mult
                                       ).then_inc(scm_dve, 1)
                v.tensor_copy(scm[:, 2 * n + 1], modT[:, sh:sh + KD]).then_inc(scm_dve, 1)
                dve.wait_ge(scm_dve, 2 * n + 2)

            modulation_rows(0, bank[0])
            modulation_columns(0, bank[0])
            dve.wait_ge(adaT_dve, 1)
            scale_shift(0, cols24[:, 0:8], 8, 0)
            dve.wait_ge(xt_act, 2 * NB)
            for k in range(0, KD, 2):
                v.tensor_scalar(hT[:, k], hT[:, k], scm[:, 0, k:k + 1], scm[:, 1, k:k + 1], ALU.mult, ALU.add
                                ).then_inc(h_dve, 1)

            dve.wait_ge(pos_in, 16)
            dve.wait_ge(const_in, 16)
            step(v.tensor_copy(pos_f[:, :], pos_i[:, :]))
            ang, turns, red, tmp = (atmp[:, u] for u in range(4))
            for b in range(NB):
                mark(v.tensor_scalar(ang[:, 32 * b:32 * (b + 1)], C("freq"), pos_f[:, b:b + 1], None, ALU.mult))
            own_done()
            step(v.tensor_scalar(turns, ang, 1.0 / (2 * np.pi), None, ALU.mult))
            step(v.tensor_scalar(turns, turns, ROUNDER, None, ALU.add))
            step(v.tensor_scalar(turns, turns, ROUNDER, None, ALU.subtract))
            step(v.scalar_tensor_tensor(red, turns, -TWO_PI_HI, ang, ALU.mult, ALU.add))
            step(v.scalar_tensor_tensor(red, turns, -TWO_PI_MID, red, ALU.mult, ALU.add))
            step(v.scalar_tensor_tensor(red, turns, -TWO_PI_LO, red, ALU.mult, ALU.add))
            step(v.tensor_scalar(red, red, PI_IN, -PI_IN, ALU.min, ALU.max))
            step(v.tensor_scalar(tmp, red, np.pi / 2, None, ALU.is_gt))
            step(v.scalar_tensor_tensor(tmp, tmp, -2 * np.pi, red, ALU.mult, ALU.add))
            step(v.tensor_scalar(tmp, tmp, np.pi / 2, None, ALU.add))
            step(v.tensor_scalar(tmp, tmp, PI_IN, -PI_IN, ALU.min, ALU.max))
            a4 = args.rearrange("p (b u n) -> p b u n", b=NB, u=4)
            for u in range(2):
                v.tensor_copy(a4[:, :, u], tmp.rearrange("p (b n) -> p b n", b=NB)).then_inc(ang_part, 1)
            v.tensor_scalar(a4[:, :, 2], red.rearrange("p (b n) -> p b n", b=NB), -1.0, None,
                            ALU.mult).then_inc(ang_part, 1)
            v.tensor_copy(a4[:, :, 3], red.rearrange("p (b n) -> p b n", b=NB)).then_inc(ang_dve, 1)

            def rotate(src, heads, cos, sin, a, b):
                s3 = src.rearrange("p (h d) -> p h d", h=heads)
                a3 = a.rearrange("p (h d) -> p h d", h=heads)
                s4 = src.rearrange("p (h u d) -> p h u d", h=heads, u=2)
                b4 = b.rearrange("p (h u d) -> p h u d", h=heads, u=2)
                mark(v.tensor_tensor(a3, s3, cos.unsqueeze(1).broadcast_to([P, heads, HD]), ALU.mult))
                for u in range(2):
                    mark(v.tensor_tensor(b4[:, :, u], s4[:, :, 1 - u],
                                         sin[:, 32 * u:32 * (u + 1)].unsqueeze(1).broadcast_to([P, heads, 32]), ALU.mult))

            dve.wait_ge(ang_act, 1)
            for b in range(NB):
                dve.wait_ge(d_act, b + 1)
                if b:
                    dve.wait_ge(d_rope, b)
                mark(v.tensor_scalar(iw[:, b], rawd[:, b, 320:324], (IDXH * HD) ** -0.5, None, ALU.mult))
                rotate(rawd[:, b, 0:320], 5, rope_cs[:, b, 0], rope_cs[:, b, 1], tad, tbd)
                own_done()
                if b >= 2:
                    dve.wait_ge(dT_pe, b - 1)
                mark(v.tensor_tensor(rtd[:, b % 2, 0:320], tad, tbd, ALU.add))
                v.tensor_tensor(rtd[:, b % 2, 320:384], tad[:, 256:320], tbd[:, 256:320], ALU.add).then_inc(d_rope, 1)

            for n in range(3 * IDXH):
                b, h = 1 + n // IDXH, n % IDXH
                w = P * (b + 1)
                dve.wait_ge(is_act, n + 1)
                if h:
                    dve.wait_ge(is_dve, n)
                    ins = v.scalar_tensor_tensor(idx[:, b - 1, 0:w], relu[:, n % 2, 0:w], iw[:, b, h:h + 1],
                                                 idx[:, b - 1, 0:w], ALU.mult, ALU.add)
                else:
                    ins = v.tensor_scalar(idx[:, b - 1, 0:w], relu[:, n % 2, 0:w], iw[:, b, h:h + 1], None, ALU.mult)
                ins.then_inc(is_dve, 1)

            def top_k(b):
                w = P * (b + 1)
                m = idx[:, b - 1, 0:w]
                dve.wait_ge(is_dve, IDXH * b)
                step(v.tensor_tensor(idx[:, b - 1, P * b:w], idx[:, b - 1, P * b:w], win[:, P:2 * P], ALU.add))
                for _ in range(TOPK // 8):
                    step(v.max(top8[:, :], m))
                    step(v.match_replace(m, top8[:, :], m, TAKEN))
                step(v.tensor_scalar(m, m, TAKEN / 2, NEG, ALU.is_gt, ALU.mult))

            kinds = ((0, 8), (8, 2), (10, 8), (18, 2))

            def norm_and_rotate(b):
                dve.wait_ge(pr_act, b + 1)
                if b:
                    dve.wait_ge(qk_rope, b)
                step(v.tensor_reduce(hst[:, 0], sq.rearrange("p (h d) -> p h d", h=20), AX, ALU.add))
                v.tensor_scalar(hst[:, 1], hst[:, 0], 1.0 / HD, EPS, ALU.mult, ALU.add).then_inc(hss_dve, 1)
                if b == 0:
                    dve.wait_ge(gains_in, 32)
                for u in range(2):
                    mark(v.tensor_tensor(gtab[:, u], gains[:, u], rope_cs[:, b, u].unsqueeze(1).broadcast_to([P, 4, HD]),
                                         ALU.mult))
                dve.wait_ge(hrt_act, b + 1)
                step(v.reciprocal(hst[:, 0], hst[:, 2]))
                r3 = raw[b % 2].rearrange("p (h d) -> p h d", h=20)
                step(v.tensor_tensor(r3, r3, hst[:, 0].unsqueeze(2).broadcast_to([P, 20, HD]), ALU.mult))
                for k, (h0, hn) in enumerate(kinds):
                    c = slice(HD * h0, HD * (h0 + hn))
                    rotate(raw[b % 2][:, c], hn, gtab[:, 0, k], gtab[:, 1, k], ta[:, c], tb[:, c])
                own_done()
                if b >= 1:
                    dve.wait_ge(qkT_pe, b)
                for k, (h0, hn) in enumerate(kinds):
                    c = slice(HD * h0, HD * (h0 + hn))
                    if hn == HEADS:
                        i0, i1 = (t[:, c].rearrange("p (z j d) -> p z j d", z=2, j=4) for t in (ta, tb))
                        ins = v.tensor_tensor(rt[:, c].rearrange("p (j z d) -> p z j d", z=2, j=4), i0, i1, ALU.add)
                    else:
                        ins = v.tensor_tensor(rt[:, c], ta[:, c], tb[:, c], ALU.add)
                    if k < 3:
                        mark(ins)
                    else:
                        ins.then_inc(qk_rope, 1)

            for b in range(NB - 1):
                top_k(b + 1)
                norm_and_rotate(b)
            norm_and_rotate(NB - 1)

            step(v.tensor_scalar(sinks[:, 1], sinks[:, 0], -1.0, None, ALU.mult))

            def soften(g):
                n, b = GROUPS[g]
                w = P * len(key_tiles(n, b))
                if b == 0:
                    mask = win[:, P:2 * P]
                else:
                    mask = win if n == 0 else idx[:, b - 1, 0:w]
                if g == 0:
                    dve.wait_ge(qk_rope, NB)
                elif g >= 2:
                    dve.wait_ge(y_dve, g - 1)
                for h in range(HEADS):
                    u = HEADS * g + h
                    dve.wait_ge(s_pe, u + 1)
                    v.tensor_tensor_reduce(out=prob[n][:, w * h:w * (h + 1)], in0=bank[u % 3][:, 0:w], in1=mask,
                                           scale=-(HD ** -0.5), scalar=sinks[:, 1, h:h + 1] if n == 0 else 3e38,
                                           op0=ALU.add, op1=ALU.min, accum_out=nmax[:, g % 2, h:h + 1]
                                           ).then_inc(s_dve, 1)
                if n == 0:
                    dve.wait_ge(s_dve, HEADS * (g + 1))
                    v.tensor_tensor(sinkt[:, 0], nmax[:, g % 2], sinks[:, 0], ALU.add).then_inc(sink_dve, 1)

            def finish(g):
                n, b = GROUPS[g]
                tiles = key_tiles(n, b)
                w = P * len(tiles)
                dve.wait_ge(p_act, HEADS * (g + 1))
                rs = rsum[:, g % 2]
                if n == 0:
                    dve.wait_ge(sink_act, b + 1)
                    step(v.tensor_tensor(rs, rs, sinkt[:, 1], ALU.add))
                v.reciprocal(rs, rs).then_inc(rs_dve, 1)
                dve.wait_ge(rs_dve, g + 1)
                for h in range(HEADS // 2):
                    pr = prob[n][:, w * h:w * (h + 1)]
                    last = v.tensor_scalar(pr, pr, rs[:, h:h + 1], None, ALU.mult)
                last.then_inc(p_scaled[0], 1)
                for k in range(tiles_to[g], tiles_to[g + 1]):
                    dve.wait_ge(pT_pe, 2 * k + 2)
                    if k >= 2:
                        dve.wait_ge(pv_pe, k - 1)
                    v.tensor_copy(pt[k % 2][:, 512:1024], bank[5][:, :]).then_inc(pT_dve, 1)
                dve.wait_ge(pv_pe, tiles_to[g + 1])
                v.tensor_copy(yT[:, n, :, P * b:P * (b + 1)], bank[6][:, :].rearrange("p (j t) -> p j t", j=4)
                              ).then_inc(y_dve, 1)

            for g in range(len(GROUPS) + 1):
                if g < len(GROUPS):
                    soften(g)
                if g >= 1:
                    finish(g - 1)
                if g == 3:
                    modulation_rows(1, bank[3])
                elif g == 4:
                    modulation_columns(1, bank[3])
                elif g in (5, 6):
                    gate_rows(g - 5, gt_m[:, 512 * (g - 5):512 * (g - 4)], bank[3])

            for d in range(KD):
                dve.wait_ge(up_pe, 2 * (d + 1))
                dve.wait_ge(sig_act, d + 1)
                if d:
                    dve.wait_ge(merge_dve, d)
                for n in range(2):
                    mark(v.tensor_tensor(mtmp[:, n], UP_BANKS[d % 3][n][:, :], gates[d // 4][:, n, d % 4], ALU.mult))
                own_done()
                v.tensor_tensor(merged[:, d], mtmp[:, 0], mtmp[:, 1], ALU.add).then_inc(merge_dve, 1)
                if d == 2:
                    modulation_rows(2, bank[3])
                elif d == 4:
                    modulation_columns(2, bank[3])
                elif d == 6:
                    gate_rows(2, gt_f, bank[3])
            dve.wait_ge(adaT_dve, 3)
            scale_shift(1, cols24[:, 8:16], 32, 24)

            dve.wait_ge(xre_in, 16)

            def residual(b, h):
                c = slice(512 * h, 512 * (h + 1))
                dve.wait_ge(o_pe, 2 * b + h + 1)
                own_done()
                step(v.tensor_tensor(ores, bank[2 * (b % 2) + h][:, :], gt_m[:, c], ALU.mult))
                v.tensor_tensor(x_tok[:, b, c], x_tok[:, b, c], ores, ALU.add).then_inc(
                    x1_dve if h else x1_half, 1)

            def norm2(b):
                dve.wait_ge(ss2_act, b + 1)
                v.tensor_scalar(st[:, 1, b:b + 1], st[:, 0, b:b + 1], 1.0 / D, EPS, ALU.mult, ALU.add).then_inc(rt2_dve, 1)
                dve.wait_ge(rt2_act, b + 1)
                step(v.reciprocal(st[:, 2, b:b + 1], st[:, 2, b:b + 1]))
                if b >= 2:
                    dve.wait_ge(xn_stored[b % 2], 16)
                    dve.wait_ge(x2T_pe, 2 * (b - 1))
                v.tensor_scalar(xn2[:, b % 2], x_tok[:, b], st[:, 2, b:b + 1], None, ALU.mult).then_inc(xn2_dve, 1)

            def evac_h2(b):
                dve.wait_ge(x2T_pe, 2 * b + 2)
                if b >= 1:
                    dve.wait_ge(lg_pe, b)
                for k in range(4, KD):
                    last = v.tensor_scalar(h2T[:, k], bank[5][:, P * (k - 4):P * (k - 3)], scm[:, 2, k:k + 1],
                                           scm[:, 3, k:k + 1], ALU.mult, ALU.add)
                    if k < KD - 1:
                        mark(last)
                last.then_inc(x2T_dve, 1)

            def router_logits(b):
                dve.wait_ge(lg_pe, b + 1)
                if b == 0:
                    dve.wait_ge(router_in, 32)
                v.tensor_tensor(logits[:, b], bank[6][:, 0:NROUTE], route_bias[:, :], ALU.add).then_inc(lg_dve, 1)

            for b in range(NB):
                residual(b, 0)
                dve.wait_ge(x1_half, b + 1)
                if b:
                    evac_h2(b - 1)
                residual(b, 1)
                norm2(b)
                if b:
                    router_logits(b - 1)
            evac_h2(NB - 1)
            router_logits(NB - 1)

            dve.wait_ge(lg_dve, NB)
            prio = C("prio")

            def b3(a, n):
                return a.unsqueeze(2).broadcast_to([*a.shape, n])

            def first_greatest(vals, n, top, hot, work):
                step(v.tensor_reduce(top, vals, AX, ALU.max))
                step(v.tensor_tensor(hot, vals, b3(top, n), ALU.is_equal))
                step(v.tensor_tensor(hot, hot, prio[:, 0:n].unsqueeze(1).broadcast_to([P, NB, n]), ALU.mult))
                step(v.tensor_reduce(work, hot, AX, ALU.max))
                step(v.tensor_tensor(hot, hot, b3(work, n), ALU.is_equal))

            first_greatest(logits[:, :, 0:G], G, r_top[:, 0], r_hotg, r_top[:, 3])
            mark(v.tensor_tensor(rexp[:, 0:16].rearrange("p (b g) -> p b g", b=NB), logits[:, :, 0:G],
                                 b3(r_top[:, 0], G), ALU.subtract))
            step(v.tensor_scalar(r_hotg, r_hotg, -NEG, NEG, ALU.mult, ALU.add))
            step(v.tensor_tensor(r_le.rearrange("p b (g e) -> p b g e", g=G),
                                 logits[:, :, G:].rearrange("p b (g e) -> p b g e", g=G),
                                 r_hotg.unsqueeze(3).broadcast_to([P, NB, G, EPG]), ALU.add))
            first_greatest(r_le, NE, r_top[:, 1], r_hot[:, 0], r_top[:, 3])
            step(v.scalar_tensor_tensor(r_le, r_hot[:, 0], 3 * NEG, r_le, ALU.mult, ALU.add))
            first_greatest(r_le, NE, r_top[:, 2], r_hot[:, 1], r_top[:, 3])
            v.tensor_tensor(rexp[:, 16:20], r_top[:, 2], r_top[:, 1], ALU.subtract).then_inc(rexp_dve, 1)
            picks3 = picks.rearrange("p (b e) -> p b e", b=NB)
            before3 = before.rearrange("p (b e) -> p b e", b=NB)
            mark(v.memset(before3[:, 0], 0.0))
            step(v.tensor_tensor(picks3, r_hot[:, 0], r_hot[:, 1], ALU.add))
            for b in range(1, NB):
                step(v.tensor_tensor(before3[:, b], before3[:, b - 1], picks3[:, b - 1], ALU.add))
            v.tensor_tensor(per_part, before3[:, NB - 1], picks3[:, NB - 1], ALU.add).then_inc(m_dve, 1)

            dve.wait_ge(rexp_act, 1)
            mark(v.tensor_copy(picked[:, :, 0], C("ids")))
            cw = [picked[:, NB * n:NB * (n + 1), 1] for n in range(2)]
            step(v.tensor_reduce(r_top[:, 3], rexp[:, 0:16].rearrange("p (b g) -> p b g", b=NB), AX, ALU.add))
            mark(v.reciprocal(r_top[:, 3], r_top[:, 3]))
            step(v.tensor_scalar(r_top[:, 6], rexp[:, 16:20], 1.0, None, ALU.add))
            step(v.reciprocal(r_top[:, 6], r_top[:, 6]))
            v.tensor_tensor(cw[0], r_top[:, 6], r_top[:, 3], ALU.mult).then_inc(cw_dve, 1)
            dve.wait_ge(cw_dve, 1)
            v.tensor_tensor(cw[1], cw[0], rexp[:, 16:20], ALU.mult).then_inc(cw_dve, 1)

            for o in range(2):
                dve.wait_ge(cw_dve, 2)
                own_done()
                v.tensor_tensor(tile_vals[:, :, o], r_hot.rearrange("p n b e -> p (n b) e"), b3(picked[:, :, o], NE),
                                ALU.mult).then_inc(locs_dve, 1)

            dve.wait_ge(rank_pe, 1)
            dve.wait_ge(xn_stored[1], 16 * NB // 2)
            ranks = bank[0][:, 0:P].rearrange("p (b e) -> p b e", b=NB)
            count = C("count").unsqueeze(1)
            step(v.tensor_tensor(r_rank, r_hot, ranks.unsqueeze(1).broadcast_to([P, 2, NB, NE]), ALU.mult))
            step(v.tensor_reduce(r_top[:, 4:6], r_rank, AX, ALU.add))
            rank = r_top[:, 4:6].rearrange("p n b -> p (n b)")
            v.tensor_tensor(in_slot, count.broadcast_to([P, 2 * NB, SLOTS]), b3(rank, SLOTS), ALU.is_equal
                            ).then_inc(locs_dve, 1)
            mark(v.tensor_copy(r_loc, bank[0][:, 0:P]))
            mark(v.tensor_copy(r_cnt, bank[1][:, 0:NE]))

            def read_table(bk, first, n, times):
                dve.wait_ge(table_pe, times)
                tab = bk[:, 0:2 * n].rearrange("p (o t) -> p o t", o=2)
                t = slice(first, first + n)
                for s in range(2):
                    c = slice(SLOTS * s, SLOTS * (s + 1))
                    by_pair = tab[c, 0].rearrange("p (i s) -> p s i", s=2)[:, s]
                    v.tensor_scalar(slots_in[c, first // 2:(first + n) // 2], by_pair, float(S), None, ALU.add
                                    ).then_inc(slots_dve, 1)
                mark(v.tensor_copy(weights_out[:, t], tab[:, 1]))
                step(v.tensor_scalar(row_f[:, t], tab[:, 0], 2.0, C("row0"), ALU.mult, ALU.add))
                v.tensor_copy(row_i[:, t], row_f[:, t]).then_inc(row_dve, 1)

            read_table(bank[2], 0, NE, 1)

            def count_overflow():
                step(v.tensor_scalar(r_ov[:, 0], r_cnt, float(SLOTS), None, ALU.is_gt))
                for k in range(2, S // SLOTS):
                    step(v.scalar_tensor_tensor(r_ov[:, 0], r_cnt, float(SLOTS * k), r_ov[:, 0], ALU.is_gt, ALU.add))
                step(v.tensor_copy(r_ov[:, 1], r_ov[:, 0]))
                a, other = 1, 2
                for d in (1, 2, 4, 8, 16):
                    mark(v.tensor_copy(r_ov[:, other, 0:d], r_ov[:, a, 0:d]))
                    step(v.tensor_tensor(r_ov[:, other, d:], r_ov[:, a, d:], r_ov[:, a, 0:NE - d], ALU.add))
                    a, other = other, a
                step(v.tensor_tensor(r_cmp, r_ov[:, a].unsqueeze(1).broadcast_to([P, MAXOVER, NE]),
                                     C("over").unsqueeze(2).broadcast_to([P, MAXOVER, NE]), ALU.is_le))
                step(v.tensor_reduce(r_exp, r_cmp, AX, ALU.add))
                step(v.tensor_scalar(r_exp, r_exp, float(NE - 1), None, ALU.min))
                step(v.tensor_copy(oexp_i[:, :], r_exp))
                v.tensor_copy(nover_i[:, :], r_ov[:, a, NE - 1:NE]).then_inc(over_dve, 1)
                return r_ov[:, a], r_ov[:, other]

            def place_overflow(upto, first):
                step(v.tensor_tensor(first, upto, r_ov[:, 0], ALU.subtract))
                step(v.tensor_scalar(first, first, float(SLOTS), float(2 * S - SLOTS), ALU.mult, ALU.add))
                r_loc3 = r_loc.rearrange("p (b e) -> p b e", b=NB)
                step(v.tensor_scalar(r_le, r_loc3, float(SLOTS), None, ALU.is_ge))
                step(v.tensor_tensor(r_loc3, r_loc3, first.unsqueeze(1).broadcast_to([P, NB, NE]), ALU.add))
                step(v.tensor_tensor(r_loc3, r_loc3, r_le, ALU.mult))
                for n in range(2):
                    step(v.tensor_tensor(r_le, r_loc3, r_hot[:, n], ALU.mult))
                    step(v.tensor_reduce(r_top[:, 4 + n], r_le, AX, ALU.add))
                step(v.tensor_scalar(r_top[:, 4:6], r_top[:, 4:6], float(2 * S), None, ALU.subtract))
                step(v.tensor_copy(loc_i[:, 0].rearrange("p (n b) -> p n b", n=2), r_top[:, 4:6]))
                mark(v.tensor_scalar(loc_i[:, 1], loc_i[:, 0], SLOTS - 1, None, ALU.bitwise_and))
                step(v.tensor_scalar(loc_i[:, 2], loc_i[:, 0], SLOTS.bit_length() - 1, None, ALU.arith_shift_right))
                step(v.tensor_copy(loc_f[:, :, :], loc_i[:, 1:3]))
                step(v.tensor_tensor(over_tile, count[:, :, 0:MAXOVER].broadcast_to([P, 2 * NB, MAXOVER]),
                                     b3(loc_f[:, 1], MAXOVER), ALU.is_equal))
                v.tensor_tensor(over_slot, count.broadcast_to([P, 2 * NB, SLOTS]), b3(loc_f[:, 0], SLOTS), ALU.is_equal
                                ).then_inc(olocs_dve, 1)
                for o in range(2):
                    v.tensor_tensor(over_vals[:, :, o], over_tile, b3(picked[:, :, o], MAXOVER), ALU.mult
                                    ).then_inc(olocs_dve, 1)

            def experts(i, first):
                dve.wait_ge(xgT_pe, i + 1)
                for k in range(4, KD):
                    last = v.tensor_scalar(xT[:, k], bank[1][:, P * (k - 4):P * (k - 3)], scm[:, 2, k:k + 1],
                                           scm[:, 3, k:k + 1], ALU.mult, ALU.add)
                last.then_inc(xgT_dve, 1)
                for s in range(2):
                    dve.wait_ge(silu_act, i * 2 + s + 1)
                    dve.wait_ge(wu_used, i * 2 + s + 1)
                    v.tensor_tensor(hid, bank[3][:, 0:256], act_g, ALU.mult).then_inc(hid_dve, 1)
                    dve.wait_ge(wd_used, i * 2 + s + 1)
                    if not first:
                        dve.wait_ge(y_added[s], i * 16)
                    v.scalar_tensor_tensor(ysb[:, s], bank[5 + s][:, :], weights_out[:, bass.ds(i * 2 + s, 1)] if not first else
                                           weights_out[:, s:s + 1], gt_f,
                                           ALU.mult, ALU.mult).then_inc(ydn_dve, 1)

            experts(0, True)
            upto, first_tile = count_overflow()
            with dve.Fori(1, PAIRS) as i:
                experts(i, False)
            n_over = dve.value_load(nover_i[0:1, 0:1], min_val=0, max_val=MAXOVER)
            with dve.If(n_over > 0):
                place_overflow(upto, first_tile)
                read_table(bank[7], NE, MAXOVER, 2)
                with dve.Fori(PAIRS, ALLPAIRS) as i:
                    experts(i, False)


_INS = ("x", "c", "w_ada", "b_ada", "g_norm_mix", "w_in", "sinks_a", "w_branch", "w_out", "g_norm_ffn",
        "w_expert_gate", "w_expert_up", "w_expert_down")


def kernel(**inputs):
    import concourse.bacc as bacc
    from concourse.bass_utils import run_bass_kernel_spmd

    nc = bacc.Bacc("TRN2", target_bir_lowering=False, num_devices=1)
    arrays = {name: np.ascontiguousarray(inputs[name]) for name in _INS}
    arrays["positions"] = np.ascontiguousarray(np.reshape(inputs["positions"], (NB, P)).T)
    head = np.concatenate([inputs[n] for n in ("q_norm_a", "k_norm_a", "q_norm_b", "k_norm_b")])
    swapped = np.concatenate([head[:, HD // 2:], head[:, :HD // 2]], axis=1)
    arrays["head_gains"] = np.concatenate([head, swapped]).reshape(1, 8 * HD)
    arrays["route_bias"] = np.concatenate([inputs["b_group"], np.reshape(inputs["b_router"], (1, NE))], axis=1)
    by_model = np.transpose(inputs["w_router"][0], (1, 0, 2)).reshape(D, NE)
    arrays["w_route"] = np.concatenate([inputs["w_group"][0], by_model], axis=1)
    arrays["consts"] = shape_constants()
    access = {name: nc.dram_tensor(f"in_{name}", a.shape, mybir.dt.from_np(a.dtype), kind="ExternalInput").ap()
              for name, a in arrays.items()}
    access["out"] = nc.dram_tensor("out_y", (2 * S, HALF), F32, kind="ExternalOutput").ap()
    build_block(nc, access)
    r = run_bass_kernel_spmd(nc, [{f"in_{name}": a for name, a in arrays.items()}], core_ids=[0])
    return r.results[0]["out_y"].reshape(1, S, D)
```
